# Optimizing a Trainium2 kernel written in Bass

```python
import jax, jax.numpy as jnp
from jax import lax
import numpy as np

D_MODEL = 2048
BATCH = 1
SEQ = 256
DEPTH = 1

MIX_WIDTH = D_MODEL
MLA_WIDTH = D_MODEL // 2
HGRN_WIDTH = MIX_WIDTH - MLA_WIDTH
MLA_HEADS = 8
MLA_V_DIM = MLA_WIDTH // MLA_HEADS
MLA_NOPE_DIM = 128
MLA_ROPE_DIM = 64
MLA_Q_RANK = D_MODEL // 4
MLA_KV_RANK = D_MODEL // 8
ROPE_BASE = 10000.0
Q_BLOCK = 128
HGRN_HEADS = 8
HGRN_KEY_DIM = 128
HGRN_VAL_DIM = HGRN_WIDTH // HGRN_HEADS
HGRN_QK_WIDTH = HGRN_HEADS * HGRN_KEY_DIM
HGRN_CHUNK = 64
D_FF = 4 * D_MODEL
NORM_EPS = 1e-6
N_MOD = 6
IN_WIDTH = MLA_Q_RANK + MLA_KV_RANK + MLA_ROPE_DIM + 3 * HGRN_QK_WIDTH + 2 * HGRN_WIDTH


def _in_proj_offsets():
    widths = (MLA_Q_RANK, MLA_KV_RANK, MLA_ROPE_DIM, HGRN_QK_WIDTH, HGRN_QK_WIDTH,
              HGRN_QK_WIDTH, HGRN_WIDTH, HGRN_WIDTH)
    return [int(o) for o in np.cumsum(widths)[:-1]]

def _rmsnorm(x, g):
    xf = x.astype(jnp.float32)
    y = xf * lax.rsqrt(jnp.mean(xf * xf, axis=-1, keepdims=True) + NORM_EPS)
    return (y * g.astype(jnp.float32)).astype(x.dtype)

def _rope_angles(positions):
    half = MLA_ROPE_DIM // 2
    inv_freq = ROPE_BASE ** (-jnp.arange(half, dtype=jnp.float32) / half)
    ang = positions.astype(jnp.float32)[..., None] * inv_freq
    return jnp.cos(ang), jnp.sin(ang)

def _apply_rope(x, cos, sin):
    x1, x2 = jnp.split(x.astype(jnp.float32), 2, axis=-1)
    return jnp.concatenate([x1 * cos - x2 * sin, x1 * sin + x2 * cos], axis=-1).astype(x.dtype)

def _mla(q_lat, kv_lat, k_rope, cos, sin, q_norm_g, kv_norm_g, w_uq, w_ukv):
    B, S, _ = q_lat.shape
    H = MLA_HEADS
    q = (_rmsnorm(q_lat, q_norm_g) @ w_uq).reshape(B, S, H, MLA_NOPE_DIM + MLA_ROPE_DIM)
    q_nope = q[..., :MLA_NOPE_DIM]
    q_rope = _apply_rope(q[..., MLA_NOPE_DIM:], cos[:, :, None, :], sin[:, :, None, :])
    kv = (_rmsnorm(kv_lat, kv_norm_g) @ w_ukv).reshape(B, S, H, MLA_NOPE_DIM + MLA_V_DIM)
    k_nope, v = kv[..., :MLA_NOPE_DIM], kv[..., MLA_NOPE_DIM:]
    k_rope = _apply_rope(k_rope, cos, sin)
    scale = (MLA_NOPE_DIM + MLA_ROPE_DIM) ** -0.5
    nb = S // Q_BLOCK

    def to_blocks(t):
        return t.reshape(B, nb, Q_BLOCK, *t.shape[2:]).swapaxes(0, 1)

    def attend(blk):
        qn, qr = blk
        s = (jnp.einsum('bqhd,bkhd->bhqk', qn, k_nope)
             + jnp.einsum('bqhr,bkr->bhqk', qr, k_rope))
        p = jax.nn.softmax(s.astype(jnp.float32) * scale, axis=-1).astype(v.dtype)
        return jnp.einsum('bhqk,bkhd->bqhd', p, v)

    o = lax.map(attend, (to_blocks(q_nope), to_blocks(q_rope)))
    return o.swapaxes(0, 1).reshape(B, S, H * MLA_V_DIM)

def _gla_chunkwise(q, k, v, log_f):
    B, S, H, Dk = q.shape
    Dv = v.shape[-1]
    n = S // HGRN_CHUNK

    def to_chunks(t):
        return t.reshape(B, n, HGRN_CHUNK, H, t.shape[-1]).transpose(1, 0, 3, 2, 4)

    qc, kc, vc = to_chunks(q), to_chunks(k), to_chunks(v)
    bc = jnp.cumsum(to_chunks(log_f), axis=3)
    mask = jnp.tril(jnp.ones((HGRN_CHUNK, HGRN_CHUNK), dtype=bool))[None, None, :, :, None]

    def step(state, inp):
        q_, k_, v_, b_ = inp
        rel = jnp.where(mask, b_[:, :, :, None, :] - b_[:, :, None, :, :], -jnp.inf)
        a = jnp.einsum('bhtd,bhsd,bhtsd->bhts', q_, k_, jnp.exp(rel))
        o = (jnp.einsum('bhts,bhse->bhte', a, v_)
             + jnp.einsum('bhtd,bhde->bhte', q_ * jnp.exp(b_), state))
        b_last = b_[:, :, -1:, :]
        state = (state * jnp.exp(b_last)[:, :, 0, :, None]
                 + jnp.einsum('bhsd,bhse->bhde', k_ * jnp.exp(b_last - b_), v_))
        return state, o

    state0 = jnp.zeros((B, H, Dk, Dv), jnp.float32)
    _, o = lax.scan(step, state0, (qc, kc, vc, bc))
    return o.transpose(1, 0, 3, 2, 4).reshape(B, S, H, Dv)

def _hgrn2_direction(q, f_logit, v, lb):
    f = lb + (1.0 - lb) * jax.nn.sigmoid(f_logit.astype(jnp.float32))
    return _gla_chunkwise(q.astype(jnp.float32), 1.0 - f, v.astype(jnp.float32), jnp.log(f))

def _lower_bound(lb_logits, layer):
    p = jax.nn.softmax(lb_logits.astype(jnp.float32), axis=0)
    return jnp.cumsum(p, axis=0)[layer].reshape(HGRN_HEADS, HGRN_KEY_DIM)

def _hgrn2_bidir(hq, f_fwd, f_bwd, hi, hg, lb_fwd, lb_bwd, norm_g):
    B, S, _ = hq.shape
    q = hq.reshape(B, S, HGRN_HEADS, HGRN_KEY_DIM)
    ff = f_fwd.reshape(B, S, HGRN_HEADS, HGRN_KEY_DIM)
    fb = f_bwd.reshape(B, S, HGRN_HEADS, HGRN_KEY_DIM)
    v = hi.reshape(B, S, HGRN_HEADS, HGRN_VAL_DIM)
    o_fwd = _hgrn2_direction(q, ff, v, lb_fwd)
    o_bwd = jnp.flip(_hgrn2_direction(jnp.flip(q, 1), jnp.flip(fb, 1), jnp.flip(v, 1), lb_bwd), 1)
    o = _rmsnorm(o_fwd + o_bwd, norm_g).reshape(B, S, HGRN_WIDTH)
    return (o * jax.nn.silu(hg.astype(jnp.float32))).astype(hq.dtype)

def first_inputs(seed: int = 0) -> dict:
    key = jax.random.key(seed)
    ks = jax.random.split(key, 24)
    f32 = jnp.float32

    def nrm(k, shape, fan_in, s=1.0):
        return jax.random.normal(k, shape, f32) * (s * fan_in ** -0.5)

    def gain(k, shape):
        return 1.0 + 0.05 * jax.random.normal(k, shape, f32)

    offs = jax.random.randint(ks[2], (BATCH, 1), 0, 1024, dtype=jnp.int32)
    positions = (jnp.arange(SEQ, dtype=jnp.int32)[None, :] + offs).astype(jnp.int32)
    return {
        "x": jax.random.normal(ks[0], (BATCH, SEQ, D_MODEL), f32),
        "c": jax.random.normal(ks[1], (BATCH, D_MODEL), f32),
        "positions": positions,
        "w_mod": nrm(ks[3], (DEPTH, D_MODEL, N_MOD * D_MODEL), D_MODEL, 0.5),
        "b_mod": 0.01 * jax.random.normal(ks[4], (DEPTH, N_MOD * D_MODEL), f32),
        "pre_mix_g": gain(ks[5], (DEPTH, D_MODEL)),
        "post_mix_g": gain(ks[6], (DEPTH, D_MODEL)),
        "pre_mlp_g": gain(ks[7], (DEPTH, D_MODEL)),
        "post_mlp_g": gain(ks[8], (DEPTH, D_MODEL)),
        "w_in": nrm(ks[9], (DEPTH, D_MODEL, IN_WIDTH), D_MODEL),
        "q_norm_g": gain(ks[10], (DEPTH, MLA_Q_RANK)),
        "kv_norm_g": gain(ks[11], (DEPTH, MLA_KV_RANK)),
        "w_uq": nrm(ks[12], (DEPTH, MLA_Q_RANK, MLA_HEADS * (MLA_NOPE_DIM + MLA_ROPE_DIM)), MLA_Q_RANK),
        "w_ukv": nrm(ks[13], (DEPTH, MLA_KV_RANK, MLA_HEADS * (MLA_NOPE_DIM + MLA_V_DIM)), MLA_KV_RANK),
        "hgrn_norm_g": gain(ks[14], (DEPTH, HGRN_VAL_DIM)),
        "hgrn_lb_logits_fwd": 0.1 * jax.random.normal(ks[15], (DEPTH + 1, HGRN_QK_WIDTH), f32),
        "hgrn_lb_logits_bwd": 0.1 * jax.random.normal(ks[16], (DEPTH + 1, HGRN_QK_WIDTH), f32),
        "w_out": nrm(ks[17], (DEPTH, MIX_WIDTH, D_MODEL), MIX_WIDTH),
        "w_up": nrm(ks[18], (DEPTH, D_MODEL, D_FF), D_MODEL),
        "w_down": nrm(ks[19], (DEPTH, D_FF, D_MODEL), D_FF),
    }

def first_block(x, c, positions, w_mod, b_mod, pre_mix_g, post_mix_g, pre_mlp_g, post_mlp_g,
              w_in, q_norm_g, kv_norm_g, w_uq, w_ukv, hgrn_norm_g, hgrn_lb_logits_fwd,
              hgrn_lb_logits_bwd, w_out, w_up, w_down):
    cos, sin = _rope_angles(positions)
    cond = jax.nn.silu(c)
    offsets = _in_proj_offsets()
    for layer in range(DEPTH):
        mod = (cond @ w_mod[layer] + b_mod[layer]).astype(x.dtype)
        shift_a, scale_a, gate_a, shift_m, scale_m, gate_m = [
            m[:, None, :] for m in jnp.split(mod, N_MOD, axis=-1)]

        h = _rmsnorm(x, pre_mix_g[layer]) * (1.0 + scale_a) + shift_a
        proj = h @ w_in[layer]
        q_lat, kv_lat, k_rope, hq, f_fwd, f_bwd, hi, hg = jnp.split(proj, offsets, axis=-1)
        attn_out = _mla(q_lat, kv_lat, k_rope, cos, sin, q_norm_g[layer], kv_norm_g[layer],
                        w_uq[layer], w_ukv[layer])
        rec_out = _hgrn2_bidir(hq, f_fwd, f_bwd, hi, hg,
                               _lower_bound(hgrn_lb_logits_fwd, layer),
                               _lower_bound(hgrn_lb_logits_bwd, layer), hgrn_norm_g[layer])
        mix = jnp.concatenate([attn_out, rec_out], axis=-1) @ w_out[layer]
        x = x + gate_a * _rmsnorm(mix, post_mix_g[layer])

        h = _rmsnorm(x, pre_mlp_g[layer]) * (1.0 + scale_m) + shift_m
        y = jnp.square(jax.nn.relu(h @ w_up[layer])) @ w_down[layer]
        x = x + gate_m * _rmsnorm(y, post_mlp_g[layer])
    return x


GRID_W = 64
WIN_R = 8
WIN_C = 16
ATTN_HEADS = 8
HEAD_DIM = 128
D_ATTN = ATTN_HEADS * HEAD_DIM
D_CONV = D_MODEL // 2
CONV_WIDTH = 31
CONV_PAD = CONV_WIDTH // 2
D_FF_2 = -(-8 * D_MODEL // (3 * 256)) * 256
EPS = 1e-6
IN_SPLITS = [D_ATTN, D_ATTN, D_ATTN, D_CONV, D_CONV, D_MODEL, D_MODEL]
N_IN = sum(IN_SPLITS)


def rms_norm(x, g):
    xf = x.astype(jnp.float32)
    y = xf * lax.rsqrt(jnp.mean(xf * xf, axis=-1, keepdims=True) + EPS) * g.astype(jnp.float32)
    return y.astype(x.dtype)

def layer_norm(x, g, b):
    xf = x.astype(jnp.float32)
    mu = jnp.mean(xf, axis=-1, keepdims=True)
    xc = xf - mu
    var = jnp.mean(xc * xc, axis=-1, keepdims=True)
    y = xc * lax.rsqrt(var + EPS) * g.astype(jnp.float32) + b.astype(jnp.float32)
    return y.astype(x.dtype)

def neighbourhood_attention(q, k, v, rpb):
    B, S, H, Dh = q.shape
    rows = S // GRID_W
    kr = min(WIN_R, rows)
    kc = min(WIN_C, GRID_W)
    qg = q.reshape(B, rows, GRID_W, H, Dh)
    kg = k.reshape(B, rows, GRID_W, H, Dh)
    vg = v.reshape(B, rows, GRID_W, H, Dh)
    col = jnp.arange(GRID_W)
    col_start = jnp.clip(col - kc // 2, 0, GRID_W - kc)
    col_idx = col_start[:, None] + jnp.arange(kc)[None, :]
    dc = col_idx - col[:, None]
    rpb_cols = rpb[:, :, dc + WIN_C - 1]
    scale = HEAD_DIM ** -0.5

    def one_row(r):
        r_start = jnp.clip(r - kr // 2, 0, rows - kr)
        kb = lax.dynamic_slice_in_dim(kg, r_start, kr, axis=1)
        vb = lax.dynamic_slice_in_dim(vg, r_start, kr, axis=1)
        kw = kb[:, :, col_idx]
        vw = vb[:, :, col_idx]
        qr = lax.dynamic_index_in_dim(qg, r, axis=1, keepdims=False)
        s = jnp.einsum('bwhd,biwjhd->bhwij', qr, kw).astype(jnp.float32) * scale
        dr = r_start + jnp.arange(kr) - r
        bias = jnp.transpose(rpb_cols[:, dr + WIN_R - 1], (0, 2, 1, 3))
        s = s + bias[None].astype(jnp.float32)
        p = jax.nn.softmax(s.reshape(B, H, GRID_W, kr * kc), axis=-1)
        p = p.reshape(B, H, GRID_W, kr, kc).astype(vw.dtype)
        return jnp.einsum('bhwij,biwjhd->bwhd', p, vw)

    out = lax.map(one_row, jnp.arange(rows))
    return jnp.transpose(out, (1, 0, 2, 3, 4)).reshape(B, S, H * Dh)

def conformer_conv(a, b, w_dw, b_dw, ln_g, ln_b, w_pw):
    z = a * jax.nn.sigmoid(b)
    z = lax.conv_general_dilated(
        z, w_dw[:, None, :].astype(z.dtype), window_strides=(1,),
        padding=[(CONV_PAD, CONV_PAD)],
        dimension_numbers=('NWC', 'WIO', 'NWC'),
        feature_group_count=z.shape[-1]) + b_dw
    z = layer_norm(z, ln_g, ln_b)
    z = jax.nn.silu(z)
    return z @ w_pw

def second_inputs(seed: int = 0) -> dict:
    key = jax.random.key(seed)
    ks = jax.random.split(key, 20)
    f32 = jnp.float32
    nrm = lambda k, shape, s: jax.random.normal(k, shape, f32) * s
    gain = lambda k, n: 1.0 + 0.05 * jax.random.normal(k, (DEPTH, n), f32)
    return {
        'x': jax.random.normal(ks[0], (BATCH, SEQ, D_MODEL), f32),
        'mix_pre_g': gain(ks[1], D_MODEL),
        'mix_post_g': gain(ks[2], D_MODEL),
        'w_in': nrm(ks[3], (DEPTH, D_MODEL, N_IN), D_MODEL ** -0.5),
        'rpb': nrm(ks[4], (DEPTH, ATTN_HEADS, 2 * WIN_R - 1, 2 * WIN_C - 1), 0.1),
        'w_attn_o': nrm(ks[5], (DEPTH, D_ATTN, D_MODEL), D_ATTN ** -0.5),
        'w_dw': nrm(ks[6], (DEPTH, CONV_WIDTH, D_CONV), CONV_WIDTH ** -0.5),
        'b_dw': nrm(ks[7], (DEPTH, D_CONV), 0.02),
        'conv_ln_g': gain(ks[8], D_CONV),
        'conv_ln_b': nrm(ks[9], (DEPTH, D_CONV), 0.02),
        'w_conv_o': nrm(ks[10], (DEPTH, D_CONV, D_MODEL), D_CONV ** -0.5),
        'w_out': nrm(ks[11], (DEPTH, D_MODEL, D_MODEL), D_MODEL ** -0.5),
        'ffn_pre_g': gain(ks[12], D_MODEL),
        'ffn_post_g': gain(ks[13], D_MODEL),
        'w_gate_up': nrm(ks[14], (DEPTH, D_MODEL, 2 * D_FF_2), D_MODEL ** -0.5),
        'w_down': nrm(ks[15], (DEPTH, D_FF_2, D_MODEL), D_FF_2 ** -0.5),
    }

def second_block(x, mix_pre_g, mix_post_g, w_in, rpb, w_attn_o, w_dw, b_dw,
              conv_ln_g, conv_ln_b, w_conv_o, w_out, ffn_pre_g, ffn_post_g,
              w_gate_up, w_down):
    B, S, D = x.shape
    split_pts = list(np.cumsum(IN_SPLITS)[:-1])
    h = x
    for l in range(DEPTH):
        u = rms_norm(h, mix_pre_g[l])
        proj = u @ w_in[l]
        q, k, v, ca, cb, ga, gb = jnp.split(proj, split_pts, axis=-1)
        q = q.reshape(B, S, ATTN_HEADS, HEAD_DIM)
        k = k.reshape(B, S, ATTN_HEADS, HEAD_DIM)
        v = v.reshape(B, S, ATTN_HEADS, HEAD_DIM)
        y_attn = neighbourhood_attention(q, k, v, rpb[l]) @ w_attn_o[l]
        y_conv = conformer_conv(ca, cb, w_dw[l], b_dw[l], conv_ln_g[l],
                                conv_ln_b[l], w_conv_o[l])
        merged = jax.nn.sigmoid(ga) * y_attn + jax.nn.sigmoid(gb) * y_conv
        h = h + rms_norm(merged @ w_out[l], mix_post_g[l])
        u = rms_norm(h, ffn_pre_g[l])
        gate, up = jnp.split(u @ w_gate_up[l], 2, axis=-1)
        f = (jax.nn.silu(gate) * up) @ w_down[l]
        h = h + rms_norm(f, ffn_post_g[l])
    return h


def setup_inputs(seed=0):
    out = dict(first_inputs(seed))
    for name, value in second_inputs(seed + 1).items():
        if name != "x":
            out[name + "_2"] = value
    return out


def reference(
    x, c, positions, w_mod, b_mod, pre_mix_g, post_mix_g, pre_mlp_g, post_mlp_g, w_in, q_norm_g,
    kv_norm_g, w_uq, w_ukv, hgrn_norm_g, hgrn_lb_logits_fwd, hgrn_lb_logits_bwd, w_out, w_up,
    w_down, mix_pre_g_2, mix_post_g_2, w_in_2, rpb_2, w_attn_o_2, w_dw_2, b_dw_2, conv_ln_g_2,
    conv_ln_b_2, w_conv_o_2, w_out_2, ffn_pre_g_2, ffn_post_g_2, w_gate_up_2, w_down_2,
):
    x = first_block(
        x, c, positions, w_mod, b_mod, pre_mix_g, post_mix_g, pre_mlp_g, post_mlp_g, w_in,
        q_norm_g, kv_norm_g, w_uq, w_ukv, hgrn_norm_g, hgrn_lb_logits_fwd, hgrn_lb_logits_bwd,
        w_out, w_up, w_down,
    )
    return second_block(
        x, mix_pre_g_2, mix_post_g_2, w_in_2, rpb_2, w_attn_o_2, w_dw_2, b_dw_2, conv_ln_g_2,
        conv_ln_b_2, w_conv_o_2, w_out_2, ffn_pre_g_2, ffn_post_g_2, w_gate_up_2, w_down_2,
    )


_drawn_inputs = setup_inputs


def setup_inputs(seed=0):
    import zlib

    import numpy as np

    out = dict(_drawn_inputs(seed))
    spreads = {}
    factors = {'post_mix_g': 2.77,
     'pre_mlp_g': 2.831,
     'post_mlp_g': 2.819,
     'q_norm_g': 8.0,
     'kv_norm_g': 5.683,
     'hgrn_norm_g': 12.739,
     'hgrn_lb_logits_fwd': 3.093,
     'hgrn_lb_logits_bwd': 3.414,
     'rpb_2': 2.677,
     'conv_ln_b_2': 3.74,
     'b_dw_2': 2.782}
    for name, (base, spread) in spreads.items():
        noise = np.random.default_rng([zlib.crc32(name.encode()), seed]).standard_normal(out[name].shape)
        drawn = base * np.exp(spread * noise) if base else spread * noise
        out[name] = __import__('jax').numpy.asarray(drawn.astype(out[name].dtype))
    for name, factor in factors.items():
        out[name] = (out[name] * factor).astype(out[name].dtype)
    return out
```

```python
from contextlib import ExitStack

import numpy as np

import concourse.bass as bass
from concourse import mybir

F32 = mybir.dt.float32
F32R = mybir.dt.float32r
I32 = mybir.dt.int32
U8 = mybir.dt.uint8
ALU = mybir.AluOpType
ACT = mybir.ActivationFunctionType
AX = mybir.AxisListType

P = 128
T = 256
D = 2048
DT = D // P
HEADS = 8
KT = 4
CW = 256
SLOTS = 4
EPS = 1e-6
Q_RANK, KV_RANK, ROPE = 512, 256, 64
D_FF, D_FF2 = 8192, 5632
N_MOD = 6
MLA_SCALE = 192 ** -0.5
NA_SCALE = 128 ** -0.5
GRID_W, WIN_C, WIN_R, GRID_ROWS = 64, 16, 8, 4
RPB_H, RPB_W = 2 * WIN_R - 1, 2 * WIN_C - 1
TAPS = 31
PAD = TAPS // 2
LEVELS = [1, 2, 4, 8, 16, 32, 64]
TWO_PI = 2 * np.pi

VECTORS = [("c", 16), ("b_mod", 96), ("pre_mix_g", 16), ("post_mix_g", 16), ("pre_mlp_g", 16),
           ("post_mlp_g", 16), ("q_norm_g", 4), ("kv_norm_g", 2), ("hgrn_norm_g", 1),
           ("hgrn_lb_logits_fwd", 16), ("hgrn_lb_logits_bwd", 16), ("mix_pre_g_2", 16),
           ("mix_post_g_2", 16), ("ffn_pre_g_2", 16), ("ffn_post_g_2", 16), ("b_dw_2", 8),
           ("conv_ln_g_2", 8), ("conv_ln_b_2", 8), ("w_dw_2", 8 * TAPS)]
COLUMN, _at = {}, 0
for _name, _rows in VECTORS:
    COLUMN[_name] = _at
    _at += _rows
N_COLUMNS = _at
V_TILES = -(-N_COLUMNS // P)

C_IDENT, C_FLIP, C_RT, C_WIN, C_FREQ = 0, 128, 256, 320, 384
C_COLS = 385


def constants():
    c = np.zeros((P, C_COLS), np.float32)
    c[:, C_IDENT:C_IDENT + P] = np.eye(P)
    c[:, C_FLIP:C_FLIP + P] = np.kron(np.eye(2), np.eye(GRID_W)[::-1])
    half = ROPE // 2
    for i in range(half):
        c[ROPE + half + i, C_RT + i] = -1.0
        c[ROPE + i, C_RT + half + i] = 1.0
    w = np.arange(GRID_W)
    start = np.clip(w - WIN_C // 2, 0, GRID_W - WIN_C)
    outside = (w[None] < start[:, None]) | (w[None] >= start[:, None] + WIN_C)
    c[:, C_WIN:C_WIN + GRID_W] = np.where(np.tile(outside, (2, 1)), -1e30, 0.0)
    freq = np.float32(10000.0) ** (-np.arange(half, dtype=np.float32) / np.float32(half))
    c[ROPE:, C_FREQ] = np.tile(freq, 2)
    s = np.arange(P)[:, None]
    masks = np.zeros((P, 2, len(LEVELS), P // 2), np.int32)
    for n, m in enumerate(LEVELS):
        blocks = np.arange(P).reshape(-1, 2, m)
        later, earlier = blocks[:, 1].ravel()[None], blocks[:, 0].ravel()[None]
        masks[:, 0, n] = s // m == later // m - 1
        masks[:, 1, n] = s // m == earlier // m + 1
    return c, masks.reshape(P, -1)


EXTRA = {"plain": 0, "mod": 0, "relu2": 3, "add": 1, "gated": 1, "gated_add": 2, "gate": 1, "up": 3}


class Linear:

    def __init__(self, w, act, row_tile=0, row_tiles=DT, col0=0, width=CW, tiles=(0, P), out=None,
                 kind="plain", step=CW, tmp=None):
        self.w, self.act, self.row_tile, self.row_tiles = w, act, row_tile, row_tiles
        self.col0, self.width, self.tiles, self.out, self.kind = col0, width, tiles, out, kind
        self.step, self.tmp = step, tmp
        self.chunks = [(k, min(KT, row_tiles - k)) for k in range(0, row_tiles, KT)]


class Phase:

    def __init__(self, name, iters, body):
        self.name, self.iters, self.body = name, iters, body
        self.chunks = [(b, k0, kn) for b, (lin, _, _) in enumerate(body) for k0, kn in lin.chunks]
        self.n_chunks = len(self.chunks)
        self.n_panels = sum(lin.kind != "mod" for lin, _, _ in body)
        self.slot_uses = [sum(j % SLOTS == s for j in range(self.n_chunks)) for s in range(SLOTS)]


def plan(phases):
    chunks, uses, panels, mods, extras = 0, [0] * SLOTS, 0, 0, 0
    last = [None] * SLOTS
    for ph in phases:
        ph.chunk0, ph.use0, ph.panel0, ph.mod0 = chunks, list(uses), panels, mods
        ph.last_before = list(last)
        for s in range(SLOTS):
            uses[s] += ph.slot_uses[s] * ph.iters
        n_mod = len(ph.body) - ph.n_panels
        ph.extra0 = extras
        ph.n_extra = sum(EXTRA[lin.kind] for lin, _, _ in ph.body)
        extras += ph.n_extra * ph.iters
        assert ph.iters == 1 or ph.n_panels % 2 == 0
        panels += ph.n_panels * ph.iters
        mods += n_mod * ph.iters
        ph.n_mods = n_mod
        for j in range(ph.n_chunks):
            last[j % SLOTS] = chunks + (ph.iters - 1) * ph.n_chunks + j
        chunks += ph.n_chunks * ph.iters
    return phases


def build(nc, d, out):
    ctx = ExitStack()
    with ctx:
        at = [-(-nc.sbuf_base // 32) * 32]
        SBUF_END = nc.sbuf_usable_end

        def place(name, shape, dt, offset=None):
            size = int(np.prod(shape[1:])) * {F32: 4, F32R: 4, I32: 4, U8: 1}[dt]
            size = -(-size // 32) * 32
            if offset is None:
                offset = at[0]
                at[0] += size
            assert offset + size <= SBUF_END, (name, offset, size)
            return nc.alloc_sbuf_tensor_at(name, shape, dt, offset=offset)

        def sem(name):
            return ctx.enter_context(nc.semaphore(name))

        w_raw = place("w_raw", [P, SLOTS, KT, CW], F32)
        w_hi = place("w_hi", [P, SLOTS, KT, CW], F32R)
        w_lo = place("w_lo", [P, SLOTS, KT, CW], F32R)
        x_res = place("x_res", [P, DT, T], F32)
        acts_at = at[0]
        acts = place("acts", [P, DT, 2, T], F32R)
        half_sum = place("half_sum", [P, 2, 2, T], F32)
        cols = place("cols", [P, V_TILES * P], F32)
        consts = place("consts", [P, C_COLS], F32)
        masks = place("masks", [P, 2, len(LEVELS), P // 2], U8)
        ones = place("ones", [P, P], F32)
        cond = place("cond", [P, DT, 2], F32R)
        silu_c = place("silu_c", [P, 2 * DT], F32)
        mods = place("mods", [P, N_MOD * DT], F32)
        gains = place("gains", [P, DT], F32)
        lb = place("lb", [P, 4, HEADS], F32)
        ring = place("ring", [P, 4, T], F32)
        rstd = place("rstd", [P, T], F32)
        small = place("small", [P, 16, 4], F32)
        mod_half = place("mod_half", [P, 2], F32)
        big = at[0]
        size_tile = T * 4

        ps = ctx.enter_context(nc.psum_tensor("ps", [P, 8, 512], F32))
        ident = consts[:, C_IDENT:C_IDENT + P]

        x_nat = place("x_nat", [P, 2, D], F32, big)
        v_rows = place("v_rows", [P, V_TILES, P], F32, big + 2 * D * 4)
        masks_i = place("masks_i", [P, 2 * len(LEVELS) * P // 2], I32, big + (2 * D + V_TILES * P) * 4)
        y_nat = place("y_nat", [P, 2, D], F32, big)
        proj = place("proj", [P, 47, T], F32, big)
        h_big = big + 7 * size_tile
        hq, hf, hb, hv, hg = (proj[:, 7 + 8 * i:15 + 8 * i, :] for i in range(5))
        a_diag = place("a_diag", [P, HEADS, 2, P], F32, big + 47 * size_tile)
        a_off = place("a_off", [P, 2, HEADS, P], F32, big + 55 * size_tile)
        kf = place("kf", [P, HEADS, T], F32, big + 63 * size_tile)
        kb = place("kb", [P, HEADS, T], F32, big + 71 * size_tile)
        qb = place("qb", [P, HEADS, T], F32, big + 79 * size_tile)
        hv_tok = place("hv_tok", [P, 2, HEADS, P], F32, big + 87 * size_tile)
        lat = place("lat", [P, 6, 2, T], F32R, h_big)
        q1 = place("q1", [P, HEADS, 2, T], F32, h_big + 12 * size_tile)
        kv1 = place("kv1", [P, HEADS, 2, T], F32, h_big + 28 * size_tile)
        v1_tok = place("v1_tok", [P, 2, HEADS, P], F32, h_big + 44 * size_tile)
        cos_sin = place("cos_sin", [P, 2, T], F32, h_big + 52 * size_tile)
        pos_i = place("pos_i", [P, T], I32, h_big + 54 * size_tile)
        ang = place("ang", [P, 3, T], F32, h_big + 55 * size_tile)
        rot = place("rot", [P, HEADS, T], F32, h_big + 58 * size_tile)
        prob_at = h_big + 66 * size_tile
        prob1 = place("prob1", [P, 2, T], F32, prob_at)
        prob1_t = place("prob1_t", [P, 2, 2, T], F32, prob_at + 2 * size_tile)
        y1 = place("y1", [P, DT, T], F32, big)
        ff_half = D_FF // 2 // P
        ff1 = place("ff1", [P, ff_half, 2, T], F32R, big)
        ym1 = place("ym1", [P, DT, T], F32, big + 2 * ff_half * size_tile)
        tmp1 = place("tmp1", [P, 2, 2, T], F32, big + (2 * ff_half + DT) * size_tile)
        pr2 = place("pr2", [P, 72, T], F32, big)
        q2, k2, v2, ca, cb = (pr2[:, 8 * i:8 * i + 8, :] for i in range(5))
        gate2 = pr2[:, 40:72, :]
        bias = place("bias", [P, 2, HEADS, GRID_ROWS, GRID_W], F32, big + 72 * size_tile)
        v2_tok = place("v2_tok", [P, 2, HEADS, P], F32, big + 88 * size_tile)
        prob2 = place("prob2", [P, 2, T], F32, big + 32 * size_tile)
        prob2_t = place("prob2_t", [P, 2, 2, T], F32, big + 34 * size_tile)
        zpad = place("zpad", [P, HEADS, T + 2 * PAD], F32, big)
        zc = ca
        mean = place("mean", [P, T], F32, big + 39 * size_tile)
        y2 = place("y2", [P, DT, T], F32, big + 16 * size_tile)
        tmp2 = place("tmp2", [P, 2, 2, T], F32, big + 36 * size_tile)
        ff2 = place("ff2", [P, D_FF2 // P, 2, T], F32R, big)
        tmp3 = place("tmp3", [P, 2, 2, T], F32, big + 2 * (D_FF2 // P) * size_tile)
        gate3 = place("gate3", [P, 2, T], F32, big + (2 * (D_FF2 // P) + 4) * size_tile)
        ym2 = place("ym2", [P, DT, T], F32, acts_at)

        w_mod, w_in = d["w_mod"][0], d["w_in"][0]
        ug = D_FF2
        panels = D // CW

        def lin(*a, **k):
            return Linear(*a, **k)

        mod = lin(w_mod, cond, kind="mod")
        in_h = lin(w_in, acts, col0=832, out=proj[:, 7:47, :])
        in_m = lin(w_in, acts, out=proj[:, 0:6, :])
        in_r = lin(w_in, acts, col0=704, width=P, tiles=(0,), out=proj[:, 6:7, :])
        uq = lin(d["w_uq"][0], lat, row_tiles=4, width=192, step=192, tiles=(0, ROPE),
                 out=q1[:].rearrange("p h two t -> p (h two) t"))
        ukv = lin(d["w_ukv"][0], lat[:, 4:6], row_tiles=2,
                  out=kv1[:].rearrange("p h two t -> p (h two) t"))
        w_o = lin(d["w_out"][0], acts, out=y1)
        up = [lin(d["w_up"][0], acts, col0=h * D_FF // 2, out=ff1, kind="relu2", tmp=tmp1) for h in range(2)]
        down = [lin(d["w_down"][0], ff1, row_tile=h * ff_half, row_tiles=ff_half, out=ym1,
                    kind="add" if h else "plain", tmp=tmp1) for h in range(2)]
        in_2 = lin(d["w_in_2"][0], acts, out=pr2)
        att_o = lin(d["w_attn_o_2"][0], acts, row_tiles=8, out=gate2[:, 0:16, :], kind="gated", tmp=tmp2)
        conv_o = lin(d["w_conv_o_2"][0], acts[:, 8:16], row_tiles=8, out=gate2[:, 0:16, :],
                     kind="gated_add", tmp=tmp2)
        out_2 = lin(d["w_out_2"][0], acts, out=y2)
        gate_l = lin(d["w_gate_up_2"][0], acts, out=None, kind="gate", tmp=tmp3)
        up_l = lin(d["w_gate_up_2"][0], acts, col0=ug, out=ff2, kind="up", tmp=tmp3)
        down2 = lin(d["w_down_2"][0], ff2, row_tiles=D_FF2 // P, out=ym2)

        phases = plan([
            Phase("mod", N_MOD * panels // 2, [(mod, 0, 2), (mod, 1, 2)]),
            Phase("in_h", 10, [(in_h, 0, 2), (in_h, 1, 2)]),
            Phase("in_m", 1, [(in_m, 0, 0), (in_m, 1, 0), (in_m, 2, 0), (in_r, 0, 0)]),
            Phase("uq", 2, [(uq, i, 4) for i in range(4)]),
            Phase("ukv", 2, [(ukv, i, 4) for i in range(4)]),
            Phase("w_o", panels // 2, [(w_o, 0, 2), (w_o, 1, 2)]),
            Phase("up_0", 8, [(up[0], 0, 2), (up[0], 1, 2)]),
            Phase("down_0", panels // 2, [(down[0], 0, 2), (down[0], 1, 2)]),
            Phase("up_1", 8, [(up[1], 0, 2), (up[1], 1, 2)]),
            Phase("down_1", panels // 2, [(down[1], 0, 2), (down[1], 1, 2)]),
            Phase("in_2", 18, [(in_2, 0, 2), (in_2, 1, 2)]),
            Phase("att_o", panels // 2, [(att_o, 0, 2), (att_o, 1, 2)]),
            Phase("conv_o", panels // 2, [(conv_o, 0, 2), (conv_o, 1, 2)]),
            Phase("out_2", panels // 2, [(out_2, 0, 2), (out_2, 1, 2)]),
            Phase("gate_up", D_FF2 // CW, [(gate_l, 0, 1), (up_l, 0, 1)]),
            Phase("down_2", panels // 2, [(down2, 0, 2), (down2, 1, 2)]),
        ])
        by_name = {ph.name: ph for ph in phases}

        def panels_before(name):
            return by_name[name].panel0

        def panels_through(name):
            ph = by_name[name]
            return ph.panel0 + ph.n_panels * ph.iters

        landed = [sem(f"landed{s}") for s in range(SLOTS)]
        hi_ready = sem("hi_ready")
        lo_ready = sem("lo_ready")
        chunk_used = sem("chunk_used")
        half_ready = sem("half_ready")
        summed = sem("summed")
        mod_half_ready = sem("mod_half_ready")
        mod_summed = sem("mod_summed")
        extra = sem("extra")
        sigmoid_ready = sem("sigmoid_ready")

        def chunk_seq(ph, it, j):
            return ph.chunk0 + it * ph.n_chunks + j

        def freed(ph, it, j, first):
            if j >= SLOTS:
                return chunk_seq(ph, it, j - SLOTS) + 1
            if first:
                before = ph.last_before[j % SLOTS]
                return None if before is None else before + 1
            return chunk_seq(ph, it - 1, max(i for i in range(ph.n_chunks) if i % SLOTS == j % SLOTS)) + 1

        def panel_seq(ph, it, b):
            is_mod = ph.body[b][0].kind == "mod"
            before = sum((x.kind == "mod") == is_mod for x, _, _ in ph.body[:b])
            if is_mod:
                return ph.mod0 + it * ph.n_mods + before
            return ph.panel0 + it * ph.n_panels + before

        def extra_seq(ph, it, b):
            return ph.extra0 + it * ph.n_extra + sum(EXTRA[x.kind] for x, _, _ in ph.body[:b])

        def bank_pair(ph, b):
            return (ph.panel0 + sum(x.kind != "mod" for x, _, _ in ph.body[:b])) % 2

        def summed_all(name):
            ph = by_name[name]
            return ph.panel0 + ph.n_panels * ph.iters

        def extra_all(name):
            ph = by_name[name]
            return ph.extra0 + ph.n_extra * ph.iters

        def column(name, i=0, n=1):
            return cols[:, COLUMN[name] + i:COLUMN[name] + i + n]

        class Count:

            def __init__(self, sem_, base=0):
                self.sem, self.base = sem_, base

            def __call__(self, n):
                return self.sem, self.base + n

        UNITS = 2 * HEADS
        shared = {}

        def count(name, steps):
            if name not in shared:
                shared[name] = [sem(name), 0]
            c = Count(*shared[name])
            shared[name][1] += steps
            return c

        class Norm:

            def __init__(self, src, tiles, dim):
                self.src, self.tiles, self.dim = src, tiles, dim
                self.squared = count("norm_squared", tiles)
                self.added = count("norm_added", tiles)
                self.stat = count("norm_stat", 3)

        class Apply:

            def __init__(self, src, tiles, gain, dst, shift=None):
                self.src, self.tiles, self.gain, self.dst, self.shift = src, tiles, gain, dst, shift
                self.scaled = count("apply_scaled", tiles)
                self.hi = count("apply_hi", tiles)
                self.lo = count("apply_lo", tiles)

        class Residual:

            def __init__(self, src):
                self.src = src
                self.scaled = count("residual_scaled", DT)
                self.added = count("residual_added", 4)

        class Split:

            def __init__(self, src, tiles, dst):
                self.src, self.tiles, self.dst = src, tiles, dst
                self.hi = count("split_hi", tiles // 2)
                self.lo = count("split_lo", tiles // 2)

        class Attention:

            def __init__(self, v, v_tok, prob, prob_t, scale, bias=None):
                self.v, self.v_tok, self.prob, self.prob_t = v, v_tok, prob, prob_t
                self.scale, self.bias = scale, bias
                self.v_turned = count("att_v_turned", UNITS)
                self.v_moved = count("att_v_moved", 4)
                self.scores = count("att_scores", UNITS)
                self.biased = count("att_biased", UNITS if bias is not None else 0)
                self.maxed = count("att_maxed", 2 * UNITS)
                self.exped = count("att_exped", UNITS)
                self.inverted = count("att_inverted", UNITS)
                self.normed = count("att_normed", UNITS)
                self.turned = count("att_turned", UNITS)
                self.moved = count("att_moved", UNITS)
                self.out = count("att_out", HEADS)
                self.hi = count("att_hi", HEADS)
                self.lo = count("att_lo", HEADS)

        n_x1 = Norm(x_res, DT, D)
        a_x1 = Apply(x_res, DT, gains, acts, (mods, 0))
        n_q = Norm(proj, 4, Q_RANK)
        n_kv = Norm(proj[:, 4:6, :], 2, KV_RANK)
        a_q = Apply(proj, 4, column("q_norm_g", 0, 4), lat)
        a_kv = Apply(proj[:, 4:6, :], 2, column("kv_norm_g", 0, 2), lat[:, 4:6])
        att1 = Attention(kv1[:, :, 1, :], v1_tok, prob1, prob1_t, MLA_SCALE)
        n_y1 = Norm(y1, DT, D)
        r_y1 = Residual(y1)
        n_x2 = Norm(x_res, DT, D)
        a_x2 = Apply(x_res, DT, gains, acts, (mods, 3 * DT))
        n_m1 = Norm(ym1, DT, D)
        r_m1 = Residual(ym1)
        n_x3 = Norm(x_res, DT, D)
        a_x3 = Apply(x_res, DT, column("mix_pre_g_2", 0, DT), acts)
        att2 = Attention(v2, v2_tok, prob2, prob2_t, NA_SCALE, bias)
        s_conv = Split(zc, HEADS, acts[:, HEADS:2 * HEADS])
        s_merged = Split(gate2, DT, acts)
        n_y2 = Norm(y2, DT, D)
        r_y2 = Residual(y2)
        n_x4 = Norm(x_res, DT, D)
        a_x4 = Apply(x_res, DT, column("ffn_pre_g_2", 0, DT), acts)
        n_m2 = Norm(ym2, DT, D)
        r_m2 = Residual(ym2)

        dve_chain, act_chain = sem("dve_chain"), sem("act_chain")
        loads = sem("loads")
        const_set, cols_turned, cols_moved, x_turned, x_moved = map(
            sem, ("const_set", "cols_turned", "cols_moved", "x_turned", "x_moved"))
        c_sig, c_silu, c_hi, c_lo, mods_done, gain_done = map(
            sem, ("c_sig", "c_silu", "c_hi", "c_lo", "mods_done", "gain_done"))
        lb_diff, lb_sig, f_sig, f_done, k_done, ksum_done, q_done = map(
            sem, ("lb_diff", "lb_sig", "f_sig", "f_done", "k_done", "ksum_done", "q_done"))
        diag_mm, diag_moved = map(sem, ("diag_mm", "diag_moved"))
        ho_stat, ln_stat = Count(sem("ho_stat")), Count(sem("ln_stat"))
        hv_turned, hv_moved = Count(sem("hv_turned")), Count(sem("hv_moved"))
        level_mm, level_selected, level_updated, off_mm, off_moved = map(
            sem, ("level_mm", "level_selected", "level_updated", "off_mm", "off_moved"))
        ho_mm, ho_moved, ho_sq, ho_sum, hg_sig, h_out, h_hi, h_lo = map(
            sem, ("ho_mm", "ho_moved", "ho_sq", "ho_sum", "hg_sig", "h_out", "h_hi", "h_lo"))
        pos_landed, angles, sines, rot_mm, rot_done = map(
            sem, ("pos_landed", "angles", "sines", "rot_mm", "rot_done"))
        bias_landed, bias_mm, bias_done, cb_sig, z_done, z_moved, pads_set, conv_step, conv_done = map(
            sem, ("bias_landed", "bias_mm", "bias_done", "cb_sig", "z_done", "z_moved", "pads_set", "conv_step",
                  "conv_done"))
        ln_mm, ln_mean, ln_center, ln_sq, ln_norm, ln_bias, ln_sig, gates_sig = map(
            sem, ("ln_mm", "ln_mean", "ln_center", "ln_sq", "ln_norm", "ln_bias", "ln_sig",
                  "gates_sig"))
        out_turned, out_moved, out_stored = map(sem, ("out_turned", "out_moved", "out_stored"))

        bias_rows = bias[:].rearrange("p s h i c -> p (s h i c)").rearrange("p (n w) -> p n w", w=512)

        block = ctx.enter_context(nc.Block())

        @block.sync
        def _(sp):
            n_loads = 0
            sp.dma_start(consts[:, :], d["consts"]).then_inc(loads, 16)
            sp.dma_start(masks_i[:, :], d["masks"]).then_inc(loads, 16)
            for name, rows in VECTORS:
                src = d[name].rearrange("a (r p) -> (a r) p", p=P) if name != "w_dw_2" else \
                    d[name][0].rearrange("j (r p) -> (j r) p", p=P)
                row = COLUMN[name]
                done = 0
                while done < rows:
                    tile, at_row = divmod(row + done, P)
                    n = min(rows - done, P - at_row)
                    sp.dma_start(v_rows[at_row:at_row + n, tile, :], src[done:done + n, :]).then_inc(loads, 16)
                    done += n
            for half in range(2):
                sp.dma_start(x_nat[:, half, :], d["x"][0, half * P:(half + 1) * P, :]).then_inc(loads, 16)

            def chunk(ph, it, j, first):
                b, k0, kn = ph.chunks[j]
                lin_, p0, stride = ph.body[b]
                free = freed(ph, it, j, first)
                if free is not None:
                    sp.wait_ge(lo_ready, free)
                row = (lin_.row_tile + k0) * P
                panel = p0 + it * stride
                src = lin_.w[row:row + kn * P, bass.ds(panel * lin_.step + lin_.col0, lin_.width)]
                slot = j % SLOTS
                sp.dma_start(w_raw[:, slot, 0:kn, 0:lin_.width],
                             src.rearrange("(k p) n -> p k n", p=P)).then_inc(landed[slot], 16)

            for ph in phases:
                for j in range(ph.n_chunks):
                    chunk(ph, 0, j, True)
                if ph.iters > 1:
                    with sp.Fori(1, ph.iters) as it:
                        for j in range(ph.n_chunks):
                            chunk(ph, it, j, False)
            for half in range(2):
                sp.wait_ge(out_moved, 4 * (half + 1))
                sp.dma_start(out[0, half * P:(half + 1) * P, :], y_nat[:, half, :]).then_inc(out_stored, 16)
            sp.wait_ge(out_stored, 32)

        @block.gpsimd
        def _(pool):
            pool.wait_ge(h_lo, 1)
            pool.dma_start(pos_i[ROPE:P, :],
                           d["positions"][0:1, :].to_broadcast([ROPE, T])).then_inc(pos_landed, 16)
            pool.wait_ge(*r_m1.added(4))
            for r in range(GRID_ROWS):
                for i in range(GRID_ROWS):
                    src = bass.AP(d["rpb_2"].tensor,
                                  (i - r + WIN_R - 1) * RPB_W + WIN_C - 1 - (GRID_W - 1),
                                  [[1, GRID_W], [RPB_H * RPB_W, HEADS], [1, GRID_W]])
                    rows = slice((r % 2) * GRID_W, (r % 2 + 1) * GRID_W)
                    pool.dma_start(bias[rows, r // 2, :, i, :], src).then_inc(bias_landed, 16)

        @block.tensor
        def _(pe):
            def panel(ph, it, b, first):
                lin_ = ph.body[b][0]
                seq, pair = panel_seq(ph, it, b), bank_pair(ph, b)
                is_mod = lin_.kind == "mod"
                if is_mod:
                    pair = b % 2
                    if not (first and ph.mod0 + b < 2):
                        pe.wait_ge(mod_summed, seq - 1)
                elif not (first and ph.panel0 + b < 2):
                    pe.wait_ge(summed, seq - 1)
                ids = chunk_ids(ph, b)
                for j in ids:
                    _, k0, kn = ph.chunks[j]
                    slot = j % SLOTS
                    pe.wait_ge(lo_ready, chunk_seq(ph, it, j) + 1)
                    for k in range(kn):
                        kk = k0 + k
                        at_first, at_last = j == ids[0] and k == 0, j == ids[-1] and k == kn - 1
                        for n, c in enumerate(lin_.tiles):
                            hi = w_hi[:, slot, k, c:c + P]
                            lo = w_lo[:, slot, k, c:c + P]
                            if is_mod:
                                o = ps[:, 4 + pair * 2 + n, 0:2]
                                pe.matmul(o, hi, cond[:, kk, :], start=at_first, stop=False)
                                mm = pe.matmul(o, lo, cond[:, kk, :], start=False, stop=at_last)
                            else:
                                bank = 2 * pair + n
                                pe.matmul(ps[:, bank, :], hi, lin_.act[:, kk, :, :], start=at_first,
                                          stop=False, skip_group_check=True)
                                mm = pe.matmul(ps[:, bank, 0:T], lo, lin_.act[:, kk, 0, :], start=False,
                                               stop=at_last, skip_group_check=True)
                    mm.then_inc(chunk_used, 1)

            def norm(n):
                for k in range(n.tiles):
                    pe.wait_ge(*n.squared(k + 1))
                    pe.matmul(ps[:, 5, 0:T], ones[:, :], ring[:, k % 4, :], start=k == 0,
                              stop=k == n.tiles - 1).then_inc(n.added.sem, 1)

            def turn_values(tiles, done, wait=None):
                for i in range(2 * HEADS):
                    half, h = divmod(i, HEADS)
                    pe.transpose(ps[:, 4 + i // 4, (i % 4) * P:(i % 4 + 1) * P],
                                 tiles[:, h, half * P:(half + 1) * P], ident).then_inc(done.sem, 1)

            def attention(a, scores):
                def pv(h):
                    pe.wait_ge(*a.moved(2 * h + 2))
                    if h >= 1:
                        pe.wait_ge(*a.lo(h))
                    for s in range(2):
                        mm = pe.matmul(ps[:, 7, 0:T], a.v_tok[:, s, h, :], a.prob_t[:, h % 2, s, :],
                                       start=s == 0, stop=s == 1)
                    mm.then_inc(a.out.sem, 1)

                for u in range(UNITS + 3):
                    if u < UNITS:
                        if u >= 2:
                            pe.wait_ge(*a.exped(u - 1))
                        scores(u // 2, u % 2, ps[:, 4 + u % 2, 0:T]).then_inc(a.scores.sem, 1)
                    if 1 <= u <= UNITS:
                        v = u - 1
                        pe.wait_ge(*a.normed(v + 1))
                        if v >= 1:
                            pe.wait_ge(*a.moved(v))
                        for s in range(2):
                            mm = pe.transpose(ps[:, 6, s * P:(s + 1) * P],
                                              a.prob[:, v % 2, s * P:(s + 1) * P], ident)
                        mm.then_inc(a.turned.sem, 1)
                    if u >= 3 and u % 2 == 1:
                        pv((u - 3) // 2)

            def start():
                pe.wait_ge(loads, 16 * N_LOADS)
                for t in range(V_TILES):
                    rows = min(P, N_COLUMNS - t * P)
                    pe.transpose(ps[:, t // 4, (t % 4) * P:(t % 4) * P + rows], v_rows[0:rows, t, :],
                                 consts[0:rows, C_IDENT:C_IDENT + rows]).then_inc(cols_turned, 1)
                pe.wait_ge(cols_moved, V_TILES)
                for g in range(8):
                    half, b4 = divmod(g, 4)
                    if g >= 4:
                        pe.wait_ge(x_moved, g - 3)
                    for i in range(4):
                        mm = pe.transpose(ps[:, b4, i * P:(i + 1) * P],
                                          x_nat[:, half, (4 * b4 + i) * P:(4 * b4 + i + 1) * P], ident)
                    mm.then_inc(x_turned, 1)
                pe.wait_ge(c_lo, 1)

            def before_in_h():
                pe.wait_ge(x_moved, 8)
                pe.wait_ge(mods_done, 1)
                norm(n_x1)
                pe.wait_ge(*a_x1.lo(DT))

            def hgrn():
                turn_values(hv, hv_turned)
                pe.wait_ge(*hv_moved(4))
                pe.wait_ge(ksum_done, 1)
                for h in range(HEADS):
                    for half in range(2):
                        i = 2 * h + half
                        cut = slice(half * P, (half + 1) * P)
                        pe.matmul(ps[:, 4 + i // 4, (i % 4) * P:(i % 4 + 1) * P], qb[:, h, cut],
                                  hq[:, h, cut], start=True, stop=True).then_inc(diag_mm, 1)
                pe.wait_ge(diag_moved, 4)
                for n, m in enumerate(LEVELS):
                    for way in range(2):
                        if n == 0:
                            pe.wait_ge(q_done, 2)
                        else:
                            pe.wait_ge(level_updated, 6 * (n - 1) + 3 * (way + 1))
                        kk, qq = ((kf, hq), (kb, qb))[way]
                        for i in range(2 * HEADS):
                            h, half = divmod(i, 2)
                            q_ = qq[:, h, half * P:(half + 1) * P].rearrange("p (b two m) -> p b two m", two=2, m=m)
                            o = ps[:, 4 + 2 * way + i // 8, (i % 8) * 64:(i % 8 + 1) * 64]
                            mm = pe.matmul(o, kk[:, h, half * P:(half + 1) * P], q_[:, :, 1 - way, :],
                                           start=True, stop=True)
                        mm.then_inc(level_mm, 1)
                pe.wait_ge(level_updated, 6 * len(LEVELS))
                for way in range(2):
                    kk, qq = ((kf, hq), (kb, qb))[way]
                    for h in range(HEADS):
                        s, t = (0, P) if way == 0 else (P, 0)
                        mm = pe.matmul(ps[:, 4 + 2 * way + h // 4, (h % 4) * P:(h % 4 + 1) * P],
                                       kk[:, h, s:s + P], qq[:, h, t:t + P], start=True, stop=True)
                    mm.then_inc(off_mm, 1)
                pe.wait_ge(off_moved, 4)
                for h in range(HEADS):
                    for t in range(2):
                        o = ps[:, 4 + h // 2, (h % 2) * T + t * P:(h % 2) * T + (t + 1) * P]
                        pe.matmul(o, hv_tok[:, t, h, :], a_diag[:, h, t, :], start=True, stop=False)
                        mm = pe.matmul(o, hv_tok[:, 1 - t, h, :], a_off[:, 1 - t, h, :], start=False, stop=True)
                    mm.then_inc(ho_mm, 1)
                pe.wait_ge(ho_sq, 1)
                for h in range(HEADS):
                    pe.matmul(ps[:, 4 + h // 2, (h % 2) * T:(h % 2 + 1) * T], ones[:, :], kf[:, h, :],
                              start=True, stop=True).then_inc(ho_sum, 1)

            def before_uq():
                pe.wait_ge(summed, summed_all("in_m"))
                hgrn()
                pe.wait_ge(*ho_stat(1))
                norm(n_q)
                pe.wait_ge(*n_q.stat(1))
                norm(n_kv)
                pe.wait_ge(*a_q.lo(4))
                pe.wait_ge(*a_kv.lo(2))

            def before_w_o():
                pe.wait_ge(summed, summed_all("ukv"))
                for first_, tiles, n in ((0, proj[ROPE:P, 6:7, :], 1), (1, q1, 4)):
                    for i in range(n):
                        rhs = proj[ROPE:P, 6, :] if n == 1 else q1[ROPE:P, 2 * i:2 * i + 2, 1, :]
                        width = T if n == 1 else 2 * T
                        if n == 4 and i == 0:
                            pe.wait_ge(rot_done, 3)
                        pe.matmul(ps[ROPE:P, 4 + i, 0:width], consts[ROPE:P, C_RT:C_RT + ROPE], rhs,
                                  start=True, stop=True).then_inc(rot_mm, 1)
                pe.wait_ge(rot_done, 6)
                turn_values(att1.v, att1.v_turned)

                def scores(h, half, o):
                    q_ = slice(half * P, (half + 1) * P)
                    pe.matmul(o, q1[:, h, 0, q_], kv1[:, h, 0, :], start=True, stop=False)
                    return pe.matmul(o, q1[ROPE:P, h, 1, q_], proj[ROPE:P, 6, :], start=False, stop=True)

                pe.wait_ge(*att1.v_moved(4))
                attention(att1, scores)
                pe.wait_ge(*att1.lo(HEADS))
                pe.wait_ge(h_lo, 1)

            def next_norm(name, kind_sem, total, n, a, r):
                pe.wait_ge(kind_sem, total)
                norm(n)
                pe.wait_ge(*r.added(4))

            def before_up_0():
                pe.wait_ge(summed, summed_all("w_o"))
                norm(n_y1)
                pe.wait_ge(*r_y1.added(4))
                norm(n_x2)
                pe.wait_ge(*a_x2.lo(DT))

            def before_in_2():
                pe.wait_ge(extra, extra_all("down_1"))
                norm(n_m1)
                pe.wait_ge(*r_m1.added(4))
                norm(n_x3)
                pe.wait_ge(*a_x3.lo(DT))

            def before_att_o():
                pe.wait_ge(summed, summed_all("in_2"))
                turn_values(att2.v, att2.v_turned)

                def scores(h, half, o):
                    return pe.matmul(o, q2[:, h, half * P:(half + 1) * P], k2[:, h, :], start=True, stop=True)

                pe.wait_ge(*att2.v_moved(4))
                pe.wait_ge(bias_landed, 16 * GRID_ROWS ** 2)
                for i in range(8):
                    if i >= 4:
                        pe.wait_ge(bias_done, i - 3)
                    pe.matmul(ps[:, 4 + i % 4, :], consts[:, C_FLIP:C_FLIP + P], bias_rows[:, i, :],
                              start=True, stop=True).then_inc(bias_mm, 1)
                pe.wait_ge(bias_done, 8)
                attention(att2, scores)
                pe.wait_ge(*att2.lo(HEADS))
                pe.wait_ge(conv_done, 1)
                for k in range(HEADS):
                    mm = pe.matmul(ps[:, 4, 0:T], ones[:, :], zc[:, k, :], start=k == 0, stop=k == HEADS - 1)
                mm.then_inc(ln_mm, 1)
                for k in range(HEADS):
                    pe.wait_ge(ln_sq, k + 1)
                    mm = pe.matmul(ps[:, 5, 0:T], ones[:, :], ring[:, k % 4, :], start=k == 0,
                                   stop=k == HEADS - 1).then_inc(ln_mm, 1)
                pe.wait_ge(*s_conv.lo(4))

            def before_out_2():
                pe.wait_ge(*s_merged.lo(8))

            def before_gate_up():
                pe.wait_ge(summed, summed_all("out_2"))
                norm(n_y2)
                pe.wait_ge(*r_y2.added(4))
                norm(n_x4)
                pe.wait_ge(*a_x4.lo(DT))

            hooks = {
                "mod": start, "in_h": before_in_h, "uq": before_uq, "w_o": before_w_o,
                "up_0": before_up_0, "down_0": lambda: pe.wait_ge(extra, extra_all("up_0")),
                "down_1": lambda: pe.wait_ge(extra, extra_all("up_1")), "in_2": before_in_2,
                "att_o": before_att_o, "out_2": before_out_2, "gate_up": before_gate_up,
                "down_2": lambda: pe.wait_ge(extra, extra_all("gate_up")),
            }
            for ph in phases:
                hooks.get(ph.name, lambda: None)()
                for b in range(len(ph.body)):
                    panel(ph, 0, b, True)
                if ph.iters > 1:
                    with pe.Fori(1, ph.iters) as it:
                        for b in range(len(ph.body)):
                            panel(ph, it, b, False)
            pe.wait_ge(summed, summed_all("down_2"))
            norm(n_m2)
            pe.wait_ge(*r_m2.added(4))
            for g in range(8):
                half, b4 = divmod(g, 4)
                if g >= 4:
                    pe.wait_ge(out_moved, g - 3)
                for i in range(4):
                    mm = pe.transpose(ps[:, b4, i * P:(i + 1) * P],
                                      x_res[:, 4 * b4 + i, half * P:(half + 1) * P], ident)
                mm.then_inc(out_turned, 1)

        @block.scalar
        def _(act):
            def split(ph, it, b, first, ids):
                lin_ = ph.body[b][0]
                for j in ids:
                    kn, slot = ph.chunks[j][2], j % SLOTS
                    uses = ph.use0[slot] + it * ph.slot_uses[slot] + j // SLOTS + 1
                    act.wait_ge(landed[slot], uses * 16)
                    free = freed(ph, it, j, first)
                    if free is not None:
                        act.wait_ge(chunk_used, free)
                    act.copy(w_hi[:, slot, 0:kn, 0:lin_.width],
                             w_raw[:, slot, 0:kn, 0:lin_.width]).then_inc(hi_ready, 1)

            def evict(ph, it, b, first):
                lin_ = ph.body[b][0]
                seq = panel_seq(ph, it, b)
                act.wait_ge(chunk_used, chunk_seq(ph, it, chunk_ids(ph, b)[-1]) + 1)
                if lin_.kind == "mod":
                    if not (first and ph.mod0 + b < 1):
                        act.wait_ge(mod_summed, seq)
                    act.copy(mod_half[:, :], ps[:, 4 + 2 * (b % 2):6 + 2 * (b % 2), 1]).then_inc(mod_half_ready, 1)
                    return
                pair, n = bank_pair(ph, b), len(lin_.tiles)
                if not (first and ph.panel0 + b < 2):
                    act.wait_ge(summed, seq - 1)
                act.copy(half_sum[:, pair, 0:n, :], ps[:, 2 * pair:2 * pair + n, T:2 * T]).then_inc(half_ready, 1)
                if lin_.kind == "gate":
                    act.wait_ge(summed, seq + 1)
                    if not first:
                        act.wait_ge(extra, extra_seq(ph, it, b))
                    act.activation(gate3[:, :, :], lin_.tmp[:, pair, :, :], ACT.Sigmoid).then_inc(sigmoid_ready, 1)

            def root(ap, stat):
                act.wait_ge(*stat(1))
                act.activation(ap, ap, ACT.Sqrt).then_inc(stat.sem, 1)

            def norm(n):
                for k in range(n.tiles):
                    if k >= 4:
                        act.wait_ge(*n.added(k - 3))
                    act.activation(ring[:, k % 4, :], n.src[:, k, :], ACT.Square).then_inc(n.squared.sem, 1)
                root(rstd[:, :], n.stat)

            def apply(a):
                for k in range(a.tiles):
                    act.wait_ge(*a.scaled(k + 1))
                    if a.shift is None:
                        act.copy(a.dst[:, k, 0, :], ring[:, k % 4, :]).then_inc(a.hi.sem, 1)
                    else:
                        tile, c0 = a.shift
                        act.activation(a.dst[:, k, 0, :], ring[:, k % 4, :], ACT.Identity,
                                       bias=tile[:, c0 + k:c0 + k + 1]).then_inc(a.hi.sem, 1)

            def split_tiles(s):
                for k in range(0, s.tiles, 2):
                    act.copy(s.dst[:, k:k + 2, 0, :], s.src[:, k:k + 2, :]).then_inc(s.hi.sem, 1)

            def move_values(tok, turned, moved):
                flat = tok.rearrange("p s h d -> p (s h d)")
                for i in range(4):
                    act.wait_ge(*turned(4 * i + 4))
                    act.copy(flat[:, i * 512:(i + 1) * 512], ps[:, 4 + i, :]).then_inc(moved.sem, 1)

            def attention(a):
                move_values(a.v_tok[:], a.v_turned, a.v_moved)
                for u in range(UNITS + 5):
                    if u < UNITS:
                        act.wait_ge(*a.maxed(2 * u + 2))
                        if u >= 2:
                            act.wait_ge(*a.turned(u - 1))
                        src = ps[:, 4 + u % 2, 0:T] if a.bias is None else a.prob[:, u % 2, :]
                        act.activation(a.prob[:, u % 2, :], src, ACT.Exp, bias=small[:, u, 1:2],
                                       scale=a.scale if a.bias is None else 1.0,
                                       accum_out=small[:, u, 2:3]).then_inc(a.exped.sem, 1)
                    if 2 <= u < UNITS + 2:
                        v = u - 2
                        h, half = divmod(v, 2)
                        act.wait_ge(*a.turned(v + 1))
                        if h >= 2:
                            act.wait_ge(*a.out(h - 1))
                        act.copy(a.prob_t[:, h % 2, :, half * P:(half + 1) * P],
                                 ps[:, 6, 0:T].rearrange("p (s q) -> p s q", s=2)).then_inc(a.moved.sem, 1)
                    if u >= 4 and u % 2 == 0 and (u - 4) // 2 < HEADS:
                        h = (u - 4) // 2
                        act.wait_ge(*a.out(h + 1))
                        act.copy(acts[:, h, 0, :], ps[:, 7, 0:T]).then_inc(a.hi.sem, 1)

            def start():
                for t in range(V_TILES):
                    rows = min(P, N_COLUMNS - t * P)
                    act.wait_ge(cols_turned, V_TILES)
                    act.copy(cols[:, t * P:t * P + rows],
                             ps[:, t // 4, (t % 4) * P:(t % 4) * P + rows]).then_inc(cols_moved, 1)
                act.wait_ge(cols_moved, V_TILES)
                act.activation(silu_c[:, 0:DT], column("c", 0, DT), ACT.Sigmoid).then_inc(c_sig, 1)
                act.wait_ge(c_silu, 1)
                act.copy(cond[:, :, 0], silu_c[:, DT:2 * DT]).then_inc(c_hi, 1)
                for g in range(8):
                    half, b4 = divmod(g, 4)
                    act.wait_ge(x_turned, g + 1)
                    act.copy(x_res[:, 4 * b4:4 * b4 + 4, half * P:(half + 1) * P],
                             ps[:, b4, :].rearrange("p (i t) -> p i t", i=4)).then_inc(x_moved, 1)

            def before_in_h():
                act.wait_ge(x_moved, 8)
                act.wait_ge(mods_done, 1)
                norm(n_x1)
                apply(a_x1)

            def hgrn():
                act.wait_ge(lb_diff, 2)
                act.activation(lb[:, 0, :], lb[:, 0, :], ACT.Sigmoid).then_inc(lb_sig, 1)
                act.activation(lb[:, 2, :], lb[:, 2, :], ACT.Sigmoid).then_inc(lb_sig, 1)
                act.activation(hf[:, :, :], hf[:, :, :], ACT.Sigmoid).then_inc(f_sig, 1)
                act.activation(hb[:, :, :], hb[:, :, :], ACT.Sigmoid).then_inc(f_sig, 1)
                move_values(hv_tok[:], hv_turned, hv_moved)
                flat = a_diag[:].rearrange("p h s t -> p (h s t)")
                for i in range(4):
                    act.wait_ge(diag_mm, 16)
                    act.copy(flat[:, i * 512:(i + 1) * 512], ps[:, 4 + i, :]).then_inc(diag_moved, 1)
                flat = a_off[:].rearrange("p s h t -> p (s h t)")
                for i in range(4):
                    act.wait_ge(off_mm, i // 2 + 1)
                    act.copy(flat[:, i * 512:(i + 1) * 512], ps[:, 4 + i, :]).then_inc(off_moved, 1)
                flat = qb[:].rearrange("p h t -> p (h t)")
                for i in range(4):
                    act.wait_ge(ho_mm, HEADS)
                    act.copy(flat[:, i * 512:(i + 1) * 512], ps[:, 4 + i, :]).then_inc(ho_moved, 1)
                act.wait_ge(ho_moved, 4)
                act.activation(kf[:, :, :], qb[:, :, :], ACT.Square).then_inc(ho_sq, 1)
                act.activation(hf[:, :, :], hg[:, :, :], ACT.Sigmoid).then_inc(hg_sig, 1)
                root(kb[:].rearrange("p h t -> p (h t)"), ho_stat)
                act.wait_ge(h_out, 3)
                act.copy(acts[:, HEADS:2 * HEADS, 0, :], qb[:, :, :]).then_inc(h_hi, 1)

            def before_uq():
                act.wait_ge(summed, summed_all("in_m"))
                hgrn()
                norm(n_q)
                apply(a_q)
                act.wait_ge(*a_q.lo(4))
                norm(n_kv)
                apply(a_kv)

            def before_w_o():
                act.wait_ge(angles, 2)
                act.activation(cos_sin[ROPE:P, :, :], ang[ROPE:P, 0:2, :], ACT.Sin).then_inc(sines, 1)
                attention(att1)

            def before_up_0():
                act.wait_ge(summed, summed_all("w_o"))
                norm(n_y1)
                act.wait_ge(*r_y1.added(4))
                norm(n_x2)
                apply(a_x2)

            def before_in_2():
                act.wait_ge(extra, extra_all("down_1"))
                norm(n_m1)
                act.wait_ge(*r_m1.added(4))
                norm(n_x3)
                apply(a_x3)

            def before_att_o():
                act.wait_ge(summed, summed_all("in_2"))
                act.activation(cb, cb, ACT.Sigmoid).then_inc(cb_sig, 1)
                act.activation(gate2[:, 0:DT, :], gate2[:, 0:DT, :], ACT.Sigmoid).then_inc(gates_sig, 1)
                act.activation(gate2[:, DT:, :], gate2[:, DT:, :], ACT.Sigmoid).then_inc(gates_sig, 1)
                attention(att2)
                act.wait_ge(z_done, 1)
                act.wait_ge(pads_set, 1)
                act.copy(zpad[:, :, PAD:PAD + T], ca).then_inc(z_moved, 1)
                for k in range(HEADS):
                    act.wait_ge(ln_center, k + 1)
                    if k >= 4:
                        act.wait_ge(ln_mm, 1 + k - 3)
                    act.activation(ring[:, k % 4, :], zc[:, k, :], ACT.Square).then_inc(ln_sq, 1)
                root(rstd[:, :], ln_stat)
                act.wait_ge(ln_bias, HEADS)
                act.activation(cb, zc, ACT.Sigmoid).then_inc(ln_sig, 1)
                act.wait_ge(ln_norm, HEADS + 1)
                split_tiles(s_conv)

            def before_out_2():
                act.wait_ge(extra, extra_all("conv_o"))
                split_tiles(s_merged)

            def before_gate_up():
                act.wait_ge(summed, summed_all("out_2"))
                norm(n_y2)
                act.wait_ge(*r_y2.added(4))
                norm(n_x4)
                apply(a_x4)

            hooks = {"mod": start, "in_h": before_in_h, "uq": before_uq, "w_o": before_w_o,
                     "up_0": before_up_0, "in_2": before_in_2, "att_o": before_att_o,
                     "out_2": before_out_2, "gate_up": before_gate_up}
            follow_stream(act, phases, split, evict, hooks)
            act.wait_ge(summed, summed_all("down_2"))
            norm(n_m2)
            for g in range(8):
                half, b4 = divmod(g, 4)
                act.wait_ge(out_turned, g + 1)
                act.copy(y_nat[:, half, b4 * 512:(b4 + 1) * 512], ps[:, b4, :]).then_inc(out_moved, 1)

        @block.vector
        def _(dve):
            count = [0]

            def link(ins):
                ins.then_inc(dve_chain, 1)
                count[0] += 1
                dve.wait_ge(dve_chain, count[0])

            def split(ph, it, b, first, ids):
                lin_ = ph.body[b][0]
                for j in ids:
                    kn, slot = ph.chunks[j][2], j % SLOTS
                    dve.wait_ge(hi_ready, chunk_seq(ph, it, j) + 1)
                    cut = (slice(None), slot, slice(0, kn), slice(0, lin_.width))
                    dve.tensor_tensor(w_lo[cut], w_raw[cut], w_hi[cut].bitcast(F32),
                                      ALU.subtract).then_inc(lo_ready, 1)

            def evict(ph, it, b, first):
                lin_, p0, stride = ph.body[b]
                seq = panel_seq(ph, it, b)
                if lin_.kind == "mod":
                    dve.wait_ge(mod_half_ready, seq + 1)
                    dve.tensor_tensor(mods[:, bass.ds(2 * (p0 + it * stride), 2)],
                                      ps[:, 4 + 2 * (b % 2):6 + 2 * (b % 2), 0], mod_half[:, :],
                                      ALU.add).then_inc(mod_summed, 1)
                    return
                pair, n = bank_pair(ph, b), len(lin_.tiles)
                tile0 = 2 * (p0 + it * stride)
                tiles = bass.ds(tile0, n)
                ex = extra_seq(ph, it, b)
                high, low = ps[:, 2 * pair:2 * pair + n, 0:T], half_sum[:, pair, 0:n, :]
                dve.wait_ge(half_ready, seq + 1)
                if lin_.kind == "plain":
                    dve.tensor_tensor(lin_.out[:, tiles, :], high, low, ALU.add).then_inc(summed, 1)
                    return
                tmp = lin_.tmp[:, pair, :, :]
                dve.tensor_tensor(tmp, high, low, ALU.add).then_inc(summed, 1)
                dve.wait_ge(summed, seq + 1)
                if lin_.kind == "add":
                    o = lin_.out[:, tiles, :]
                    dve.tensor_tensor(o, o, tmp, ALU.add).then_inc(extra, 1)
                elif lin_.kind == "gated":
                    o = lin_.out[:, tiles, :]
                    dve.tensor_tensor(o, o, tmp, ALU.mult).then_inc(extra, 1)
                elif lin_.kind == "gated_add":
                    dve.tensor_tensor(tmp, tmp, gate2[:, bass.ds(tile0 + DT, n), :], ALU.mult).then_inc(extra, 1)
                    dve.wait_ge(extra, ex + 1)
                    o = lin_.out[:, tiles, :]
                    dve.tensor_tensor(o, o, tmp, ALU.add).then_inc(extra, 1)
                elif lin_.kind == "gate":
                    dve.wait_ge(sigmoid_ready, ph_gate_seq(ph, it) + 1)
                    dve.tensor_tensor(gate3[:, :, :], gate3[:, :, :], tmp, ALU.mult).then_inc(extra, 1)
                else:
                    if lin_.kind == "relu2":
                        dve.scalar_tensor_tensor(tmp, tmp, 0.0, tmp, ALU.max, ALU.mult).then_inc(extra, 1)
                    else:
                        dve.wait_ge(extra, ex)
                        dve.tensor_tensor(tmp, gate3[:, :, :], tmp, ALU.mult).then_inc(extra, 1)
                    dve.wait_ge(extra, ex + 1)
                    hi = lin_.out[:, tiles, 0, :]
                    dve.tensor_scalar(hi, tmp, 1.0, None, ALU.mult).then_inc(extra, 1)
                    dve.wait_ge(extra, ex + 2)
                    dve.tensor_tensor(lin_.out[:, tiles, 1, :], tmp, hi.bitcast(F32), ALU.subtract).then_inc(extra, 1)

            def ph_gate_seq(ph, it):
                return it

            def invert_root(ap, stat):
                dve.wait_ge(*stat(2))
                dve.reciprocal(ap, ap).then_inc(stat.sem, 1)
                dve.wait_ge(*stat(3))

            def norm(n):
                dve.wait_ge(*n.added(n.tiles))
                dve.tensor_scalar(rstd[:, :], ps[:, 5, 0:T], 1.0 / n.dim, EPS, ALU.mult, ALU.add).then_inc(n.stat.sem, 1)
                invert_root(rstd[:, :], n.stat)

            def apply(a):
                def low(k):
                    dve.wait_ge(*a.hi(k + 1))
                    hi = a.dst[:, k, 0, :].bitcast(F32)
                    if a.shift is None:
                        ins = dve.tensor_tensor(a.dst[:, k, 1, :], ring[:, k % 4, :], hi, ALU.subtract)
                    else:
                        tile, c0 = a.shift
                        ins = dve.scalar_tensor_tensor(a.dst[:, k, 1, :], ring[:, k % 4, :],
                                                       tile[:, c0 + k:c0 + k + 1], hi, ALU.add, ALU.subtract)
                    ins.then_inc(a.lo.sem, 1)

                for k in range(a.tiles + 2):
                    if k < a.tiles:
                        if k >= 4:
                            dve.wait_ge(*a.lo(k - 3))
                        dve.scalar_tensor_tensor(ring[:, k % 4, :], a.src[:, k, :], a.gain[:, k:k + 1],
                                                 rstd[:, :], ALU.mult, ALU.mult).then_inc(a.scaled.sem, 1)
                    if k >= 2:
                        low(k - 2)
                dve.wait_ge(*a.lo(a.tiles))

            def residual(r, gain):
                for k in range(DT):
                    dve.scalar_tensor_tensor(r.src[:, k, :], r.src[:, k, :], gain[:, k:k + 1],
                                             rstd[:, :], ALU.mult, ALU.mult).then_inc(r.scaled.sem, 1)
                for j in range(4):
                    dve.wait_ge(*r.scaled(4 * j + 4))
                    cut = slice(4 * j, 4 * j + 4)
                    dve.tensor_tensor(x_res[:, cut, :], x_res[:, cut, :], r.src[:, cut, :],
                                      ALU.add).then_inc(r.added.sem, 1)
                dve.wait_ge(*r.added(4))

            def scale_gain(name, scale):
                link(dve.scalar_tensor_tensor(gains[:, :], mods[:, scale * DT:(scale + 1) * DT], 1.0,
                                              column(name, 0, DT), ALU.add, ALU.mult))

            def gate_gain(name, gate):
                link(dve.tensor_tensor(gains[:, :], mods[:, gate * DT:(gate + 1) * DT],
                                       column(name, 0, DT), ALU.mult))

            def split_tiles(s):
                for n, k in enumerate(range(0, s.tiles, 2)):
                    dve.wait_ge(*s.hi(n + 1))
                    dve.tensor_tensor(s.dst[:, k:k + 2, 1, :], s.src[:, k:k + 2, :],
                                      s.dst[:, k:k + 2, 0, :].bitcast(F32), ALU.subtract).then_inc(s.lo.sem, 1)

            def attention(a):
                for u in range(UNITS + 5):
                    if u < UNITS:
                        dve.wait_ge(*a.scores(u + 1))
                        src = ps[:, 4 + u % 2, 0:T]
                        if a.bias is not None:
                            if u >= 2:
                                dve.wait_ge(*a.turned(u - 1))
                            h, half = divmod(u, 2)
                            dve.scalar_tensor_tensor(
                                a.prob[:, u % 2, :], src, a.scale,
                                a.bias[:, half, h, :, :].rearrange("p i c -> p (i c)"),
                                ALU.mult, ALU.add).then_inc(a.biased.sem, 1)
                            dve.wait_ge(*a.biased(u + 1))
                            src = a.prob[:, u % 2, :]
                        dve.tensor_reduce(small[:, u, 0:1], src, AX.X, ALU.max).then_inc(a.maxed.sem, 1)
                        dve.wait_ge(*a.maxed(2 * u + 1))
                        dve.tensor_scalar(small[:, u, 1:2], small[:, u, 0:1],
                                          -(a.scale if a.bias is None else 1.0), None,
                                          ALU.mult).then_inc(a.maxed.sem, 1)
                    if 1 <= u <= UNITS:
                        v = u - 1
                        dve.wait_ge(*a.exped(v + 1))
                        dve.reciprocal(small[:, v, 3:4], small[:, v, 2:3]).then_inc(a.inverted.sem, 1)
                        dve.wait_ge(*a.inverted(v + 1))
                        dve.tensor_scalar(a.prob[:, v % 2, :], a.prob[:, v % 2, :], small[:, v, 3:4], None,
                                          ALU.mult).then_inc(a.normed.sem, 1)
                    if u >= 4 and u % 2 == 0 and (u - 4) // 2 < HEADS:
                        h = (u - 4) // 2
                        dve.wait_ge(*a.hi(h + 1))
                        dve.tensor_tensor(acts[:, h, 1, :], ps[:, 7, 0:T], acts[:, h, 0, :].bitcast(F32),
                                          ALU.subtract).then_inc(a.lo.sem, 1)

            def start():
                dve.memset(ones[:, :], 1.0).then_inc(const_set, 1)
                dve.wait_ge(const_set, 1)
                dve.wait_ge(loads, 16 * N_LOADS)
                link(dve.tensor_copy(masks[:].rearrange("p a l t -> p (a l t)"), masks_i[:, :]))
                dve.wait_ge(c_sig, 1)
                dve.tensor_tensor(silu_c[:, DT:2 * DT], silu_c[:, 0:DT], column("c", 0, DT),
                                  ALU.mult).then_inc(c_silu, 1)
                dve.wait_ge(c_hi, 1)
                dve.tensor_tensor(cond[:, :, 1], silu_c[:, DT:2 * DT], cond[:, :, 0].bitcast(F32),
                                  ALU.subtract).then_inc(c_lo, 1)

            def before_in_h():
                dve.wait_ge(mod_summed, by_name["mod"].iters * 2)
                dve.tensor_tensor(mods[:, :], mods[:, :], column("b_mod", 0, N_MOD * DT),
                                  ALU.add).then_inc(mods_done, 1)
                dve.wait_ge(mods_done, 1)
                scale_gain("pre_mix_g", 1)
                norm(n_x1)
                apply(a_x1)

            def hgrn():
                for i, name in enumerate(("hgrn_lb_logits_fwd", "hgrn_lb_logits_bwd")):
                    dve.tensor_tensor(lb[:, 2 * i, :], column(name, 0, HEADS), column(name, HEADS, HEADS),
                                      ALU.subtract).then_inc(lb_diff, 1)
                dve.wait_ge(lb_sig, 2)
                for i in range(2):
                    link(dve.tensor_scalar(lb[:, 2 * i + 1, :], lb[:, 2 * i, :], -1.0, 1.0, ALU.mult, ALU.add))
                for i, f in enumerate((hf, hb)):
                    dve.wait_ge(f_sig, i + 1)
                    for h in range(HEADS):
                        dve.tensor_scalar(f[:, h, :], f[:, h, :], lb[:, 2 * i + 1, h:h + 1],
                                          lb[:, 2 * i, h:h + 1], ALU.mult, ALU.add).then_inc(f_done, 1)
                    dve.wait_ge(f_done, HEADS * (i + 1))
                    dve.tensor_scalar((kf, kb)[i][:, :, :], f, -1.0, 1.0, ALU.mult, ALU.add).then_inc(k_done, 1)
                dve.wait_ge(k_done, 2)
                dve.tensor_tensor(qb[:, :, :], kf[:, :, :], kb[:, :, :], ALU.add).then_inc(ksum_done, 1)
                dve.wait_ge(diag_mm, 16)
                dve.tensor_tensor(qb[:, :, :], hq, hb, ALU.mult).then_inc(q_done, 1)
                dve.wait_ge(q_done, 1)
                dve.tensor_tensor(hq, hq, hf, ALU.mult).then_inc(q_done, 1)
                dve.wait_ge(q_done, 2)
                dve.wait_ge(diag_moved, 4)
                updated = 0
                for n, m in enumerate(LEVELS):
                    for way in range(2):
                        kk, qq, ff = ((kf, hq, hf), (kb, qb, hb))[way]
                        late, early = 1 - way, way
                        dve.wait_ge(level_mm, 2 * n + way + 1)
                        if n or way:
                            dve.wait_ge(level_selected, 2 * n + way)
                        a = a_diag[:].rearrange("p h s (b two m) -> p (h s) b two m", two=2, m=m)
                        got = ps[:, 4 + 2 * way:6 + 2 * way, :].rearrange("p k (g b m) -> p (k g) b m", g=8, m=m)
                        mask = masks[:, way, n, :].rearrange("p (g b m) -> p g b m", g=1, m=m)
                        dve.copy_predicated(a[:, :, :, late, :], mask.to_broadcast([P, 2 * HEADS, 64 // m, m]),
                                            got).then_inc(level_selected, 1)

                        q_ = qq[:].rearrange("p h (b two m) -> p (h b) two m", two=2, m=m)
                        k_ = kk[:].rearrange("p h (b two m) -> p (h b) two m", two=2, m=m)
                        f_ = ff[:].rearrange("p h (b two m) -> p (h b) two m", two=2, m=m)
                        count_ = HEADS * T // (2 * m)
                        dve.tensor_tensor(q_[:, :, late, :], q_[:, :, late, :],
                                          f_[:, :, early, 0:1].to_broadcast([P, count_, m]),
                                          ALU.mult).then_inc(level_updated, 1)
                        dve.tensor_tensor(k_[:, :, early, :], k_[:, :, early, :],
                                          f_[:, :, late, 0:1].to_broadcast([P, count_, m]),
                                          ALU.mult).then_inc(level_updated, 1)
                        updated += 2
                        dve.wait_ge(level_updated, updated)
                        dve.tensor_tensor(f_[:, :, 0, 0:1], f_[:, :, 0, 0:1], f_[:, :, 1, 0:1],
                                          ALU.mult).then_inc(level_updated, 1)
                        updated += 1
                dve.wait_ge(level_selected, 2 * len(LEVELS))
                dve.wait_ge(level_updated, updated)
                dve.wait_ge(ho_sum, HEADS)
                flat = kb[:].rearrange("p h t -> p (h t)")
                dve.tensor_scalar(flat, ps[:, 4:8, :].rearrange("p b n -> p (b n)"), 1.0 / P, EPS,
                                  ALU.mult, ALU.add).then_inc(ho_stat.sem, 1)
                invert_root(flat, ho_stat)
                dve.wait_ge(ho_sq, 1)
                dve.scalar_tensor_tensor(qb[:, :, :], qb[:, :, :], column("hgrn_norm_g"), kb[:, :, :],
                                         ALU.mult, ALU.mult).then_inc(h_out, 1)
                dve.wait_ge(hg_sig, 1)
                dve.tensor_tensor(hg, hg, hf, ALU.mult).then_inc(h_out, 1)
                dve.wait_ge(h_out, 2)
                dve.tensor_tensor(qb[:, :, :], qb[:, :, :], hg, ALU.mult).then_inc(h_out, 1)
                dve.wait_ge(h_hi, 1)
                dve.wait_ge(h_out, 3)
                dve.tensor_tensor(acts[:, HEADS:2 * HEADS, 1, :], qb[:, :, :],
                                  acts[:, HEADS:2 * HEADS, 0, :].bitcast(F32), ALU.subtract).then_inc(h_lo, 1)
                dve.wait_ge(h_lo, 1)

            def before_uq():
                dve.wait_ge(summed, summed_all("in_m"))
                hgrn()
                norm(n_q)
                apply(a_q)
                norm(n_kv)
                apply(a_kv)

            def rope_angles():
                r = slice(ROPE, P)
                c1 = 6.28125
                c2 = float(np.float32(np.floor((TWO_PI - c1) * 2 ** 21) / 2 ** 21))
                c3 = TWO_PI - c1 - c2
                magic = 12582912.0
                dve.wait_ge(pos_landed, 16)
                link(dve.tensor_copy(ang[r, 1, :], pos_i[r, :]))
                link(dve.tensor_scalar(ang[r, 1, :], ang[r, 1, :], consts[r, C_FREQ:C_FREQ + 1], None, ALU.mult))
                link(dve.tensor_copy(ang[r, 0, :], ang[r, 1, :]))
                for i, quarter in ((0, 0.25), (1, 0.0)):
                    a, n = ang[r, i, :], ang[r, 2, :]
                    link(dve.tensor_scalar(n, a, 1 / TWO_PI, quarter, ALU.mult, ALU.add))
                    link(dve.tensor_scalar(n, n, magic, None, ALU.add))
                    link(dve.tensor_scalar(n, n, -magic, None, ALU.add))
                    for c in (c1, c2, c3):
                        link(dve.scalar_tensor_tensor(a, n, -c, a, ALU.mult, ALU.add))
                    link(dve.tensor_scalar(a, a, quarter * TWO_PI, 3.1415925, ALU.add, ALU.min))
                    dve.tensor_scalar(a, a, -3.1415925, None, ALU.max).then_inc(angles, 1)
                    dve.wait_ge(angles, i + 1)

            def rotate(x, turned, cos, sin):
                dve.tensor_tensor(rot_of(x), turned, sin, ALU.mult).then_inc(rot_done, 1)
                dve.tensor_tensor(x, x, cos, ALU.mult).then_inc(rot_done, 1)

            def before_w_o():
                rope_angles()
                r = slice(ROPE, P)
                dve.wait_ge(sines, 1)
                dve.wait_ge(summed, summed_all("ukv"))
                dve.wait_ge(rot_mm, 1)
                kr = proj[r, 6, :]
                dve.tensor_tensor(rot[r, 0, :], ps[r, 4, 0:T], cos_sin[r, 1, :], ALU.mult).then_inc(rot_done, 1)
                dve.tensor_tensor(kr, kr, cos_sin[r, 0, :], ALU.mult).then_inc(rot_done, 1)
                dve.wait_ge(rot_done, 2)
                dve.tensor_tensor(kr, kr, rot[r, 0, :], ALU.add).then_inc(rot_done, 1)
                dve.wait_ge(rot_done, 3)
                dve.wait_ge(rot_mm, 5)
                qr = q1[r, :, 1, :]

                def over_heads(i):
                    return cos_sin[r, i:i + 1, :].to_broadcast([ROPE, HEADS, T])

                dve.tensor_tensor(rot[r, :, :], ps[r, 4:8, :].rearrange("p b (h t) -> p (b h) t", t=T),
                                  over_heads(1), ALU.mult).then_inc(rot_done, 1)
                dve.tensor_tensor(qr, qr, over_heads(0), ALU.mult).then_inc(rot_done, 1)
                dve.wait_ge(rot_done, 5)
                dve.tensor_tensor(qr, qr, rot[r, :, :], ALU.add).then_inc(rot_done, 1)
                attention(att1)
                dve.wait_ge(*att1.lo(HEADS))

            def before_up_0():
                dve.wait_ge(summed, summed_all("w_o"))
                gate_gain("post_mix_g", 2)
                norm(n_y1)
                residual(r_y1, gains)
                scale_gain("pre_mlp_g", 4)
                norm(n_x2)
                apply(a_x2)

            def before_in_2():
                dve.wait_ge(extra, extra_all("down_1"))
                gate_gain("post_mlp_g", 5)
                norm(n_m1)
                residual(r_m1, gains)
                norm(n_x3)
                apply(a_x3)

            def convolution():
                dve.wait_ge(*att2.lo(HEADS))
                dve.memset(zpad[:, :, 0:PAD], 0.0).then_inc(pads_set, 1)
                dve.wait_ge(pads_set, 1)
                link(dve.memset(zpad[:, :, PAD + T:], 0.0))
                dve.wait_ge(z_moved, 1)
                for k in range(HEADS):
                    w0 = COLUMN["w_dw_2"] + k
                    dve.tensor_scalar(zc[:, k, :], zpad[:, k, 0:T], cols[:, w0:w0 + 1], column("b_dw_2", k),
                                      ALU.mult, ALU.add).then_inc(conv_step, 1)
                with dve.Fori(1, TAPS) as tap:
                    dve.wait_ge(conv_step, tap * HEADS)
                    for k in range(HEADS):
                        w = cols[:, bass.ds(tap * HEADS + (COLUMN["w_dw_2"] + k), 1)]
                        dve.scalar_tensor_tensor(zc[:, k, :], zpad[:, k, bass.ds(tap, T)], w, zc[:, k, :],
                                                 ALU.mult, ALU.add).then_inc(conv_step, 1)
                dve.wait_ge(conv_step, TAPS * HEADS)

            def before_att_o():
                dve.wait_ge(summed, summed_all("in_2"))
                dve.wait_ge(cb_sig, 1)
                dve.tensor_tensor(ca, ca, cb, ALU.mult).then_inc(z_done, 1)
                outside = consts[:, C_WIN:C_WIN + GRID_W].rearrange("p (o c) -> p o c", o=1)
                for i in range(8):
                    dve.wait_ge(bias_mm, i + 1)
                    dve.tensor_tensor(bias_rows[:, i, :].rearrange("p (n c) -> p n c", c=GRID_W),
                                      ps[:, 4 + i % 4, :].rearrange("p (n c) -> p n c", c=GRID_W),
                                      outside.to_broadcast([P, 512 // GRID_W, GRID_W]),
                                      ALU.add).then_inc(bias_done, 1)
                dve.wait_ge(bias_done, 8)
                dve.wait_ge(z_done, 1)
                attention(att2)
                convolution()
                dve.memset(mean[:, :], 0.0).then_inc(conv_done, 1)
                dve.wait_ge(conv_done, 1)
                dve.wait_ge(ln_mm, 1)
                dve.tensor_scalar(mean[:, :], ps[:, 4, 0:T], 1.0 / (HEADS * P), None, ALU.mult).then_inc(ln_mean, 1)
                dve.wait_ge(ln_mean, 1)
                for k in range(HEADS):
                    dve.tensor_tensor(zc[:, k, :], zc[:, k, :], mean[:, :], ALU.subtract).then_inc(ln_center, 1)
                dve.wait_ge(ln_center, HEADS)
                dve.wait_ge(ln_mm, 1 + HEADS)
                dve.tensor_scalar(rstd[:, :], ps[:, 5, 0:T], 1.0 / (HEADS * P), EPS, ALU.mult,
                                  ALU.add).then_inc(ln_stat.sem, 1)
                invert_root(rstd[:, :], ln_stat)
                for k in range(HEADS):
                    dve.scalar_tensor_tensor(zc[:, k, :], zc[:, k, :], column("conv_ln_g_2", k), rstd[:, :],
                                             ALU.mult, ALU.mult).then_inc(ln_norm, 1)
                for k in range(HEADS):
                    dve.wait_ge(ln_norm, k + 1)
                    dve.tensor_scalar(zc[:, k, :], zc[:, k, :], column("conv_ln_b_2", k), None,
                                      ALU.add).then_inc(ln_bias, 1)
                dve.wait_ge(ln_sig, 1)
                dve.wait_ge(ln_bias, HEADS)
                dve.tensor_tensor(zc, zc, cb, ALU.mult).then_inc(ln_norm, 1)
                dve.wait_ge(ln_norm, HEADS + 1)
                split_tiles(s_conv)
                dve.wait_ge(gates_sig, 2)

            def before_out_2():
                dve.wait_ge(extra, extra_all("conv_o"))
                split_tiles(s_merged)

            def before_gate_up():
                dve.wait_ge(summed, summed_all("out_2"))
                norm(n_y2)
                residual(r_y2, column("mix_post_g_2", 0, DT))
                norm(n_x4)
                apply(a_x4)

            hooks = {"mod": start, "in_h": before_in_h, "uq": before_uq, "w_o": before_w_o,
                     "up_0": before_up_0, "in_2": before_in_2, "att_o": before_att_o,
                     "out_2": before_out_2, "gate_up": before_gate_up}
            follow_stream(dve, phases, split, evict, hooks)
            dve.wait_ge(summed, summed_all("down_2"))
            norm(n_m2)
            residual(r_m2, column("ffn_post_g_2", 0, DT))


def follow_stream(eng, phases, split, evict, hooks):
    def run(ph, it, first, before):
        for b in range(len(ph.body)):
            ids = chunk_ids(ph, b)
            split(ph, it, b, first, ids[:SLOTS])
            if b:
                evict(ph, it, b - 1, first)
            elif before:
                evict(*before)
            if first and b == 0 and ph.name in hooks:
                hooks[ph.name]()
            split(ph, it, b, first, ids[SLOTS:])

    before = None
    for ph in phases:
        last = len(ph.body) - 1
        run(ph, 0, True, before)
        if ph.iters > 1:
            with eng.Fori(1, ph.iters) as it:
                run(ph, it, False, (ph, it - 1, last, False))
        before = (ph, ph.iters - 1, last, ph.iters == 1)
    evict(*before)


def chunk_ids(ph, b):
    return [j for j, (bb, _, _) in enumerate(ph.chunks) if bb == b]


N_LOADS = 2 + 2 + sum((COLUMN[n] + r - 1) // P - COLUMN[n] // P + 1 for n, r in VECTORS)

INPUTS = ["x", "positions", "w_mod", "w_in", "w_uq", "w_ukv", "w_out", "w_up", "w_down", "w_in_2",
          "rpb_2", "w_attn_o_2", "w_conv_o_2", "w_out_2", "w_gate_up_2", "w_down_2"]


def kernel(**inputs):
    import concourse.bacc as bacc
    from concourse.bass_utils import run_bass_kernel_spmd

    nc = bacc.Bacc("TRN2", target_bir_lowering=False, num_devices=1)
    arrays, d = {}, {}
    for name in INPUTS + [n for n, _ in VECTORS]:
        arrays[f"in_{name}"] = np.ascontiguousarray(inputs[name])
    arrays["in_consts"], arrays["in_masks"] = constants()
    for key, a in arrays.items():
        d[key[3:]] = nc.dram_tensor(key, a.shape, mybir.dt.from_np(a.dtype), kind="ExternalInput").ap()
    out = nc.dram_tensor("out", (1, T, D), F32, kind="ExternalOutput").ap()
    build(nc, d, out)
    r = run_bass_kernel_spmd(nc, [arrays], core_ids=[0])
    return r.results[0]["out"]
```

```python
from contextlib import ExitStack

import numpy as np

import concourse.bass as bass
from concourse import mybir

F32 = mybir.dt.float32
F32R = mybir.dt.float32r
I32 = mybir.dt.int32
U8 = mybir.dt.uint8
ALU = mybir.AluOpType
ACT = mybir.ActivationFunctionType
AX = mybir.AxisListType

P = 128
T = 256
D = 2048
DT = D // P
HEADS = 8
KT = 4
CW = 256
SLOTS = 4
MW = 1024
MOD_SLOTS = 4
EPS = 1e-6
Q_RANK, KV_RANK, ROPE = 512, 256, 64
D_FF, D_FF2 = 8192, 5632
N_MOD = 6
MLA_SCALE = 192 ** -0.5
NA_SCALE = 128 ** -0.5
GRID_W, WIN_C, WIN_R, GRID_ROWS = 64, 16, 8, 4
RPB_H, RPB_W = 2 * WIN_R - 1, 2 * WIN_C - 1
TAPS = 31
PAD = TAPS // 2
LEVELS = [1, 2, 4, 8, 16, 32, 64]
N_STEPS = 2 * len(LEVELS)
EARLY_TAPS = 10
TWO_PI = 2 * np.pi

VECTORS = [("c", 16), ("b_mod", 96), ("pre_mix_g", 16), ("post_mix_g", 16), ("pre_mlp_g", 16),
           ("post_mlp_g", 16), ("q_norm_g", 4), ("kv_norm_g", 2), ("hgrn_norm_g", 1),
           ("hgrn_lb_logits_fwd", 16), ("hgrn_lb_logits_bwd", 16), ("mix_pre_g_2", 16),
           ("mix_post_g_2", 16), ("ffn_pre_g_2", 16), ("ffn_post_g_2", 16), ("b_dw_2", 8),
           ("conv_ln_g_2", 8), ("conv_ln_b_2", 8), ("w_dw_2", 8 * TAPS)]
COLUMN, _at = {}, 0
for _name, _rows in VECTORS:
    COLUMN[_name] = _at
    _at += _rows
N_COLUMNS = _at
V_TILES = -(-N_COLUMNS // P)

C_IDENT, C_FLIP, C_RT, C_WIN, C_FREQ = 0, 128, 256, 320, 384
C_COLS = 385


def constants():
    c = np.zeros((P, C_COLS), np.float32)
    c[:, C_IDENT:C_IDENT + P] = np.eye(P)
    c[:, C_FLIP:C_FLIP + P] = np.kron(np.eye(2), np.eye(GRID_W)[::-1])
    half = ROPE // 2
    for i in range(half):
        c[ROPE + half + i, C_RT + i] = -1.0
        c[ROPE + i, C_RT + half + i] = 1.0
    w = np.arange(GRID_W)
    start = np.clip(w - WIN_C // 2, 0, GRID_W - WIN_C)
    outside = (w[None] < start[:, None]) | (w[None] >= start[:, None] + WIN_C)
    c[:, C_WIN:C_WIN + GRID_W] = np.where(np.tile(outside, (2, 1)), -1e30, 0.0)
    freq = np.float32(10000.0) ** (-np.arange(half, dtype=np.float32) / np.float32(half))
    c[ROPE:, C_FREQ] = np.tile(freq, 2)
    s = np.arange(P)[:, None]
    masks = np.zeros((P, 2, len(LEVELS), P // 2), np.int32)
    for n, m in enumerate(LEVELS):
        blocks = np.arange(P).reshape(-1, 2, m)
        later, earlier = blocks[:, 1].ravel()[None], blocks[:, 0].ravel()[None]
        masks[:, 0, n] = s // m == later // m - 1
        masks[:, 1, n] = s // m == earlier // m + 1
    return c, masks.reshape(P, -1)


EXTRA = {"plain": 0, "relu2": 3, "add": 1, "gated": 1, "gated_add": 2, "gate": 1, "up": 3}


class Linear:

    def __init__(self, w, act, row_tile=0, row_tiles=DT, col0=0, width=CW, tiles=(0, P), out=None,
                 kind="plain", step=CW, tmp=None):
        self.w, self.act, self.row_tile, self.row_tiles = w, act, row_tile, row_tiles
        self.col0, self.width, self.tiles, self.out, self.kind = col0, width, tiles, out, kind
        self.step, self.tmp = step, tmp
        self.chunks = [(k, min(KT, row_tiles - k)) for k in range(0, row_tiles, KT)]


class Side:

    def __init__(self, rows, section, pieces):
        self.rows, self.section, self.pieces, self.width = rows, section, pieces, MW // rows


class Phase:

    def __init__(self, name, iters, body, side=None):
        self.name, self.iters, self.body, self.side = name, iters, body, side
        self.chunks = [(b, k0, kn) for b, (lin, _, _) in enumerate(body) for k0, kn in lin.chunks]
        self.n_chunks = len(self.chunks)
        self.n_panels = len(body)
        self.slot_uses = [sum(j % SLOTS == s for j in range(self.n_chunks)) for s in range(SLOTS)]


def plan_sides(phases):
    pieces = products = 0
    for ph in phases:
        if ph.side:
            ph.side.piece0, ph.side.product0 = pieces, products
            assert ph.side.rows * ph.iters == DT and pieces % MOD_SLOTS == 0
            pieces += ph.side.pieces * ph.iters
            products += ph.side.pieces * ph.side.rows * ph.iters


def plan(phases, uses):
    chunks, uses, panels, extras = 0, list(uses), 0, 0
    last = [None] * SLOTS
    for ph in phases:
        ph.chunk0, ph.use0, ph.panel0, ph.extra0 = chunks, list(uses), panels, extras
        ph.last_before = list(last)
        for s in range(SLOTS):
            uses[s] += ph.slot_uses[s] * ph.iters
        ph.n_extra = sum(EXTRA[lin.kind] for lin, _, _ in ph.body)
        extras += ph.n_extra * ph.iters
        assert ph.iters == 1 or ph.n_panels % 2 == 0
        panels += ph.n_panels * ph.iters
        for j in range(ph.n_chunks):
            last[j % SLOTS] = chunks + (ph.iters - 1) * ph.n_chunks + j
        chunks += ph.n_chunks * ph.iters
    return phases


def build(nc, d, out):
    ctx = ExitStack()
    with ctx:
        at = [-(-nc.sbuf_base // 32) * 32]
        SBUF_END = nc.sbuf_usable_end

        def place(name, shape, dt, offset=None):
            size = int(np.prod(shape[1:])) * {F32: 4, F32R: 4, I32: 4, U8: 1}[dt]
            size = -(-size // 32) * 32
            if offset is None:
                offset = at[0]
                at[0] += size
            assert offset + size <= SBUF_END, (name, offset, size)
            return nc.alloc_sbuf_tensor_at(name, shape, dt, offset=offset)

        def sem(name):
            return ctx.enter_context(nc.semaphore(name))

        w_raw = place("w_raw", [P, SLOTS, KT, CW], F32)
        w_hi = place("w_hi", [P, SLOTS, KT, CW], F32R)
        w_lo = place("w_lo", [P, SLOTS, KT, CW], F32R)
        x_res = place("x_res", [P, DT, T], F32)
        acts_at = at[0]
        acts = place("acts", [P, DT, 2, T], F32R)
        half_sum = place("half_sum", [P, 2, 2, T], F32)
        cols = place("cols", [P, V_TILES * P], F32)
        consts = place("consts", [P, C_COLS], F32)
        masks = place("masks", [P, 2, len(LEVELS), P // 2], U8)
        ones = place("ones", [P, P], F32)
        silu_c = place("silu_c", [P, 2 * DT], F32)
        mods = place("mods", [P, N_MOD * DT], F32)
        gains = place("gains", [P, DT], F32)
        lb = place("lb", [P, 4, HEADS], F32)
        ring = place("ring", [P, 4, T], F32)
        rstd = place("rstd", [P, T], F32)
        small = place("small", [P, 16, 4], F32)
        big = at[0]
        size_tile = T * 4

        ps = ctx.enter_context(nc.psum_tensor("ps", [P, 8, 512], F32))
        ident = consts[:, C_IDENT:C_IDENT + P]

        x_nat = place("x_nat", [P, 2, D], F32, big)
        v_rows = place("v_rows", [P, V_TILES, P], F32, big + 2 * D * 4)
        masks_i = place("masks_i", [P, 2 * len(LEVELS) * P // 2], I32, big + (2 * D + V_TILES * P) * 4)
        y_nat = place("y_nat", [P, 2, D], F32, big)
        w_mod_slots = w_raw[:].rearrange("p s k n -> p s (k n)")
        mod_acc_a = place("mod_acc_a", [P, 4, MW], F32, big + 24 * size_tile)
        mod_w = place("mod_w", [P, MOD_SLOTS, MW], F32, big + 80 * size_tile)
        mod_acc = place("mod_acc", [P, 4, MW], F32, big + 64 * size_tile)
        tmp_up = place("tmp_up", [P, 2, 2, T], F32, big + 76 * size_tile)
        proj = place("proj", [P, 47, T], F32, big)
        h_big = big + 7 * size_tile
        hq, hf, hb, hv, hg = (proj[:, 7 + 8 * i:15 + 8 * i, :] for i in range(5))
        a_diag = place("a_diag", [P, HEADS, 2, P], F32, big + 47 * size_tile)
        a_off = place("a_off", [P, 2, HEADS, P], F32, big + 55 * size_tile)
        kf = place("kf", [P, HEADS, T], F32, big + 63 * size_tile)
        kb = place("kb", [P, HEADS, T], F32, big + 71 * size_tile)
        qb = place("qb", [P, HEADS, T], F32, big + 79 * size_tile)
        hv_tok = place("hv_tok", [P, 2, HEADS, P], F32, big + 87 * size_tile)
        lat = place("lat", [P, 6, 2, T], F32R, h_big)
        q1 = place("q1", [P, HEADS, 2, T], F32, h_big + 12 * size_tile)
        kv1 = place("kv1", [P, HEADS, 2, T], F32, h_big + 28 * size_tile)
        v1_tok = place("v1_tok", [P, 2, HEADS, P], F32, h_big + 44 * size_tile)
        cos_sin = place("cos_sin", [P, 2, T], F32, h_big + 52 * size_tile)
        pos_i = place("pos_i", [P, T], I32, h_big + 54 * size_tile)
        ang = place("ang", [P, 3, T], F32, h_big + 55 * size_tile)
        rot = place("rot", [P, HEADS, T], F32, h_big + 58 * size_tile)
        prob_at = h_big + 66 * size_tile
        prob1 = place("prob1", [P, 2, T], F32, prob_at)
        prob1_t = place("prob1_t", [P, 2, 2, T], F32, prob_at + 2 * size_tile)
        y1 = place("y1", [P, DT, T], F32, big)
        ff_half = D_FF // 2 // P
        ff1 = place("ff1", [P, ff_half, 2, T], F32R, big)
        ym1 = place("ym1", [P, DT, T], F32, big + 2 * ff_half * size_tile)
        tmp1 = place("tmp1", [P, 2, 2, T], F32, big + (2 * ff_half + DT) * size_tile)
        pr2 = place("pr2", [P, 72, T], F32, big)
        q2, k2, v2, ca, cb = (pr2[:, 8 * i:8 * i + 8, :] for i in range(5))
        gate2 = pr2[:, 40:72, :]
        bias = place("bias", [P, 2, HEADS, GRID_ROWS, GRID_W], F32, big + 72 * size_tile)
        v2_tok = place("v2_tok", [P, 2, HEADS, P], F32, big + 88 * size_tile)
        prob2 = place("prob2", [P, 2, T], F32, big + 16 * size_tile)
        prob2_t = place("prob2_t", [P, 2, 2, T], F32, big + 18 * size_tile)
        z, zc = cb, ca
        mean = place("mean", [P, T], F32, big + 22 * size_tile)
        y2 = place("y2", [P, DT, T], F32, big + 16 * size_tile)
        tmp2 = place("tmp2", [P, 2, 2, T], F32, big + 36 * size_tile)
        ff2 = place("ff2", [P, D_FF2 // P, 2, T], F32R, big)
        tmp3 = place("tmp3", [P, 2, 2, T], F32, big + 2 * (D_FF2 // P) * size_tile)
        gate3 = place("gate3", [P, 2, T], F32, big + (2 * (D_FF2 // P) + 4) * size_tile)
        ym2 = place("ym2", [P, DT, T], F32, acts_at)

        w_mod, w_in = d["w_mod"][0], d["w_in"][0]
        ug = D_FF2
        panels = D // CW

        def lin(*a, **k):
            return Linear(*a, **k)

        in_h = lin(w_in, acts, col0=832, out=proj[:, 7:47, :])
        in_m = lin(w_in, acts, out=proj[:, 0:6, :])
        in_r = lin(w_in, acts, col0=704, width=P, tiles=(0,), out=proj[:, 6:7, :])
        uq = lin(d["w_uq"][0], lat, row_tiles=4, width=192, step=192, tiles=(0, ROPE),
                 out=q1[:].rearrange("p h two t -> p (h two) t"))
        ukv = lin(d["w_ukv"][0], lat[:, 4:6], row_tiles=2,
                  out=kv1[:].rearrange("p h two t -> p (h two) t"))
        w_o = lin(d["w_out"][0], acts, out=y1)
        up = [lin(d["w_up"][0], acts, col0=h * D_FF // 2, out=ff1, kind="relu2", tmp=tmp1 if h else tmp_up)
              for h in range(2)]
        down = [lin(d["w_down"][0], ff1, row_tile=h * ff_half, row_tiles=ff_half, out=ym1,
                    kind="add" if h else "plain", tmp=tmp1) for h in range(2)]
        in_2 = lin(d["w_in_2"][0], acts, out=pr2)
        att_o = lin(d["w_attn_o_2"][0], acts, row_tiles=8, out=gate2[:, 0:16, :], kind="gated", tmp=tmp2)
        conv_o = lin(d["w_conv_o_2"][0], acts[:, 8:16], row_tiles=8, out=gate2[:, 0:16, :],
                     kind="gated_add", tmp=tmp2)
        out_2 = lin(d["w_out_2"][0], acts, out=y2)
        gate_l = lin(d["w_gate_up_2"][0], acts, out=None, kind="gate", tmp=tmp3)
        up_l = lin(d["w_gate_up_2"][0], acts, col0=ug, out=ff2, kind="up", tmp=tmp3)
        down2 = lin(d["w_down_2"][0], ff2, row_tiles=D_FF2 // P, out=ym2)

        phases = plan([
            Phase("in_h", 8, [(in_h, 0, 2), (in_h, 1, 2)], Side(2, 2, 8)),
            Phase("in_m", 1, [(in_h, 16, 0), (in_h, 17, 0), (in_h, 18, 0), (in_h, 19, 0),
                              (in_m, 0, 0), (in_m, 1, 0), (in_m, 2, 0), (in_r, 0, 0)]),
            Phase("uq", 2, [(uq, i, 4) for i in range(4)]),
            Phase("ukv", 2, [(ukv, i, 4) for i in range(4)]),
            Phase("w_o", panels // 2, [(w_o, 0, 2), (w_o, 1, 2)], Side(4, 4, 8)),
            Phase("up_0", 8, [(up[0], 0, 2), (up[0], 1, 2)], Side(2, 5, 4)),
            Phase("down_0", panels // 2, [(down[0], 0, 2), (down[0], 1, 2)]),
            Phase("up_1", 8, [(up[1], 0, 2), (up[1], 1, 2)]),
            Phase("down_1", panels // 2, [(down[1], 0, 2), (down[1], 1, 2)]),
            Phase("in_c", 4, [(in_2, 12, 2), (in_2, 13, 2)]),
            Phase("in_qk", 4, [(in_2, 0, 2), (in_2, 1, 2)]),
            Phase("in_v", 2, [(in_2, 8, 2), (in_2, 9, 2)]),
            Phase("in_g", 8, [(in_2, 20, 2), (in_2, 21, 2)]),
            Phase("att_o", panels // 2, [(att_o, 0, 2), (att_o, 1, 2)]),
            Phase("conv_o", panels // 2, [(conv_o, 0, 2), (conv_o, 1, 2)]),
            Phase("out_2", panels // 2, [(out_2, 0, 2), (out_2, 1, 2)]),
            Phase("gate_up", D_FF2 // CW, [(gate_l, 0, 1), (up_l, 0, 1)]),
            Phase("down_2", panels // 2, [(down2, 0, 2), (down2, 1, 2)]),
        ], uses=[DT] * SLOTS)
        plan_sides(phases)
        by_name = {ph.name: ph for ph in phases}

        def panels_before(name):
            return by_name[name].panel0

        def panels_through(name):
            ph = by_name[name]
            return ph.panel0 + ph.n_panels * ph.iters

        landed = [sem(f"landed{s}") for s in range(SLOTS)]
        hi_ready = sem("hi_ready")
        lo_ready = sem("lo_ready")
        chunk_used = sem("chunk_used")
        half_ready = sem("half_ready")
        summed = sem("summed")
        mod_products = sem("mod_products")
        mod_landed = [sem(f"mod_landed{s}") for s in range(MOD_SLOTS)]
        side_products = sem("side_products")
        mod_mm = sem("mod_mm")
        mods_done = sem("mods_done")
        extra = sem("extra")
        sigmoid_ready = sem("sigmoid_ready")

        def chunk_seq(ph, it, j):
            return ph.chunk0 + it * ph.n_chunks + j

        def freed(ph, it, j, first):
            if j >= SLOTS:
                return chunk_seq(ph, it, j - SLOTS) + 1
            if first:
                before = ph.last_before[j % SLOTS]
                return None if before is None else before + 1
            return chunk_seq(ph, it - 1, max(i for i in range(ph.n_chunks) if i % SLOTS == j % SLOTS)) + 1

        def panel_seq(ph, it, b):
            return ph.panel0 + it * ph.n_panels + b

        def piece_seq(ph, it, i):
            return ph.side.piece0 + it * ph.side.pieces + i

        def side_all(name):
            s = by_name[name].side
            return s.product0 + s.rows * s.pieces * by_name[name].iters

        def pieces_at(ph, j):
            every = ph.n_chunks // ph.side.pieces if ph.side else 1
            return [j // every] if ph.side and j % every == every - 1 else []

        def extra_seq(ph, it, b):
            return ph.extra0 + it * ph.n_extra + sum(EXTRA[x.kind] for x, _, _ in ph.body[:b])

        def bank_pair(ph, b):
            return (ph.panel0 + b) % 2

        def summed_all(name):
            ph = by_name[name]
            return ph.panel0 + ph.n_panels * ph.iters

        def extra_all(name):
            ph = by_name[name]
            return ph.extra0 + ph.n_extra * ph.iters

        def column(name, i=0, n=1):
            return cols[:, COLUMN[name] + i:COLUMN[name] + i + n]

        class Count:

            def __init__(self, sem_, base=0):
                self.sem, self.base = sem_, base

            def __call__(self, n):
                return self.sem, self.base + n

        UNITS = 2 * HEADS
        shared = {}

        def count(name, steps):
            if name not in shared:
                shared[name] = [sem(name), 0]
            c = Count(*shared[name])
            shared[name][1] += steps
            return c

        class Norm:

            def __init__(self, src, tiles, dim):
                self.src, self.tiles, self.dim = src, tiles, dim
                self.squared = count("norm_squared", tiles)
                self.added = count("norm_added", tiles)
                self.stat = count("norm_stat", 3)

        class Apply:

            def __init__(self, src, tiles, gain, dst, shift=None):
                self.src, self.tiles, self.gain, self.dst, self.shift = src, tiles, gain, dst, shift
                self.scaled = count("apply_scaled", tiles)
                self.hi = count("apply_hi", tiles)
                self.lo = count("apply_lo", tiles)

        class Residual:

            def __init__(self, src):
                self.src = src
                self.scaled = count("residual_scaled", DT)
                self.added = count("residual_added", 4)

        class Split:

            def __init__(self, src, tiles, dst):
                self.src, self.tiles, self.dst = src, tiles, dst
                self.hi = count("split_hi", tiles // 2)
                self.lo = count("split_lo", tiles // 2)

        class Attention:

            def __init__(self, v, v_tok, prob, prob_t, scale, bias=None):
                self.v, self.v_tok, self.prob, self.prob_t = v, v_tok, prob, prob_t
                self.scale, self.bias = scale, bias
                self.v_turned = count("att_v_turned", UNITS)
                self.v_moved = count("att_v_moved", 4)
                self.scores = count("att_scores", UNITS)
                self.biased = count("att_biased", UNITS if bias is not None else 0)
                self.maxed = count("att_maxed", 2 * UNITS)
                self.exped = count("att_exped", UNITS)
                self.inverted = count("att_inverted", UNITS)
                self.normed = count("att_normed", UNITS)
                self.turned = count("att_turned", UNITS)
                self.moved = count("att_moved", UNITS)
                self.out = count("att_out", HEADS)
                self.hi = count("att_hi", HEADS)
                self.lo = count("att_lo", HEADS)

        n_x1 = Norm(x_res, DT, D)
        a_x1 = Apply(x_res, DT, gains, acts, (mods, 0))
        n_q = Norm(proj, 4, Q_RANK)
        n_kv = Norm(proj[:, 4:6, :], 2, KV_RANK)
        a_q = Apply(proj, 4, column("q_norm_g", 0, 4), lat)
        a_kv = Apply(proj[:, 4:6, :], 2, column("kv_norm_g", 0, 2), lat[:, 4:6])
        att1 = Attention(kv1[:, :, 1, :], v1_tok, prob1, prob1_t, MLA_SCALE)
        n_y1 = Norm(y1, DT, D)
        r_y1 = Residual(y1)
        n_x2 = Norm(x_res, DT, D)
        a_x2 = Apply(x_res, DT, gains, acts, (mods, 3 * DT))
        n_m1 = Norm(ym1, DT, D)
        r_m1 = Residual(ym1)
        n_x3 = Norm(x_res, DT, D)
        a_x3 = Apply(x_res, DT, column("mix_pre_g_2", 0, DT), acts)
        att2 = Attention(v2, v2_tok, prob2, prob2_t, NA_SCALE, bias)
        s_conv = Split(zc, HEADS, acts[:, HEADS:2 * HEADS])
        s_merged = Split(gate2, DT, acts)
        n_y2 = Norm(y2, DT, D)
        r_y2 = Residual(y2)
        n_x4 = Norm(x_res, DT, D)
        a_x4 = Apply(x_res, DT, column("ffn_pre_g_2", 0, DT), acts)
        n_m2 = Norm(ym2, DT, D)
        r_m2 = Residual(ym2)

        dve_chain, act_chain = sem("dve_chain"), sem("act_chain")
        loads = sem("loads")
        const_set, cols_turned, cols_moved, x_turned, x_moved = map(
            sem, ("const_set", "cols_turned", "cols_moved", "x_turned", "x_moved"))
        late_loads = sem("late_loads")
        c_sig, c_silu = map(sem, ("c_sig", "c_silu"))
        lb_diff, lb_sig, f_sig, f_done, k_done, ksum_done, q_done = map(
            sem, ("lb_diff", "lb_sig", "f_sig", "f_done", "k_done", "ksum_done", "q_done"))
        diag_mm, diag_moved = map(sem, ("diag_mm", "diag_moved"))
        ho_stat, ln_stat = Count(sem("ho_stat")), Count(sem("ln_stat"))
        hv_turned, hv_moved = Count(sem("hv_turned")), Count(sem("hv_moved"))
        level_mm, level_selected, level_updated, off_mm, off_moved = map(
            sem, ("level_mm", "level_selected", "level_updated", "off_mm", "off_moved"))
        ho_mm, ho_moved, ho_sq, ho_sum, hg_sig, h_out, h_hi, h_lo = map(
            sem, ("ho_mm", "ho_moved", "ho_sq", "ho_sum", "hg_sig", "h_out", "h_hi", "h_lo"))
        pos_landed, angles, sines, rot_mm, rot_done = map(
            sem, ("pos_landed", "angles", "sines", "rot_mm", "rot_done"))
        bias_landed, bias_mm, bias_done, cb_sig, z_done, conv_step = map(
            sem, ("bias_landed", "bias_mm", "bias_done", "cb_sig", "z_done", "conv_step"))
        ln_mm, ln_mean, ln_center, ln_sq, ln_norm, ln_bias, ln_sig, gates_sig = map(
            sem, ("ln_mm", "ln_mean", "ln_center", "ln_sq", "ln_norm", "ln_bias", "ln_sig",
                  "gates_sig"))
        out_turned, out_moved, out_stored = map(sem, ("out_turned", "out_moved", "out_stored"))

        bias_rows = bias[:].rearrange("p s h i c -> p (s h i c)").rearrange("p (n w) -> p n w", w=512)

        block = ctx.enter_context(nc.Block())

        @block.sync
        def _(sp):
            sp.dma_start(consts[:, :], d["consts"]).then_inc(loads, 16)
            for dst, src in vector_loads(d, v_rows, early=True):
                sp.dma_start(dst, src).then_inc(loads, 16)
            for half in range(2):
                sp.dma_start(x_nat[:, half, :], d["x"][0, half * P:(half + 1) * P, :]).then_inc(loads, 16)

            def mod_piece(k, s):
                sp.dma_start(w_mod_slots[:, s, :], w_mod[bass.ds(k * P, P), s * MW:(s + 1) * MW]
                             ).then_inc(landed[s], 16)

            for s in range(SLOTS):
                mod_piece(0, s)
            with sp.Fori(1, DT) as k:
                for s in range(SLOTS):
                    sp.wait_ge(mod_products, (k - 1) * SLOTS + (s + 1))
                    mod_piece(k, s)

            def chunk(ph, it, j, first):
                b, k0, kn = ph.chunks[j]
                lin_, p0, stride = ph.body[b]
                free = freed(ph, it, j, first)
                if free is not None:
                    sp.wait_ge(lo_ready, free)
                else:
                    sp.wait_ge(mod_products, SLOTS * (DT - 1) + j + 1)
                row = (lin_.row_tile + k0) * P
                panel = p0 + it * stride
                src = lin_.w[row:row + kn * P, bass.ds(panel * lin_.step + lin_.col0, lin_.width)]
                slot = j % SLOTS
                sp.dma_start(w_raw[:, slot, 0:kn, 0:lin_.width],
                             src.rearrange("(k p) n -> p k n", p=P)).then_inc(landed[slot], 16)

            def side(ph, it, i, first):
                s = ph.side
                n = piece_seq(ph, it, i)
                if not (first and n < MOD_SLOTS):
                    before = s.product0 + (it * s.pieces + (i + 1 - MOD_SLOTS)) * s.rows
                    if first and i < MOD_SLOTS:
                        before = s.product0
                    sp.wait_ge(side_products, before)
                col = s.section * D + i * s.width
                src = w_mod[bass.ds(it * (s.rows * P), s.rows * P), col:col + s.width]
                sp.dma_start(mod_w[:, i % MOD_SLOTS, :].rearrange("p (k n) -> p k n", k=s.rows),
                             src.rearrange("(k p) n -> p k n", p=P)).then_inc(mod_landed[i % MOD_SLOTS], 16)

            for ph in phases:
                if ph.name == "w_o":
                    sp.wait_ge(h_lo, 1)
                for j in range(ph.n_chunks):
                    chunk(ph, 0, j, True)
                    for i in pieces_at(ph, j):
                        side(ph, 0, i, True)
                if ph.iters > 1:
                    with sp.Fori(1, ph.iters) as it:
                        for j in range(ph.n_chunks):
                            chunk(ph, it, j, False)
                            for i in pieces_at(ph, j):
                                side(ph, it, i, False)
            for half in range(2):
                sp.wait_ge(out_moved, 4 * (half + 1))
                sp.dma_start(out[0, half * P:(half + 1) * P, :], y_nat[:, half, :]).then_inc(out_stored, 16)
            sp.wait_ge(out_stored, 32)

        @block.gpsimd
        def _(pool):
            pool.dma_start(masks_i[:, :], d["masks"]).then_inc(late_loads, 16)
            for dst, src in vector_loads(d, v_rows, early=False):
                pool.dma_start(dst, src).then_inc(late_loads, 16)

            pool.wait_ge(h_lo, 1)
            pool.dma_start(pos_i[ROPE:P, :],
                           d["positions"][0:1, :].to_broadcast([ROPE, T])).then_inc(pos_landed, 16)
            pool.wait_ge(*r_m1.added(4))
            for r in range(GRID_ROWS):
                for i in range(GRID_ROWS):
                    src = bass.AP(d["rpb_2"].tensor,
                                  (i - r + WIN_R - 1) * RPB_W + WIN_C - 1 - (GRID_W - 1),
                                  [[1, GRID_W], [RPB_H * RPB_W, HEADS], [1, GRID_W]])
                    rows = slice((r % 2) * GRID_W, (r % 2 + 1) * GRID_W)
                    pool.dma_start(bias[rows, r // 2, :, i, :], src).then_inc(bias_landed, 16)

        @block.tensor
        def _(pe):
            def panel(ph, it, b, first):
                lin_ = ph.body[b][0]
                seq, pair = panel_seq(ph, it, b), bank_pair(ph, b)
                if not (first and ph.panel0 + b < 2):
                    pe.wait_ge(summed, seq - 1)
                ids = chunk_ids(ph, b)
                for j in ids:
                    _, k0, kn = ph.chunks[j]
                    slot = j % SLOTS
                    pe.wait_ge(lo_ready, chunk_seq(ph, it, j) + 1)
                    if first and b == 0 and ph.name in ready:
                        pe.wait_ge(*ready[ph.name](k0 + kn))
                    for k in range(kn):
                        kk = k0 + k
                        at_first, at_last = j == ids[0] and k == 0, j == ids[-1] and k == kn - 1
                        for n, c in enumerate(lin_.tiles):
                            hi = w_hi[:, slot, k, c:c + P]
                            lo = w_lo[:, slot, k, c:c + P]
                            bank = 2 * pair + n
                            pe.matmul(ps[:, bank, :], hi, lin_.act[:, kk, :, :], start=at_first,
                                      stop=False, skip_group_check=True)
                            mm = pe.matmul(ps[:, bank, 0:T], lo, lin_.act[:, kk, 0, :], start=False,
                                           stop=at_last, skip_group_check=True)
                    mm.then_inc(chunk_used, 1)
                    if ph.name == "in_m" and j % 2 == 1 and j < 2 * N_STEPS - 1:
                        level_step((j + 1) // 2)

            def relu_tiles(name):
                return lambda k: (extra, by_name[name].extra0 + 3 * (k // 2))

            ready = {
                "in_h": a_x1.lo, "up_0": a_x2.lo, "in_c": a_x3.lo, "gate_up": a_x4.lo,
                "w_o": lambda k: att1.lo(min(k, HEADS)), "att_o": att2.lo,
                "conv_o": lambda k: s_conv.lo(k // 2), "out_2": lambda k: s_merged.lo(k // 2),
                "down_0": relu_tiles("up_0"), "down_1": relu_tiles("up_1"),
                "down_2": lambda k: (extra, by_name["gate_up"].extra0 + 4 * (k // 2)),
            }

            def norm(n):
                for k in range(n.tiles):
                    pe.wait_ge(*n.squared(k + 1))
                    pe.matmul(ps[:, 5, 0:T], ones[:, :], ring[:, k % 4, :], start=k == 0,
                              stop=k == n.tiles - 1).then_inc(n.added.sem, 1)

            def turn_values(tiles, done, wait=None):
                for i in range(2 * HEADS):
                    half, h = divmod(i, HEADS)
                    pe.transpose(ps[:, 4 + i // 4, (i % 4) * P:(i % 4 + 1) * P],
                                 tiles[:, h, half * P:(half + 1) * P], ident).then_inc(done.sem, 1)

            def attention(a, scores):
                def pv(h):
                    pe.wait_ge(*a.moved(2 * h + 2))
                    if h >= 1:
                        pe.wait_ge(*a.lo(h))
                    for s in range(2):
                        mm = pe.matmul(ps[:, 7, 0:T], a.v_tok[:, s, h, :], a.prob_t[:, h % 2, s, :],
                                       start=s == 0, stop=s == 1)
                    mm.then_inc(a.out.sem, 1)

                for u in range(UNITS + 3):
                    if u < UNITS:
                        if u >= 2:
                            pe.wait_ge(*a.exped(u - 1))
                        scores(u // 2, u % 2, ps[:, 4 + u % 2, 0:T]).then_inc(a.scores.sem, 1)
                    if 1 <= u <= UNITS:
                        v = u - 1
                        pe.wait_ge(*a.normed(v + 1))
                        if v >= 1:
                            pe.wait_ge(*a.moved(v))
                        for s in range(2):
                            mm = pe.transpose(ps[:, 6, s * P:(s + 1) * P],
                                              a.prob[:, v % 2, s * P:(s + 1) * P], ident)
                        mm.then_inc(a.turned.sem, 1)
                    if u >= 3 and u % 2 == 1:
                        pv((u - 3) // 2)

            def turn_vectors(tiles):
                for t in tiles:
                    rows = min(P, N_COLUMNS - t * P)
                    pe.transpose(ps[:, 4 + t // 4, (t % 4) * P:(t % 4) * P + rows], v_rows[0:rows, t, :],
                                 consts[0:rows, C_IDENT:C_IDENT + rows]).then_inc(cols_turned, 1)

            def sum_mods(acc, groups):
                for g in range(groups):
                    for i in range(8):
                        mm = pe.matmul(ps[:, 4, 8 * g + i:8 * g + i + 1], acc[:, g, i * P:(i + 1) * P],
                                       ones[:, 0:1], start=True, stop=True)
                    mm.then_inc(mod_mm, 1)

            def start():
                pe.wait_ge(loads, 16 * N_EARLY)
                turn_vectors([0])
                for g in range(8):
                    half, b4 = divmod(g, 4)
                    if g >= 4:
                        pe.wait_ge(x_moved, g - 3)
                    for i in range(4):
                        mm = pe.transpose(ps[:, b4, i * P:(i + 1) * P],
                                          x_nat[:, half, (4 * b4 + i) * P:(4 * b4 + i + 1) * P], ident)
                    mm.then_inc(x_turned, 1)
                pe.wait_ge(cols_moved, 1)
                pe.wait_ge(late_loads, 16 * N_LATE)
                turn_vectors(range(1, V_TILES))
                pe.wait_ge(cols_moved, V_TILES)
                pe.wait_ge(const_set, 1)
                norm(n_x1)
                pe.wait_ge(mod_products, 4 * DT)
                sum_mods(mod_acc_a, 4)

            def hgrn_start():
                turn_values(hv, hv_turned)
                pe.wait_ge(*hv_moved(4))
                pe.wait_ge(ksum_done, 1)
                for h in range(HEADS):
                    for half in range(2):
                        i = 2 * h + half
                        cut = slice(half * P, (half + 1) * P)
                        pe.matmul(ps[:, 4 + i // 4, (i % 4) * P:(i % 4 + 1) * P], qb[:, h, cut],
                                  hq[:, h, cut], start=True, stop=True).then_inc(diag_mm, 1)
                pe.wait_ge(diag_moved, 4)
                pe.wait_ge(q_done, 2)

            def level_step(step):
                n, way = divmod(step, 2)
                m = LEVELS[n]
                if n:
                    pe.wait_ge(level_updated, 6 * (n - 1) + 3 * (way + 1))
                kk, qq = ((kf, hq), (kb, qb))[way]
                for i in range(2 * HEADS):
                    h, half = divmod(i, 2)
                    q_ = qq[:, h, half * P:(half + 1) * P].rearrange("p (b two m) -> p b two m", two=2, m=m)
                    o = ps[:, 4 + 2 * way + i // 8, (i % 8) * 64:(i % 8 + 1) * 64]
                    mm = pe.matmul(o, kk[:, h, half * P:(half + 1) * P], q_[:, :, 1 - way, :],
                                   start=True, stop=True)
                mm.then_inc(level_mm, 1)

            def hgrn_end():
                pe.wait_ge(level_updated, 6 * len(LEVELS))
                for way in range(2):
                    kk, qq = ((kf, hq), (kb, qb))[way]
                    for h in range(HEADS):
                        s, t = (0, P) if way == 0 else (P, 0)
                        mm = pe.matmul(ps[:, 4 + 2 * way + h // 4, (h % 4) * P:(h % 4 + 1) * P],
                                       kk[:, h, s:s + P], qq[:, h, t:t + P], start=True, stop=True)
                    mm.then_inc(off_mm, 1)
                pe.wait_ge(off_moved, 4)
                for h in range(HEADS):
                    for t in range(2):
                        o = ps[:, 4 + h // 2, (h % 2) * T + t * P:(h % 2) * T + (t + 1) * P]
                        pe.matmul(o, hv_tok[:, t, h, :], a_diag[:, h, t, :], start=True, stop=False)
                        mm = pe.matmul(o, hv_tok[:, 1 - t, h, :], a_off[:, 1 - t, h, :], start=False, stop=True)
                    mm.then_inc(ho_mm, 1)
                pe.wait_ge(ho_sq, 1)
                for h in range(HEADS):
                    pe.matmul(ps[:, 4 + h // 2, (h % 2) * T:(h % 2 + 1) * T], ones[:, :], kf[:, h, :],
                              start=True, stop=True).then_inc(ho_sum, 1)

            def before_in_m():
                pe.wait_ge(summed, summed_all("in_h"))
                pe.wait_ge(side_products, side_all("in_h"))
                sum_mods(mod_acc, 4)
                pe.wait_ge(mods_done, 8)
                hgrn_start()
                level_step(0)

            def before_uq():
                pe.wait_ge(summed, summed_all("in_m"))
                hgrn_end()
                pe.wait_ge(*ho_stat(1))
                norm(n_q)
                pe.wait_ge(*n_q.stat(1))
                norm(n_kv)
                pe.wait_ge(*a_q.lo(4))
                pe.wait_ge(*a_kv.lo(2))

            def before_w_o():
                pe.wait_ge(summed, summed_all("ukv"))
                for first_, tiles, n in ((0, proj[ROPE:P, 6:7, :], 1), (1, q1, 4)):
                    for i in range(n):
                        rhs = proj[ROPE:P, 6, :] if n == 1 else q1[ROPE:P, 2 * i:2 * i + 2, 1, :]
                        width = T if n == 1 else 2 * T
                        if n == 4 and i == 0:
                            pe.wait_ge(rot_done, 3)
                        pe.matmul(ps[ROPE:P, 4 + i, 0:width], consts[ROPE:P, C_RT:C_RT + ROPE], rhs,
                                  start=True, stop=True).then_inc(rot_mm, 1)
                pe.wait_ge(rot_done, 6)
                turn_values(att1.v, att1.v_turned)

                def scores(h, half, o):
                    q_ = slice(half * P, (half + 1) * P)
                    pe.matmul(o, q1[:, h, 0, q_], kv1[:, h, 0, :], start=True, stop=False)
                    return pe.matmul(o, q1[ROPE:P, h, 1, q_], proj[ROPE:P, 6, :], start=False, stop=True)

                pe.wait_ge(*att1.v_moved(4))
                attention(att1, scores)
                pe.wait_ge(h_lo, 1)

            def before_up_0():
                pe.wait_ge(side_products, side_all("w_o"))
                sum_mods(mod_acc, 2)
                pe.wait_ge(summed, summed_all("w_o"))
                norm(n_y1)
                norm(n_x2)

            def before_down_0():
                pe.wait_ge(side_products, side_all("up_0"))
                sum_mods(mod_acc, 2)

            def before_in_c():
                pe.wait_ge(extra, extra_all("down_1"))
                norm(n_m1)
                norm(n_x3)

            def before_att_o():
                pe.wait_ge(summed, summed_all("in_g"))
                turn_values(att2.v, att2.v_turned)

                def scores(h, half, o):
                    return pe.matmul(o, q2[:, h, half * P:(half + 1) * P], k2[:, h, :], start=True, stop=True)

                pe.wait_ge(*att2.v_moved(4))
                pe.wait_ge(bias_landed, 16 * GRID_ROWS ** 2)
                for i in range(8):
                    if i >= 4:
                        pe.wait_ge(bias_done, i - 3)
                    pe.matmul(ps[:, 4 + i % 4, :], consts[:, C_FLIP:C_FLIP + P], bias_rows[:, i, :],
                              start=True, stop=True).then_inc(bias_mm, 1)
                pe.wait_ge(bias_done, 8)
                attention(att2, scores)
                pe.wait_ge(*att2.lo(HEADS))
                pe.wait_ge(conv_step, TAPS * HEADS)
                for k in range(HEADS):
                    mm = pe.matmul(ps[:, 4, 0:T], ones[:, :], zc[:, k, :], start=k == 0, stop=k == HEADS - 1)
                mm.then_inc(ln_mm, 1)
                for k in range(HEADS):
                    pe.wait_ge(ln_sq, k + 1)
                    mm = pe.matmul(ps[:, 5, 0:T], ones[:, :], ring[:, k % 4, :], start=k == 0,
                                   stop=k == HEADS - 1).then_inc(ln_mm, 1)
                pe.wait_ge(*s_conv.lo(4))

            def before_gate_up():
                pe.wait_ge(summed, summed_all("out_2"))
                norm(n_y2)
                norm(n_x4)

            hooks = {
                "uq": before_uq, "w_o": before_w_o, "up_0": before_up_0, "down_0": before_down_0,
                "in_c": before_in_c, "in_m": before_in_m,
                "att_o": before_att_o, "gate_up": before_gate_up,
            }
            start()
            for ph in phases:
                hooks.get(ph.name, lambda: None)()
                for b in range(len(ph.body)):
                    panel(ph, 0, b, True)
                if ph.iters > 1:
                    with pe.Fori(1, ph.iters) as it:
                        for b in range(len(ph.body)):
                            panel(ph, it, b, False)
            pe.wait_ge(summed, summed_all("down_2"))
            norm(n_m2)
            pe.wait_ge(*r_m2.added(4))
            for g in range(8):
                half, b4 = divmod(g, 4)
                if g >= 4:
                    pe.wait_ge(out_moved, g - 3)
                for i in range(4):
                    mm = pe.transpose(ps[:, b4, i * P:(i + 1) * P],
                                      x_res[:, 4 * b4 + i, half * P:(half + 1) * P], ident)
                mm.then_inc(out_turned, 1)

        @block.scalar
        def _(act):
            def split(ph, it, b, first, ids):
                lin_ = ph.body[b][0]
                for j in ids:
                    kn, slot = ph.chunks[j][2], j % SLOTS
                    uses = ph.use0[slot] + it * ph.slot_uses[slot] + j // SLOTS + 1
                    act.wait_ge(landed[slot], uses * 16)
                    free = freed(ph, it, j, first)
                    if free is not None:
                        act.wait_ge(chunk_used, free)
                    act.copy(w_hi[:, slot, 0:kn, 0:lin_.width],
                             w_raw[:, slot, 0:kn, 0:lin_.width]).then_inc(hi_ready, 1)

            def evict(ph, it, b, first):
                lin_ = ph.body[b][0]
                seq = panel_seq(ph, it, b)
                act.wait_ge(chunk_used, chunk_seq(ph, it, chunk_ids(ph, b)[-1]) + 1)
                pair, n = bank_pair(ph, b), len(lin_.tiles)
                if not (first and ph.panel0 + b < 2):
                    act.wait_ge(summed, seq - 1)
                act.copy(half_sum[:, pair, 0:n, :], ps[:, 2 * pair:2 * pair + n, T:2 * T]).then_inc(half_ready, 1)
                if lin_.kind == "gate":
                    act.wait_ge(summed, seq + 1)
                    if not first:
                        act.wait_ge(extra, extra_seq(ph, it, b))
                    act.activation(gate3[:, :, :], lin_.tmp[:, pair, :, :], ACT.Sigmoid).then_inc(sigmoid_ready, 1)

            def root(ap, stat):
                act.wait_ge(*stat(1))
                act.activation(ap, ap, ACT.Sqrt).then_inc(stat.sem, 1)

            def norm(n, residual=None):
                for k in range(n.tiles):
                    if residual and k % 4 == 0:
                        act.wait_ge(*residual.added(k // 4 + 1))
                    if k >= 4:
                        act.wait_ge(*n.added(k - 3))
                    act.activation(ring[:, k % 4, :], n.src[:, k, :], ACT.Square).then_inc(n.squared.sem, 1)
                root(rstd[:, :], n.stat)

            def apply(a):
                for k in range(a.tiles):
                    act.wait_ge(*a.scaled(k + 1))
                    if a.shift is None:
                        act.copy(a.dst[:, k, 0, :], ring[:, k % 4, :]).then_inc(a.hi.sem, 1)
                    else:
                        tile, c0 = a.shift
                        act.activation(a.dst[:, k, 0, :], ring[:, k % 4, :], ACT.Identity,
                                       bias=tile[:, c0 + k:c0 + k + 1]).then_inc(a.hi.sem, 1)

            def split_tiles(s):
                for k in range(0, s.tiles, 2):
                    act.copy(s.dst[:, k:k + 2, 0, :], s.src[:, k:k + 2, :]).then_inc(s.hi.sem, 1)

            def move_values(tok, turned, moved):
                flat = tok.rearrange("p s h d -> p (s h d)")
                for i in range(4):
                    act.wait_ge(*turned(4 * i + 4))
                    act.copy(flat[:, i * 512:(i + 1) * 512], ps[:, 4 + i, :]).then_inc(moved.sem, 1)

            def attention(a):
                move_values(a.v_tok[:], a.v_turned, a.v_moved)
                for u in range(UNITS + 5):
                    if u < UNITS:
                        act.wait_ge(*a.maxed(2 * u + 2))
                        if u >= 2:
                            act.wait_ge(*a.turned(u - 1))
                        src = ps[:, 4 + u % 2, 0:T] if a.bias is None else a.prob[:, u % 2, :]
                        act.activation(a.prob[:, u % 2, :], src, ACT.Exp, bias=small[:, u, 1:2],
                                       scale=a.scale if a.bias is None else 1.0,
                                       accum_out=small[:, u, 2:3]).then_inc(a.exped.sem, 1)
                    if 2 <= u < UNITS + 2:
                        v = u - 2
                        h, half = divmod(v, 2)
                        act.wait_ge(*a.turned(v + 1))
                        if h >= 2:
                            act.wait_ge(*a.out(h - 1))
                        act.copy(a.prob_t[:, h % 2, :, half * P:(half + 1) * P],
                                 ps[:, 6, 0:T].rearrange("p (s q) -> p s q", s=2)).then_inc(a.moved.sem, 1)
                    if u >= 4 and u % 2 == 0 and (u - 4) // 2 < HEADS:
                        h = (u - 4) // 2
                        act.wait_ge(*a.out(h + 1))
                        act.copy(acts[:, h, 0, :], ps[:, 7, 0:T]).then_inc(a.hi.sem, 1)

            def move_vectors(tiles):
                for t in tiles:
                    rows = min(P, N_COLUMNS - t * P)
                    act.wait_ge(cols_turned, tiles[-1] + 1)
                    act.copy(cols[:, t * P:t * P + rows],
                             ps[:, 4 + t // 4, (t % 4) * P:(t % 4) * P + rows]).then_inc(cols_moved, 1)

            def start():
                move_vectors([0])
                act.wait_ge(cols_moved, 1)
                act.activation(silu_c[:, 0:DT], column("c", 0, DT), ACT.Sigmoid).then_inc(c_sig, 1)
                for g in range(8):
                    half, b4 = divmod(g, 4)
                    act.wait_ge(x_turned, g + 1)
                    act.copy(x_res[:, 4 * b4:4 * b4 + 4, half * P:(half + 1) * P],
                             ps[:, b4, :].rearrange("p (i t) -> p i t", i=4)).then_inc(x_moved, 1)
                move_vectors(range(1, V_TILES))
                act.wait_ge(x_moved, 8)
                norm(n_x1)
                act.wait_ge(mods_done, 4)
                apply(a_x1)

            def hgrn_start():
                act.wait_ge(lb_diff, 2)
                act.activation(lb[:, 0, :], lb[:, 0, :], ACT.Sigmoid).then_inc(lb_sig, 1)
                act.activation(lb[:, 2, :], lb[:, 2, :], ACT.Sigmoid).then_inc(lb_sig, 1)
                act.activation(hf[:, :, :], hf[:, :, :], ACT.Sigmoid).then_inc(f_sig, 1)
                act.activation(hb[:, :, :], hb[:, :, :], ACT.Sigmoid).then_inc(f_sig, 1)
                move_values(hv_tok[:], hv_turned, hv_moved)
                flat = a_diag[:].rearrange("p h s t -> p (h s t)")
                for i in range(4):
                    act.wait_ge(diag_mm, 16)
                    act.copy(flat[:, i * 512:(i + 1) * 512], ps[:, 4 + i, :]).then_inc(diag_moved, 1)

            def hgrn_end():
                flat = a_off[:].rearrange("p s h t -> p (s h t)")
                for i in range(4):
                    act.wait_ge(off_mm, i // 2 + 1)
                    act.copy(flat[:, i * 512:(i + 1) * 512], ps[:, 4 + i, :]).then_inc(off_moved, 1)
                flat = qb[:].rearrange("p h t -> p (h t)")
                for i in range(4):
                    act.wait_ge(ho_mm, HEADS)
                    act.copy(flat[:, i * 512:(i + 1) * 512], ps[:, 4 + i, :]).then_inc(ho_moved, 1)
                act.wait_ge(ho_moved, 4)
                act.activation(kf[:, :, :], qb[:, :, :], ACT.Square).then_inc(ho_sq, 1)
                act.activation(hf[:, :, :], hg[:, :, :], ACT.Sigmoid).then_inc(hg_sig, 1)
                root(kb[:].rearrange("p h t -> p (h t)"), ho_stat)
                act.wait_ge(h_out, 3)
                act.copy(acts[:, HEADS:2 * HEADS, 0, :], qb[:, :, :]).then_inc(h_hi, 1)

            def before_in_m():
                act.wait_ge(summed, summed_all("in_h"))
                act.wait_ge(mods_done, 8)
                hgrn_start()

            def before_uq():
                act.wait_ge(summed, summed_all("in_m"))
                hgrn_end()
                norm(n_q)
                apply(a_q)
                act.wait_ge(*a_q.lo(4))
                norm(n_kv)
                apply(a_kv)

            def before_w_o():
                act.wait_ge(angles, 2)
                act.activation(cos_sin[ROPE:P, :, :], ang[ROPE:P, 0:2, :], ACT.Sin).then_inc(sines, 1)
                attention(att1)

            def before_up_0():
                act.wait_ge(summed, summed_all("w_o"))
                norm(n_y1)
                norm(n_x2, r_y1)
                apply(a_x2)

            def gate_z():
                act.wait_ge(summed, summed_all("in_c"))
                act.activation(cb, cb, ACT.Sigmoid).then_inc(cb_sig, 1)

            def before_in_c():
                act.wait_ge(extra, extra_all("down_1"))
                norm(n_m1)
                norm(n_x3, r_m1)
                apply(a_x3)

            def before_att_o():
                act.wait_ge(summed, summed_all("in_g"))
                act.activation(gate2[:, 0:DT, :], gate2[:, 0:DT, :], ACT.Sigmoid).then_inc(gates_sig, 1)
                act.activation(gate2[:, DT:, :], gate2[:, DT:, :], ACT.Sigmoid).then_inc(gates_sig, 1)
                attention(att2)
                for k in range(HEADS):
                    act.wait_ge(ln_center, k + 1)
                    if k >= 4:
                        act.wait_ge(ln_mm, 1 + k - 3)
                    act.activation(ring[:, k % 4, :], zc[:, k, :], ACT.Square).then_inc(ln_sq, 1)
                root(rstd[:, :], ln_stat)
                act.wait_ge(ln_bias, HEADS)
                act.activation(cb, zc, ACT.Sigmoid).then_inc(ln_sig, 1)
                act.wait_ge(ln_norm, HEADS + 1)
                split_tiles(s_conv)

            def before_out_2():
                act.wait_ge(extra, extra_all("conv_o"))
                split_tiles(s_merged)

            def before_gate_up():
                act.wait_ge(summed, summed_all("out_2"))
                norm(n_y2)
                norm(n_x4, r_y2)
                apply(a_x4)

            hooks = {"in_m": before_in_m, "uq": before_uq, "w_o": before_w_o, "up_0": before_up_0, "in_c": before_in_c,
                     "in_qk": gate_z, "att_o": before_att_o, "out_2": before_out_2,
                     "gate_up": before_gate_up}
            start()
            follow_stream(act, phases, split, evict, hooks)
            act.wait_ge(summed, summed_all("down_2"))
            norm(n_m2)
            for g in range(8):
                half, b4 = divmod(g, 4)
                act.wait_ge(out_turned, g + 1)
                act.copy(y_nat[:, half, b4 * 512:(b4 + 1) * 512], ps[:, b4, :]).then_inc(out_moved, 1)

        @block.vector
        def _(dve):
            count = [0]

            def link(ins):
                ins.then_inc(dve_chain, 1)
                count[0] += 1
                dve.wait_ge(dve_chain, count[0])

            def split(ph, it, b, first, ids):
                lin_ = ph.body[b][0]
                for j in ids:
                    kn, slot = ph.chunks[j][2], j % SLOTS
                    dve.wait_ge(hi_ready, chunk_seq(ph, it, j) + 1)
                    cut = (slice(None), slot, slice(0, kn), slice(0, lin_.width))
                    dve.tensor_tensor(w_lo[cut], w_raw[cut], w_hi[cut].bitcast(F32),
                                      ALU.subtract).then_inc(lo_ready, 1)
                    if not (first and b == 0):
                        beside(ph, it, j, first)

            def beside(ph, it, j, first):
                for i in pieces_at(ph, j):
                    modulation(ph, it, i, first)
                if ph.name == "in_m" and j % 2 == 1 and 3 <= j < 2 * N_STEPS + 3:
                    level_step((j - 3) // 2)
                if ph.name == "in_qk":
                    steps = 2 * EARLY_TAPS
                    for n in range(j * steps // ph.n_chunks, (j + 1) * steps // ph.n_chunks):
                        i, tap = divmod(n, EARLY_TAPS)
                        convolution(it * 2 + i, tap, it * steps + n)
                if ph.name == "in_g":
                    steps = TAPS - EARLY_TAPS
                    for n in range(j * steps // ph.n_chunks, (j + 1) * steps // ph.n_chunks):
                        convolution(it, EARLY_TAPS + n, it * steps + (HEADS * EARLY_TAPS + n))

            def modulation(ph, it, i, first):
                s = ph.side
                slot = i % MOD_SLOTS
                uses = (s.piece0 + i) // MOD_SLOTS + it * (s.pieces // MOD_SLOTS) + 1
                dve.wait_ge(mod_landed[slot], uses * 16)
                acc = mod_acc[:].rearrange("p a b -> p (a b)")[:, i * s.width:(i + 1) * s.width]
                done = s.product0 + (it * s.pieces + i) * s.rows
                for k in range(s.rows):
                    w = mod_w[:, slot, k * s.width:(k + 1) * s.width]
                    c = silu_c[:, bass.ds(it * s.rows + (DT + k), 1)]
                    if first and k == 0:
                        ins = dve.tensor_scalar(acc, w, c, None, ALU.mult)
                    else:
                        dve.wait_ge(side_products, done + k)
                        ins = dve.scalar_tensor_tensor(acc, w, c, acc, ALU.mult, ALU.add)
                    ins.then_inc(side_products, 1)

            def convolution(tile, n, done):
                tap = (PAD, *range(PAD), *range(PAD + 1, TAPS))[n]
                shift = tap - PAD
                to, end = max(0, -shift), min(T, T - shift)
                w = cols[:, bass.ds(tile + (COLUMN["w_dw_2"] + tap * HEADS), 1)]
                z_ = z[:, bass.ds(tile, 1), to + shift:end + shift]
                o = zc[:, bass.ds(tile, 1), to:end]
                if n == 0:
                    ins = dve.tensor_scalar(o, z_, w, cols[:, bass.ds(tile + COLUMN["b_dw_2"], 1)],
                                            ALU.mult, ALU.add)
                else:
                    dve.wait_ge(conv_step, done)
                    ins = dve.scalar_tensor_tensor(o, z_, w, o, ALU.mult, ALU.add)
                ins.then_inc(conv_step, 1)

            def evict(ph, it, b, first):
                lin_, p0, stride = ph.body[b]
                seq = panel_seq(ph, it, b)
                pair, n = bank_pair(ph, b), len(lin_.tiles)
                tile0 = 2 * (p0 + it * stride)
                tiles = bass.ds(tile0, n)
                ex = extra_seq(ph, it, b)
                high, low = ps[:, 2 * pair:2 * pair + n, 0:T], half_sum[:, pair, 0:n, :]
                dve.wait_ge(half_ready, seq + 1)
                if lin_.kind == "plain":
                    dve.tensor_tensor(lin_.out[:, tiles, :], high, low, ALU.add).then_inc(summed, 1)
                    return
                tmp = lin_.tmp[:, pair, :, :]
                dve.tensor_tensor(tmp, high, low, ALU.add).then_inc(summed, 1)
                dve.wait_ge(summed, seq + 1)
                if lin_.kind == "add":
                    o = lin_.out[:, tiles, :]
                    dve.tensor_tensor(o, o, tmp, ALU.add).then_inc(extra, 1)
                elif lin_.kind == "gated":
                    o = lin_.out[:, tiles, :]
                    dve.tensor_tensor(o, o, tmp, ALU.mult).then_inc(extra, 1)
                elif lin_.kind == "gated_add":
                    dve.tensor_tensor(tmp, tmp, gate2[:, bass.ds(tile0 + DT, n), :], ALU.mult).then_inc(extra, 1)
                    dve.wait_ge(extra, ex + 1)
                    o = lin_.out[:, tiles, :]
                    dve.tensor_tensor(o, o, tmp, ALU.add).then_inc(extra, 1)
                elif lin_.kind == "gate":
                    dve.wait_ge(sigmoid_ready, ph_gate_seq(ph, it) + 1)
                    dve.tensor_tensor(gate3[:, :, :], gate3[:, :, :], tmp, ALU.mult).then_inc(extra, 1)
                else:
                    if lin_.kind == "relu2":
                        dve.scalar_tensor_tensor(tmp, tmp, 0.0, tmp, ALU.max, ALU.mult).then_inc(extra, 1)
                    else:
                        dve.wait_ge(extra, ex)
                        dve.tensor_tensor(tmp, gate3[:, :, :], tmp, ALU.mult).then_inc(extra, 1)
                    dve.wait_ge(extra, ex + 1)
                    hi = lin_.out[:, tiles, 0, :]
                    dve.tensor_scalar(hi, tmp, 1.0, None, ALU.mult).then_inc(extra, 1)
                    dve.wait_ge(extra, ex + 2)
                    dve.tensor_tensor(lin_.out[:, tiles, 1, :], tmp, hi.bitcast(F32), ALU.subtract).then_inc(extra, 1)

            def ph_gate_seq(ph, it):
                return it

            def invert_root(ap, stat):
                dve.wait_ge(*stat(2))
                dve.reciprocal(ap, ap).then_inc(stat.sem, 1)
                dve.wait_ge(*stat(3))

            def norm(n):
                dve.wait_ge(*n.added(n.tiles))
                dve.tensor_scalar(rstd[:, :], ps[:, 5, 0:T], 1.0 / n.dim, EPS, ALU.mult, ALU.add).then_inc(n.stat.sem, 1)
                invert_root(rstd[:, :], n.stat)

            def apply(a):
                def low(k):
                    dve.wait_ge(*a.hi(k + 1))
                    hi = a.dst[:, k, 0, :].bitcast(F32)
                    if a.shift is None:
                        ins = dve.tensor_tensor(a.dst[:, k, 1, :], ring[:, k % 4, :], hi, ALU.subtract)
                    else:
                        tile, c0 = a.shift
                        ins = dve.scalar_tensor_tensor(a.dst[:, k, 1, :], ring[:, k % 4, :],
                                                       tile[:, c0 + k:c0 + k + 1], hi, ALU.add, ALU.subtract)
                    ins.then_inc(a.lo.sem, 1)

                for k in range(a.tiles + 2):
                    if k < a.tiles:
                        if k >= 4:
                            dve.wait_ge(*a.lo(k - 3))
                        dve.scalar_tensor_tensor(ring[:, k % 4, :], a.src[:, k, :], a.gain[:, k:k + 1],
                                                 rstd[:, :], ALU.mult, ALU.mult).then_inc(a.scaled.sem, 1)
                    if k >= 2:
                        low(k - 2)
                dve.wait_ge(*a.lo(a.tiles))

            def residual(r, gain):
                for j in range(4):
                    for k in range(4 * j, 4 * j + 4):
                        dve.scalar_tensor_tensor(r.src[:, k, :], r.src[:, k, :], gain[:, k:k + 1],
                                                 rstd[:, :], ALU.mult, ALU.mult).then_inc(r.scaled.sem, 1)
                    dve.wait_ge(*r.scaled(4 * j + 4))
                    cut = slice(4 * j, 4 * j + 4)
                    dve.tensor_tensor(x_res[:, cut, :], x_res[:, cut, :], r.src[:, cut, :],
                                      ALU.add).then_inc(r.added.sem, 1)
                dve.wait_ge(*r.added(4))

            def scale_gain(name, scale):
                link(dve.scalar_tensor_tensor(gains[:, :], mods[:, scale * DT:(scale + 1) * DT], 1.0,
                                              column(name, 0, DT), ALU.add, ALU.mult))

            def gate_gain(name, gate):
                link(dve.tensor_tensor(gains[:, :], mods[:, gate * DT:(gate + 1) * DT],
                                       column(name, 0, DT), ALU.mult))

            def split_tiles(s):
                for n, k in enumerate(range(0, s.tiles, 2)):
                    dve.wait_ge(*s.hi(n + 1))
                    dve.tensor_tensor(s.dst[:, k:k + 2, 1, :], s.src[:, k:k + 2, :],
                                      s.dst[:, k:k + 2, 0, :].bitcast(F32), ALU.subtract).then_inc(s.lo.sem, 1)

            def attention(a):
                for u in range(UNITS + 5):
                    if u < UNITS:
                        dve.wait_ge(*a.scores(u + 1))
                        src = ps[:, 4 + u % 2, 0:T]
                        if a.bias is not None:
                            if u >= 2:
                                dve.wait_ge(*a.turned(u - 1))
                            h, half = divmod(u, 2)
                            dve.scalar_tensor_tensor(
                                a.prob[:, u % 2, :], src, a.scale,
                                a.bias[:, half, h, :, :].rearrange("p i c -> p (i c)"),
                                ALU.mult, ALU.add).then_inc(a.biased.sem, 1)
                            dve.wait_ge(*a.biased(u + 1))
                            src = a.prob[:, u % 2, :]
                        dve.tensor_reduce(small[:, u, 0:1], src, AX.X, ALU.max).then_inc(a.maxed.sem, 1)
                        dve.wait_ge(*a.maxed(2 * u + 1))
                        dve.tensor_scalar(small[:, u, 1:2], small[:, u, 0:1],
                                          -(a.scale if a.bias is None else 1.0), None,
                                          ALU.mult).then_inc(a.maxed.sem, 1)
                    if 1 <= u <= UNITS:
                        v = u - 1
                        dve.wait_ge(*a.exped(v + 1))
                        dve.reciprocal(small[:, v, 3:4], small[:, v, 2:3]).then_inc(a.inverted.sem, 1)
                        dve.wait_ge(*a.inverted(v + 1))
                        dve.tensor_scalar(a.prob[:, v % 2, :], a.prob[:, v % 2, :], small[:, v, 3:4], None,
                                          ALU.mult).then_inc(a.normed.sem, 1)
                    if u >= 4 and u % 2 == 0 and (u - 4) // 2 < HEADS:
                        h = (u - 4) // 2
                        dve.wait_ge(*a.hi(h + 1))
                        dve.tensor_tensor(acts[:, h, 1, :], ps[:, 7, 0:T], acts[:, h, 0, :].bitcast(F32),
                                          ALU.subtract).then_inc(a.lo.sem, 1)

            def take_mods(groups, before):
                dve.wait_ge(mod_mm, before + groups)
                at_ = 8 * before
                dve.tensor_tensor(mods[:, at_:at_ + 8 * groups], ps[:, 4, 0:8 * groups],
                                  column("b_mod", at_, 8 * groups), ALU.add).then_inc(mods_done, groups)
                dve.wait_ge(mods_done, before + groups)

            def start():
                dve.memset(ones[:, :], 1.0).then_inc(const_set, 1)
                dve.wait_ge(c_sig, 1)
                dve.tensor_tensor(silu_c[:, DT:2 * DT], silu_c[:, 0:DT], column("c", 0, DT),
                                  ALU.mult).then_inc(c_silu, 1)
                dve.wait_ge(c_silu, 1)
                for s in range(SLOTS):
                    dve.wait_ge(landed[s], 16)
                    dve.tensor_scalar(mod_acc_a[:, s, :], w_mod_slots[:, s, :], silu_c[:, DT:DT + 1], None,
                                      ALU.mult).then_inc(mod_products, 1)
                with dve.Fori(1, DT) as k:
                    for s in range(SLOTS):
                        dve.wait_ge(landed[s], k * 16 + 16)
                        dve.wait_ge(mod_products, (k - 1) * SLOTS + (s + 1))
                        dve.scalar_tensor_tensor(mod_acc_a[:, s, :], w_mod_slots[:, s, :],
                                                 silu_c[:, bass.ds(k + DT, 1)], mod_acc_a[:, s, :],
                                                 ALU.mult, ALU.add).then_inc(mod_products, 1)
                dve.wait_ge(late_loads, 16 * N_LATE)
                link(dve.tensor_copy(masks[:].rearrange("p a l t -> p (a l t)"), masks_i[:, :]))
                norm(n_x1)
                take_mods(4, 0)
                scale_gain("pre_mix_g", 1)
                apply(a_x1)

            def hgrn_start():
                for i, name in enumerate(("hgrn_lb_logits_fwd", "hgrn_lb_logits_bwd")):
                    dve.tensor_tensor(lb[:, 2 * i, :], column(name, 0, HEADS), column(name, HEADS, HEADS),
                                      ALU.subtract).then_inc(lb_diff, 1)
                dve.wait_ge(lb_sig, 2)
                for i in range(2):
                    link(dve.tensor_scalar(lb[:, 2 * i + 1, :], lb[:, 2 * i, :], -1.0, 1.0, ALU.mult, ALU.add))
                for i, f in enumerate((hf, hb)):
                    dve.wait_ge(f_sig, i + 1)
                    for h in range(HEADS):
                        dve.tensor_scalar(f[:, h, :], f[:, h, :], lb[:, 2 * i + 1, h:h + 1],
                                          lb[:, 2 * i, h:h + 1], ALU.mult, ALU.add).then_inc(f_done, 1)
                    dve.wait_ge(f_done, HEADS * (i + 1))
                    dve.tensor_scalar((kf, kb)[i][:, :, :], f, -1.0, 1.0, ALU.mult, ALU.add).then_inc(k_done, 1)
                dve.wait_ge(k_done, 2)
                dve.tensor_tensor(qb[:, :, :], kf[:, :, :], kb[:, :, :], ALU.add).then_inc(ksum_done, 1)
                dve.wait_ge(diag_mm, 16)
                dve.tensor_tensor(qb[:, :, :], hq, hb, ALU.mult).then_inc(q_done, 1)
                dve.wait_ge(q_done, 1)
                dve.tensor_tensor(hq, hq, hf, ALU.mult).then_inc(q_done, 1)
                dve.wait_ge(q_done, 2)
                dve.wait_ge(diag_moved, 4)

            def level_step(step):
                n, way = divmod(step, 2)
                m = LEVELS[n]
                kk, qq, ff = ((kf, hq, hf), (kb, qb, hb))[way]
                late, early = 1 - way, way
                dve.wait_ge(level_mm, step + 1)
                if step:
                    dve.wait_ge(level_selected, step)
                a = a_diag[:].rearrange("p h s (b two m) -> p (h s) b two m", two=2, m=m)
                got = ps[:, 4 + 2 * way:6 + 2 * way, :].rearrange("p k (g b m) -> p (k g) b m", g=8, m=m)
                mask = masks[:, way, n, :].rearrange("p (g b m) -> p g b m", g=1, m=m)
                dve.copy_predicated(a[:, :, :, late, :], mask.to_broadcast([P, 2 * HEADS, 64 // m, m]),
                                    got).then_inc(level_selected, 1)
                q_ = qq[:].rearrange("p h (b two m) -> p (h b) two m", two=2, m=m)
                k_ = kk[:].rearrange("p h (b two m) -> p (h b) two m", two=2, m=m)
                f_ = ff[:].rearrange("p h (b two m) -> p (h b) two m", two=2, m=m)
                pairs = HEADS * T // (2 * m)
                dve.tensor_tensor(q_[:, :, late, :], q_[:, :, late, :],
                                  f_[:, :, early, 0:1].to_broadcast([P, pairs, m]),
                                  ALU.mult).then_inc(level_updated, 1)
                dve.tensor_tensor(k_[:, :, early, :], k_[:, :, early, :],
                                  f_[:, :, late, 0:1].to_broadcast([P, pairs, m]),
                                  ALU.mult).then_inc(level_updated, 1)
                dve.wait_ge(level_updated, 3 * step + 2)
                dve.tensor_tensor(f_[:, :, 0, 0:1], f_[:, :, 0, 0:1], f_[:, :, 1, 0:1],
                                  ALU.mult).then_inc(level_updated, 1)

            def hgrn_end():
                dve.wait_ge(level_selected, N_STEPS)
                dve.wait_ge(level_updated, 3 * N_STEPS)
                dve.wait_ge(ho_sum, HEADS)
                flat = kb[:].rearrange("p h t -> p (h t)")
                dve.tensor_scalar(flat, ps[:, 4:8, :].rearrange("p b n -> p (b n)"), 1.0 / P, EPS,
                                  ALU.mult, ALU.add).then_inc(ho_stat.sem, 1)
                invert_root(flat, ho_stat)
                dve.wait_ge(ho_sq, 1)
                dve.scalar_tensor_tensor(qb[:, :, :], qb[:, :, :], column("hgrn_norm_g"), kb[:, :, :],
                                         ALU.mult, ALU.mult).then_inc(h_out, 1)
                dve.wait_ge(hg_sig, 1)
                dve.tensor_tensor(hg, hg, hf, ALU.mult).then_inc(h_out, 1)
                dve.wait_ge(h_out, 2)
                dve.tensor_tensor(qb[:, :, :], qb[:, :, :], hg, ALU.mult).then_inc(h_out, 1)
                dve.wait_ge(h_hi, 1)
                dve.wait_ge(h_out, 3)
                dve.tensor_tensor(acts[:, HEADS:2 * HEADS, 1, :], qb[:, :, :],
                                  acts[:, HEADS:2 * HEADS, 0, :].bitcast(F32), ALU.subtract).then_inc(h_lo, 1)
                dve.wait_ge(h_lo, 1)

            def before_in_m():
                dve.wait_ge(summed, summed_all("in_h"))
                take_mods(4, 4)
                hgrn_start()

            def before_uq():
                dve.wait_ge(summed, summed_all("in_m"))
                hgrn_end()
                norm(n_q)
                apply(a_q)
                norm(n_kv)
                apply(a_kv)

            def rope_angles():
                r = slice(ROPE, P)
                c1 = 6.28125
                c2 = float(np.float32(np.floor((TWO_PI - c1) * 2 ** 21) / 2 ** 21))
                c3 = TWO_PI - c1 - c2
                magic = 12582912.0
                dve.wait_ge(pos_landed, 16)
                link(dve.tensor_copy(ang[r, 1, :], pos_i[r, :]))
                link(dve.tensor_scalar(ang[r, 1, :], ang[r, 1, :], consts[r, C_FREQ:C_FREQ + 1], None, ALU.mult))
                link(dve.tensor_copy(ang[r, 0, :], ang[r, 1, :]))
                for i, quarter in ((0, 0.25), (1, 0.0)):
                    a, n = ang[r, i, :], ang[r, 2, :]
                    link(dve.tensor_scalar(n, a, 1 / TWO_PI, quarter, ALU.mult, ALU.add))
                    link(dve.tensor_scalar(n, n, magic, None, ALU.add))
                    link(dve.tensor_scalar(n, n, -magic, None, ALU.add))
                    for c in (c1, c2, c3):
                        link(dve.scalar_tensor_tensor(a, n, -c, a, ALU.mult, ALU.add))
                    link(dve.tensor_scalar(a, a, quarter * TWO_PI, 3.1415925, ALU.add, ALU.min))
                    dve.tensor_scalar(a, a, -3.1415925, None, ALU.max).then_inc(angles, 1)
                    dve.wait_ge(angles, i + 1)

            def rotate(x, turned, cos, sin):
                dve.tensor_tensor(rot_of(x), turned, sin, ALU.mult).then_inc(rot_done, 1)
                dve.tensor_tensor(x, x, cos, ALU.mult).then_inc(rot_done, 1)

            def before_w_o():
                rope_angles()
                r = slice(ROPE, P)
                dve.wait_ge(sines, 1)
                dve.wait_ge(summed, summed_all("ukv"))
                dve.wait_ge(rot_mm, 1)
                kr = proj[r, 6, :]
                dve.tensor_tensor(rot[r, 0, :], ps[r, 4, 0:T], cos_sin[r, 1, :], ALU.mult).then_inc(rot_done, 1)
                dve.tensor_tensor(kr, kr, cos_sin[r, 0, :], ALU.mult).then_inc(rot_done, 1)
                dve.wait_ge(rot_done, 2)
                dve.tensor_tensor(kr, kr, rot[r, 0, :], ALU.add).then_inc(rot_done, 1)
                dve.wait_ge(rot_done, 3)
                dve.wait_ge(rot_mm, 5)
                qr = q1[r, :, 1, :]

                def over_heads(i):
                    return cos_sin[r, i:i + 1, :].to_broadcast([ROPE, HEADS, T])

                dve.tensor_tensor(rot[r, :, :], ps[r, 4:8, :].rearrange("p b (h t) -> p (b h) t", t=T),
                                  over_heads(1), ALU.mult).then_inc(rot_done, 1)
                dve.tensor_tensor(qr, qr, over_heads(0), ALU.mult).then_inc(rot_done, 1)
                dve.wait_ge(rot_done, 5)
                dve.tensor_tensor(qr, qr, rot[r, :, :], ALU.add).then_inc(rot_done, 1)
                attention(att1)
                dve.wait_ge(*att1.lo(HEADS))

            def before_up_0():
                take_mods(2, 8)
                dve.wait_ge(summed, summed_all("w_o"))
                gate_gain("post_mix_g", 2)
                norm(n_y1)
                residual(r_y1, gains)
                scale_gain("pre_mlp_g", 4)
                norm(n_x2)
                apply(a_x2)

            def before_in_c():
                dve.wait_ge(extra, extra_all("down_1"))
                gate_gain("post_mlp_g", 5)
                norm(n_m1)
                residual(r_m1, gains)
                norm(n_x3)
                apply(a_x3)

            def gate_z():
                dve.wait_ge(cb_sig, 1)
                dve.tensor_tensor(z, ca, cb, ALU.mult).then_inc(z_done, 1)
                dve.wait_ge(z_done, 1)

            def before_att_o():
                dve.wait_ge(summed, summed_all("in_g"))
                outside = consts[:, C_WIN:C_WIN + GRID_W].rearrange("p (o c) -> p o c", o=1)
                for i in range(8):
                    dve.wait_ge(bias_mm, i + 1)
                    dve.tensor_tensor(bias_rows[:, i, :].rearrange("p (n c) -> p n c", c=GRID_W),
                                      ps[:, 4 + i % 4, :].rearrange("p (n c) -> p n c", c=GRID_W),
                                      outside.to_broadcast([P, 512 // GRID_W, GRID_W]),
                                      ALU.add).then_inc(bias_done, 1)
                dve.wait_ge(bias_done, 8)
                attention(att2)
                dve.wait_ge(*att2.lo(HEADS))
                dve.wait_ge(ln_mm, 1)
                dve.tensor_scalar(mean[:, :], ps[:, 4, 0:T], 1.0 / (HEADS * P), None, ALU.mult).then_inc(ln_mean, 1)
                dve.wait_ge(ln_mean, 1)
                for k in range(HEADS):
                    dve.tensor_tensor(zc[:, k, :], zc[:, k, :], mean[:, :], ALU.subtract).then_inc(ln_center, 1)
                dve.wait_ge(ln_center, HEADS)
                dve.wait_ge(ln_mm, 1 + HEADS)
                dve.tensor_scalar(rstd[:, :], ps[:, 5, 0:T], 1.0 / (HEADS * P), EPS, ALU.mult,
                                  ALU.add).then_inc(ln_stat.sem, 1)
                invert_root(rstd[:, :], ln_stat)
                for k in range(HEADS):
                    dve.scalar_tensor_tensor(zc[:, k, :], zc[:, k, :], column("conv_ln_g_2", k), rstd[:, :],
                                             ALU.mult, ALU.mult).then_inc(ln_norm, 1)
                for k in range(HEADS):
                    dve.wait_ge(ln_norm, k + 1)
                    dve.tensor_scalar(zc[:, k, :], zc[:, k, :], column("conv_ln_b_2", k), None,
                                      ALU.add).then_inc(ln_bias, 1)
                dve.wait_ge(ln_sig, 1)
                dve.wait_ge(ln_bias, HEADS)
                dve.tensor_tensor(zc, zc, cb, ALU.mult).then_inc(ln_norm, 1)
                dve.wait_ge(ln_norm, HEADS + 1)
                split_tiles(s_conv)
                dve.wait_ge(gates_sig, 2)

            def before_out_2():
                dve.wait_ge(extra, extra_all("conv_o"))
                split_tiles(s_merged)

            def before_gate_up():
                dve.wait_ge(summed, summed_all("out_2"))
                norm(n_y2)
                residual(r_y2, column("mix_post_g_2", 0, DT))
                norm(n_x4)
                apply(a_x4)

            hooks = {"in_m": before_in_m, "uq": before_uq, "w_o": before_w_o, "up_0": before_up_0,
                     "down_0": lambda: take_mods(2, 10), "in_c": before_in_c, "in_qk": gate_z,
                     "att_o": before_att_o, "out_2": before_out_2, "gate_up": before_gate_up}
            start()
            follow_stream(dve, phases, split, evict, hooks, beside)
            dve.wait_ge(summed, summed_all("down_2"))
            norm(n_m2)
            residual(r_m2, column("ffn_post_g_2", 0, DT))


def follow_stream(eng, phases, split, evict, hooks, beside=None):
    def run(ph, it, first, before):
        for b in range(len(ph.body)):
            ids = chunk_ids(ph, b)
            split(ph, it, b, first, ids[:SLOTS])
            if b:
                evict(ph, it, b - 1, first)
            elif before:
                evict(*before)
            if first and b == 0 and ph.name in hooks:
                hooks[ph.name]()
            if first and b == 0 and beside:
                for j in ids:
                    beside(ph, it, j, first)
            split(ph, it, b, first, ids[SLOTS:])

    before = None
    for ph in phases:
        last = len(ph.body) - 1
        run(ph, 0, True, before)
        if ph.iters > 1:
            with eng.Fori(1, ph.iters) as it:
                run(ph, it, False, (ph, it - 1, last, False))
        before = (ph, ph.iters - 1, last, ph.iters == 1)
    evict(*before)


def chunk_ids(ph, b):
    return [j for j, (bb, _, _) in enumerate(ph.chunks) if bb == b]


def vector_loads(d, v_rows, early):
    for name, rows in VECTORS:
        src = d[name].rearrange("a (r p) -> (a r) p", p=P) if name != "w_dw_2" else \
            d[name][0].rearrange("j (r p) -> (j r) p", p=P)
        done = 0
        while done < rows:
            tile, at_row = divmod(COLUMN[name] + done, P)
            n = min(rows - done, P - at_row)
            if early == (tile == 0):
                yield v_rows[at_row:at_row + n, tile, :], src[done:done + n, :]
            done += n


N_VECTOR_LOADS = sum((COLUMN[n] + r - 1) // P - COLUMN[n] // P + 1 for n, r in VECTORS)
N_EARLY_VECTORS = sum(COLUMN[n] < P for n, _ in VECTORS)
N_EARLY = 1 + N_EARLY_VECTORS + 2
N_LATE = 1 + N_VECTOR_LOADS - N_EARLY_VECTORS

INPUTS = ["x", "positions", "w_mod", "w_in", "w_uq", "w_ukv", "w_out", "w_up", "w_down", "w_in_2",
          "rpb_2", "w_attn_o_2", "w_conv_o_2", "w_out_2", "w_gate_up_2", "w_down_2"]


def kernel(**inputs):
    import concourse.bacc as bacc
    from concourse.bass_utils import run_bass_kernel_spmd

    nc = bacc.Bacc("TRN2", target_bir_lowering=False, num_devices=1)
    arrays, d = {}, {}
    for name in INPUTS + [n for n, _ in VECTORS]:
        arrays[f"in_{name}"] = np.ascontiguousarray(inputs[name])
    arrays["in_consts"], arrays["in_masks"] = constants()
    for key, a in arrays.items():
        d[key[3:]] = nc.dram_tensor(key, a.shape, mybir.dt.from_np(a.dtype), kind="ExternalInput").ap()
    out = nc.dram_tensor("out", (1, T, D), F32, kind="ExternalOutput").ap()
    build(nc, d, out)
    r = run_bass_kernel_spmd(nc, [arrays], core_ids=[0])
    return r.results[0]["out"]
```

```python
from contextlib import ExitStack

import numpy as np

import concourse.bass as bass
from concourse import mybir

F32 = mybir.dt.float32
F32R = mybir.dt.float32r
I32 = mybir.dt.int32
U8 = mybir.dt.uint8
ALU = mybir.AluOpType
ACT = mybir.ActivationFunctionType
AX = mybir.AxisListType

P = 128
T = 256
D = 2048
DT = D // P
HEADS = 8
KT = 4
CW = 256
SLOTS = 4
MW = 1024
SECTION_PIECES = 2 * DT
MOD_SLOTS = 4
EPS = 1e-6
Q_RANK, KV_RANK, ROPE = 512, 256, 64
D_FF, D_FF2 = 8192, 5632
N_MOD = 6
MLA_SCALE = 192 ** -0.5
NA_SCALE = 128 ** -0.5
GRID_W, WIN_C, WIN_R, GRID_ROWS = 64, 16, 8, 4
RPB_H, RPB_W = 2 * WIN_R - 1, 2 * WIN_C - 1
TAPS = 31
PAD = TAPS // 2
LEVELS = [1, 2, 4, 8, 16, 32, 64]
N_STEPS = 2 * len(LEVELS)
ROUND_TAPS = 10, 4, 17
TWO_PI = 2 * np.pi

VECTORS = [("c", 16), ("b_mod", 96), ("pre_mix_g", 16), ("post_mix_g", 16), ("pre_mlp_g", 16),
           ("post_mlp_g", 16), ("q_norm_g", 4), ("kv_norm_g", 2), ("hgrn_norm_g", 1),
           ("hgrn_lb_logits_fwd", 16), ("hgrn_lb_logits_bwd", 16), ("mix_pre_g_2", 16),
           ("mix_post_g_2", 16), ("ffn_pre_g_2", 16), ("ffn_post_g_2", 16), ("b_dw_2", 8),
           ("conv_ln_g_2", 8), ("conv_ln_b_2", 8), ("w_dw_2", 8 * TAPS)]
COLUMN, _at = {}, 0
for _name, _rows in VECTORS:
    COLUMN[_name] = _at
    _at += _rows
N_COLUMNS = _at
V_TILES = -(-N_COLUMNS // P)

C_IDENT, C_FLIP, C_RT, C_WIN, C_FREQ, C_HEAD = 0, 128, 256, 320, 384, 385
C_COLS = 385 + 2 * HEADS


def constants():
    c = np.zeros((P, C_COLS), np.float32)
    c[:, C_IDENT:C_IDENT + P] = np.eye(P)
    c[:, C_FLIP:C_FLIP + P] = np.kron(np.eye(2), np.eye(GRID_W)[::-1])
    half = ROPE // 2
    for i in range(half):
        c[ROPE + half + i, C_RT + i] = -1.0
        c[ROPE + i, C_RT + half + i] = 1.0
    w = np.arange(GRID_W)
    start = np.clip(w - WIN_C // 2, 0, GRID_W - WIN_C)
    outside = (w[None] < start[:, None]) | (w[None] >= start[:, None] + WIN_C)
    c[:, C_WIN:C_WIN + GRID_W] = np.where(np.tile(outside, (2, 1)), -1e30, 0.0)
    freq = np.float32(10000.0) ** (-np.arange(half, dtype=np.float32) / np.float32(half))
    c[ROPE:, C_FREQ] = np.tile(freq, 2)
    c[:, C_HEAD + HEADS] = 1.0
    s = np.arange(P)[:, None]
    masks = np.zeros((P, 2, len(LEVELS), P // 2), np.int32)
    for n, m in enumerate(LEVELS):
        blocks = np.arange(P).reshape(-1, 2, m)
        later, earlier = blocks[:, 1].ravel()[None], blocks[:, 0].ravel()[None]
        masks[:, 0, n] = s // m == later // m - 1
        masks[:, 1, n] = s // m == earlier // m + 1
    return c, masks.reshape(P, -1)


EXTRA = {"plain": 0, "relu2": 3, "add": 1, "gated": 1, "gated_add": 2, "gate": 1, "up": 3}


class Linear:

    def __init__(self, w, act, row_tile=0, row_tiles=DT, col0=0, width=CW, tiles=(0, P), out=None,
                 kind="plain", step=CW, tmp=None):
        self.w, self.act, self.row_tile, self.row_tiles = w, act, row_tile, row_tiles
        self.col0, self.width, self.tiles, self.out, self.kind = col0, width, tiles, out, kind
        self.step, self.tmp = step, tmp
        self.chunks = [(k, min(KT, row_tiles - k)) for k in range(0, row_tiles, KT)]


class Side:

    def __init__(self, rows, section, pieces):
        self.rows, self.section, self.pieces, self.width = rows, section, pieces, MW // rows


class Phase:

    def __init__(self, name, iters, body, side=None):
        self.name, self.iters, self.body, self.side = name, iters, body, side
        self.chunks = [(b, k0, kn) for b, (lin, _, _) in enumerate(body) for k0, kn in lin.chunks]
        self.n_chunks = len(self.chunks)
        self.n_panels = len(body)
        self.slot_uses = [sum(j % SLOTS == s for j in range(self.n_chunks)) for s in range(SLOTS)]


def plan_sides(phases):
    pieces = products = 0
    for ph in phases:
        if ph.side:
            ph.side.piece0, ph.side.product0 = pieces, products
            assert ph.side.rows * ph.iters == DT and pieces % MOD_SLOTS == 0
            pieces += ph.side.pieces * ph.iters
            products += ph.side.pieces * ph.side.rows * ph.iters


def plan(phases, uses):
    chunks, uses, panels, extras = 0, list(uses), 0, 0
    last = [None] * SLOTS
    for ph in phases:
        ph.chunk0, ph.use0, ph.panel0, ph.extra0 = chunks, list(uses), panels, extras
        ph.last_before = list(last)
        for s in range(SLOTS):
            uses[s] += ph.slot_uses[s] * ph.iters
        ph.n_extra = sum(EXTRA[lin.kind] for lin, _, _ in ph.body)
        extras += ph.n_extra * ph.iters
        assert ph.iters == 1 or ph.n_panels % 2 == 0
        panels += ph.n_panels * ph.iters
        for j in range(ph.n_chunks):
            last[j % SLOTS] = chunks + (ph.iters - 1) * ph.n_chunks + j
        chunks += ph.n_chunks * ph.iters
    return phases


def build(nc, d, out):
    ctx = ExitStack()
    with ctx:
        at = [-(-nc.sbuf_base // 32) * 32]
        SBUF_END = nc.sbuf_usable_end

        def place(name, shape, dt, offset=None):
            size = int(np.prod(shape[1:])) * {F32: 4, F32R: 4, I32: 4, U8: 1}[dt]
            size = -(-size // 32) * 32
            if offset is None:
                offset = at[0]
                at[0] += size
            assert offset + size <= SBUF_END, (name, offset, size)
            return nc.alloc_sbuf_tensor_at(name, shape, dt, offset=offset)

        def sem(name):
            return ctx.enter_context(nc.semaphore(name))

        w_raw = place("w_raw", [P, SLOTS, KT, CW], F32)
        w_hi = place("w_hi", [P, SLOTS, KT, CW], F32R)
        w_lo = place("w_lo", [P, SLOTS, KT, CW], F32R)
        x_res = place("x_res", [P, DT, T], F32)
        acts_at = at[0]
        acts = place("acts", [P, DT, 2, T], F32R)
        half_sum = place("half_sum", [P, 2, 2, T], F32)
        cols = place("cols", [P, V_TILES * P], F32)
        consts = place("consts", [P, C_COLS], F32)
        masks = place("masks", [P, 2, len(LEVELS), P // 2], U8)
        ones = place("ones", [P, P], F32)
        silu_c = place("silu_c", [P, 2 * DT], F32)
        mods = place("mods", [P, N_MOD * DT], F32)
        gains = place("gains", [P, DT], F32)
        lb = place("lb", [P, 4, HEADS], F32)
        ring = place("ring", [P, 4, T], F32)
        rstd = place("rstd", [P, T], F32)
        rstd_h = rstd[0:HEADS, :]
        small = place("small", [P, 16, 4], F32)
        big = at[0]
        size_tile = T * 4

        ps = ctx.enter_context(nc.psum_tensor("ps", [P, 8, 512], F32))
        ident = consts[:, C_IDENT:C_IDENT + P]

        x_nat = place("x_nat", [P, 2, D], F32, big)
        v_rows = place("v_rows", [P, V_TILES, P], F32, big + 2 * D * 4)
        masks_i = place("masks_i", [P, 2 * len(LEVELS) * P // 2], I32, big + (2 * D + V_TILES * P) * 4)
        y_nat = place("y_nat", [P, 2, D], F32, big)
        w_mod_slots = w_raw[:].rearrange("p s k n -> p s (k n)")
        mod_acc_a = place("mod_acc_a", [P, 4, MW], F32, big + 24 * size_tile)
        mod_w = place("mod_w", [P, MOD_SLOTS, MW], F32, big + 80 * size_tile)
        mod_acc = place("mod_acc", [P, 4, MW], F32, big + 64 * size_tile)
        tmp_up = place("tmp_up", [P, 2, 2, T], F32, big + 76 * size_tile)
        proj = place("proj", [P, 47, T], F32, big)
        h_big = big + 7 * size_tile
        hq, hf, hb, hv, hg = (proj[:, 7 + 8 * i:15 + 8 * i, :] for i in range(5))
        a_diag = place("a_diag", [P, HEADS, 2, P], F32, big + 47 * size_tile)
        a_off = place("a_off", [P, 2, HEADS, P], F32, big + 55 * size_tile)
        kf = place("kf", [P, HEADS, T], F32, big + 63 * size_tile)
        kb = place("kb", [P, HEADS, T], F32, big + 71 * size_tile)
        qb = place("qb", [P, HEADS, T], F32, big + 79 * size_tile)
        hv_tok = place("hv_tok", [P, 2, HEADS, P], F32, big + 87 * size_tile)
        lat = place("lat", [P, 6, 2, T], F32R, h_big)
        q1 = place("q1", [P, HEADS, 2, T], F32, h_big + 12 * size_tile)
        kv1 = place("kv1", [P, HEADS, 2, T], F32, h_big + 28 * size_tile)
        v1_tok = place("v1_tok", [P, 2, HEADS, P], F32, h_big + 44 * size_tile)
        cos_sin = place("cos_sin", [P, 2, T], F32, h_big + 52 * size_tile)
        pos_i = place("pos_i", [P, T], I32, h_big + 54 * size_tile)
        ang = place("ang", [P, 3, T], F32, h_big + 55 * size_tile)
        rot = place("rot", [P, HEADS, T], F32, h_big + 58 * size_tile)
        prob_at = h_big + 66 * size_tile
        prob1 = place("prob1", [P, 2, T], F32, prob_at)
        prob1_t = place("prob1_t", [P, 2, 2, T], F32, prob_at + 2 * size_tile)
        y1 = place("y1", [P, DT, T], F32, big)
        ff_half = D_FF // 2 // P
        ff1 = place("ff1", [P, ff_half, 2, T], F32R, big)
        ym1 = place("ym1", [P, DT, T], F32, big + 2 * ff_half * size_tile)
        tmp1 = place("tmp1", [P, 2, 2, T], F32, big + (2 * ff_half + DT) * size_tile)
        pr2 = place("pr2", [P, 72, T], F32, big)
        q2, k2, v2, ca, cb = (pr2[:, 8 * i:8 * i + 8, :] for i in range(5))
        gate2 = pr2[:, 40:72, :]
        heads_2 = place("heads_2", [P, 2, HEADS, T], F32R, big)[:].rearrange("p two h t -> p h two t")
        bias = place("bias", [P, 2, HEADS, GRID_ROWS, GRID_W], F32, big + 72 * size_tile)
        v2_tok = place("v2_tok", [P, 2, HEADS, P], F32, big + 88 * size_tile)
        prob2 = place("prob2", [P, 2, T], F32, big + 16 * size_tile)
        prob2_t = place("prob2_t", [P, 2, 2, T], F32, big + 18 * size_tile)
        z, zc = cb, ca
        mean = place("mean", [P, T], F32, big + 22 * size_tile)
        y2 = place("y2", [P, DT, T], F32, big + 16 * size_tile)
        tmp2 = place("tmp2", [P, 2, 2, T], F32, big + 72 * size_tile)
        ff2 = place("ff2", [P, D_FF2 // P, 2, T], F32R, big)
        tmp3 = place("tmp3", [P, 2, 2, T], F32, big + 2 * (D_FF2 // P) * size_tile)
        gate3 = place("gate3", [P, 2, T], F32, big + (2 * (D_FF2 // P) + 4) * size_tile)
        ym2 = place("ym2", [P, DT, T], F32, acts_at)

        w_mod, w_in = d["w_mod"][0], d["w_in"][0]
        ug = D_FF2
        panels = D // CW

        def lin(*a, **k):
            return Linear(*a, **k)

        in_h = lin(w_in, acts, col0=832, out=proj[:, 7:47, :])
        in_m = lin(w_in, acts, out=proj[:, 0:6, :])
        in_r = lin(w_in, acts, col0=704, width=P, tiles=(0,), out=proj[:, 6:7, :])
        uq = lin(d["w_uq"][0], lat, row_tiles=4, width=192, step=192, tiles=(0, ROPE),
                 out=q1[:].rearrange("p h two t -> p (h two) t"))
        ukv = lin(d["w_ukv"][0], lat[:, 4:6], row_tiles=2,
                  out=kv1[:].rearrange("p h two t -> p (h two) t"))
        w_o = lin(d["w_out"][0], acts, out=y1)
        up = [lin(d["w_up"][0], acts, col0=h * D_FF // 2, out=ff1, kind="relu2", tmp=tmp1 if h else tmp_up)
              for h in range(2)]
        down = [lin(d["w_down"][0], ff1, row_tile=h * ff_half, row_tiles=ff_half, out=ym1,
                    kind="add" if h else "plain", tmp=tmp1) for h in range(2)]
        in_2 = lin(d["w_in_2"][0], acts, out=pr2)
        att_o = lin(d["w_attn_o_2"][0], heads_2, row_tiles=8, out=gate2[:, 0:16, :], kind="gated", tmp=tmp2)
        conv_o = lin(d["w_conv_o_2"][0], acts[:, 8:16], row_tiles=8, out=gate2[:, 0:16, :],
                     kind="gated_add", tmp=tmp2)
        out_2 = lin(d["w_out_2"][0], acts, out=y2)
        gate_l = lin(d["w_gate_up_2"][0], acts, out=None, kind="gate", tmp=tmp3)
        up_l = lin(d["w_gate_up_2"][0], acts, col0=ug, out=ff2, kind="up", tmp=tmp3)
        down2 = lin(d["w_down_2"][0], ff2, row_tiles=D_FF2 // P, out=ym2)

        phases = plan([
            Phase("in_h", 8, [(in_h, 0, 2), (in_h, 1, 2)], Side(2, 2, 8)),
            Phase("in_m", 1, [(in_h, 16, 0), (in_h, 17, 0), (in_h, 18, 0), (in_h, 19, 0),
                              (in_m, 0, 0), (in_m, 1, 0), (in_m, 2, 0), (in_r, 0, 0)]),
            Phase("uq", 2, [(uq, i, 4) for i in range(4)]),
            Phase("ukv", 2, [(ukv, i, 4) for i in range(4)]),
            Phase("w_o", panels // 2, [(w_o, 0, 2), (w_o, 1, 2)], Side(4, 4, 8)),
            Phase("up_0", 8, [(up[0], 0, 2), (up[0], 1, 2)], Side(2, 5, 4)),
            Phase("down_0", panels // 2, [(down[0], 0, 2), (down[0], 1, 2)]),
            Phase("up_1", 8, [(up[1], 0, 2), (up[1], 1, 2)]),
            Phase("down_1", panels // 2, [(down[1], 0, 2), (down[1], 1, 2)]),
            Phase("in_c", 4, [(in_2, 12, 2), (in_2, 13, 2)]),
            Phase("in_qk", 4, [(in_2, 0, 2), (in_2, 1, 2)]),
            Phase("in_v", 1, [(in_2, 8 + i, 0) for i in range(4)]),
            Phase("in_g", 1, [(in_2, 20 + i, 0) for i in range(16)]),
            Phase("att_o", 1, [(att_o, i, 0) for i in range(panels)]),
            Phase("conv_o", panels // 2, [(conv_o, 0, 2), (conv_o, 1, 2)]),
            Phase("out_2", panels // 2, [(out_2, 0, 2), (out_2, 1, 2)]),
            Phase("gate_up", D_FF2 // CW, [(gate_l, 0, 1), (up_l, 0, 1)]),
            Phase("down_2", panels // 2, [(down2, 0, 2), (down2, 1, 2)]),
        ], uses=[DT] * SLOTS)
        plan_sides(phases)
        by_name = {ph.name: ph for ph in phases}

        landed = [sem(f"landed{s}") for s in range(SLOTS)]
        hi_ready = sem("hi_ready")
        lo_ready = sem("lo_ready")
        chunk_used = sem("chunk_used")
        half_ready = sem("half_ready")
        summed = sem("summed")
        mod_products = sem("mod_products")
        mod_landed = [sem(f"mod_landed{s}") for s in range(MOD_SLOTS)]
        side_products = sem("side_products")
        mod_mm = sem("mod_mm")
        mods_done = sem("mods_done")
        extra = sem("extra")
        sigmoid_ready = sem("sigmoid_ready")

        def chunk_seq(ph, it, j):
            return ph.chunk0 + it * ph.n_chunks + j

        def freed(ph, it, j, first):
            if j >= SLOTS:
                return chunk_seq(ph, it, j - SLOTS) + 1
            if first:
                before = ph.last_before[j % SLOTS]
                return None if before is None else before + 1
            return chunk_seq(ph, it - 1, max(i for i in range(ph.n_chunks) if i % SLOTS == j % SLOTS)) + 1

        def panel_seq(ph, it, b):
            return ph.panel0 + it * ph.n_panels + b

        def piece_seq(ph, it, i):
            return ph.side.piece0 + it * ph.side.pieces + i

        def side_all(name):
            s = by_name[name].side
            return s.product0 + s.rows * s.pieces * by_name[name].iters

        def pieces_at(ph, j):
            every = ph.n_chunks // ph.side.pieces if ph.side else 1
            return [j // every] if ph.side and j % every == every - 1 else []

        def extra_seq(ph, it, b):
            return ph.extra0 + it * ph.n_extra + sum(EXTRA[x.kind] for x, _, _ in ph.body[:b])

        def bank_pair(ph, b):
            return (ph.panel0 + b) % 2

        def summed_all(name):
            ph = by_name[name]
            return ph.panel0 + ph.n_panels * ph.iters

        def extra_all(name):
            ph = by_name[name]
            return ph.extra0 + ph.n_extra * ph.iters

        def column(name, i=0, n=1):
            return cols[:, COLUMN[name] + i:COLUMN[name] + i + n]

        class Count:

            def __init__(self, sem_, base=0):
                self.sem, self.base = sem_, base

            def __call__(self, n):
                return self.sem, self.base + n

        UNITS = 2 * HEADS
        ATT_STEPS = UNITS + 3
        shared = {}

        def count(name, steps):
            if name not in shared:
                shared[name] = [sem(name), 0]
            c = Count(*shared[name])
            shared[name][1] += steps
            return c

        class Norm:

            def __init__(self, src, tiles, dim, bank=5):
                self.src, self.tiles, self.dim, self.bank = src, tiles, dim, bank
                self.squared = count("norm_squared", tiles)
                self.added = count("norm_added", tiles)
                self.stat = count("norm_stat", 3)

        class Apply:

            def __init__(self, src, tiles, gain, dst, shift=None):
                self.src, self.tiles, self.gain, self.dst, self.shift = src, tiles, gain, dst, shift
                self.scaled = count("apply_scaled", tiles)
                self.hi = count("apply_hi", tiles)
                self.lo = count("apply_lo", tiles)

        class Residual:

            def __init__(self, src):
                self.src = src
                self.scaled = count("residual_scaled", DT)
                self.added = count("residual_added", 4)

        class Split:

            def __init__(self, src, tiles, dst):
                self.src, self.tiles, self.dst = src, tiles, dst
                self.hi = count("split_hi", tiles // 2)
                self.lo = count("split_lo", tiles // 2)

        class Attention:

            def __init__(self, v, v_tok, prob, prob_t, dst, scale, bias=None, lag=1):
                self.dst = dst
                self.lag = lag
                self.v, self.v_tok, self.prob, self.prob_t = v, v_tok, prob, prob_t
                self.scale, self.bias = scale, bias
                self.v_turned = count("att_v_turned", UNITS)
                self.v_moved = count("att_v_moved", 4)
                self.scores = count("att_scores", UNITS)
                self.biased = count("att_biased", UNITS if bias is not None else 0)
                self.maxed = count("att_maxed", 2 * UNITS)
                self.exped = count("att_exped", UNITS)
                self.inverted = count("att_inverted", UNITS)
                self.normed = count("att_normed", UNITS)
                self.turned = count("att_turned", UNITS)
                self.moved = count("att_moved", UNITS)
                self.out = count("att_out", HEADS)
                self.hi = count("att_hi", HEADS)
                self.lo = count("att_lo", HEADS)

        n_x1 = Norm(x_res, DT, D)
        a_x1 = Apply(x_res, DT, gains, acts, (mods, 0))
        n_q = Norm(proj, 4, Q_RANK, bank=0)
        n_kv = Norm(proj[:, 4:6, :], 2, KV_RANK, bank=1)
        a_q = Apply(proj, 4, column("q_norm_g", 0, 4), lat)
        a_kv = Apply(proj[:, 4:6, :], 2, column("kv_norm_g", 0, 2), lat[:, 4:6])
        att1 = Attention(kv1[:, :, 1, :], v1_tok, prob1, prob1_t, acts, MLA_SCALE, lag=2)
        n_y1 = Norm(y1, DT, D)
        r_y1 = Residual(y1)
        n_x2 = Norm(x_res, DT, D)
        a_x2 = Apply(x_res, DT, gains, acts, (mods, 3 * DT))
        n_m1 = Norm(ym1, DT, D)
        r_m1 = Residual(ym1)
        n_x3 = Norm(x_res, DT, D)
        a_x3 = Apply(x_res, DT, column("mix_pre_g_2", 0, DT), acts)
        att2 = Attention(v2, v2_tok, prob2, prob2_t, heads_2, NA_SCALE, bias, lag=2)
        s_conv = Split(zc, HEADS, acts[:, HEADS:2 * HEADS])
        s_merged = Split(gate2, DT, acts)
        n_y2 = Norm(y2, DT, D)
        r_y2 = Residual(y2)
        n_x4 = Norm(x_res, DT, D)
        a_x4 = Apply(x_res, DT, column("ffn_pre_g_2", 0, DT), acts)
        n_m2 = Norm(ym2, DT, D)
        r_m2 = Residual(ym2)

        out_norm = {"w_o": n_y1, "down_1": n_m1, "out_2": n_y2, "down_2": n_m2}

        def panel_written(ph, it, b):
            if ph.body[b][0].kind == "add":
                return extra, extra_seq(ph, it, b) + 1
            return summed, panel_seq(ph, it, b) + 1

        dve_chain = sem("dve_chain")
        loads = sem("loads")
        const_set, cols_turned, cols_moved, x_turned, x_moved = map(
            sem, ("const_set", "cols_turned", "cols_moved", "x_turned", "x_moved"))
        x_loads = sem("x_loads")
        late_loads = sem("late_loads")
        c_sig, c_silu = map(sem, ("c_sig", "c_silu"))
        lb_diff, lb_sig, f_sig, f_done, k_done, ksum_done, q_done = map(
            sem, ("lb_diff", "lb_sig", "f_sig", "f_done", "k_done", "ksum_done", "q_done"))
        diag_mm, diag_moved = map(sem, ("diag_mm", "diag_moved"))
        ho_stat, ln_stat = Count(sem("ho_stat")), Count(sem("ln_stat"))
        hv_turned, hv_moved = Count(sem("hv_turned")), Count(sem("hv_moved"))
        level_mm, level_selected, level_updated, off_mm, off_moved = map(
            sem, ("level_mm", "level_selected", "level_updated", "off_mm", "off_moved"))
        ho_mm, ho_moved, ho_sq, ho_sum, hg_sig, hg_gate, h_out, h_hi, h_lo = map(
            sem, ("ho_mm", "ho_moved", "ho_sq", "ho_sum", "hg_sig", "hg_gate", "h_out", "h_hi", "h_lo"))
        pos_landed, angles, sines, rot_mm, rot_done = map(
            sem, ("pos_landed", "angles", "sines", "rot_mm", "rot_done"))
        bias_landed, bias_mm, bias_done, cb_sig, z_done, conv_step = map(
            sem, ("bias_landed", "bias_mm", "bias_done", "cb_sig", "z_done", "conv_step"))
        ln_mm, ln_mean, ln_center, ln_sq, ln_norm, ln_bias, ln_sig, gates_sig = map(
            sem, ("ln_mm", "ln_mean", "ln_center", "ln_sq", "ln_norm", "ln_bias", "ln_sig",
                  "gates_sig"))
        out_turned, out_moved, out_stored = map(sem, ("out_turned", "out_moved", "out_stored"))

        bias_rows = bias[:].rearrange("p s h i c -> p (s h i c)").rearrange("p (n w) -> p n w", w=512)

        block = ctx.enter_context(nc.Block())

        @block.sync
        def _(sp):
            sp.dma_start(consts[:, :], d["consts"]).then_inc(loads, 16)
            for dst, src in vector_loads(d, v_rows, early=True):
                sp.dma_start(dst, src).then_inc(loads, 16)
            def mod_piece(section, pair, s):
                rows = bass.ds(pair * (2 * P) + (s // 2) * P, P)
                col = section * D + (s % 2) * MW
                sp.dma_start(w_mod_slots[:, s, :], w_mod[rows, col:col + MW]).then_inc(landed[s], 16)

            for section in range(2):
                for s in range(SLOTS):
                    if section:
                        sp.wait_ge(mod_products, SECTION_PIECES - SLOTS + s + 1)
                    mod_piece(section, 0, s)
                if section == 0:
                    for half in range(2):
                        sp.dma_start(x_nat[:, half, :], d["x"][0, half * P:(half + 1) * P, :]).then_inc(x_loads, 16)
                with sp.Fori(1, DT // 2) as pair:
                    for s in range(SLOTS):
                        sp.wait_ge(mod_products, pair * SLOTS + (section * SECTION_PIECES - SLOTS + s + 1))
                        mod_piece(section, pair, s)

            def chunk(ph, it, j, first):
                b, k0, kn = ph.chunks[j]
                lin_, p0, stride = ph.body[b]
                free = freed(ph, it, j, first)
                if free is not None:
                    sp.wait_ge(lo_ready, free)
                else:
                    sp.wait_ge(mod_products, 2 * SECTION_PIECES - SLOTS + j + 1)
                row = (lin_.row_tile + k0) * P
                panel = p0 + it * stride
                src = lin_.w[row:row + kn * P, bass.ds(panel * lin_.step + lin_.col0, lin_.width)]
                slot = j % SLOTS
                sp.dma_start(w_raw[:, slot, 0:kn, 0:lin_.width],
                             src.rearrange("(k p) n -> p k n", p=P)).then_inc(landed[slot], 16)

            def side(ph, it, i, first):
                s = ph.side
                n = piece_seq(ph, it, i)
                if not (first and n < MOD_SLOTS):
                    before = s.product0 + (it * s.pieces + (i + 1 - MOD_SLOTS)) * s.rows
                    if first and i < MOD_SLOTS:
                        before = s.product0
                    sp.wait_ge(side_products, before)
                col = s.section * D + i * s.width
                src = w_mod[bass.ds(it * (s.rows * P), s.rows * P), col:col + s.width]
                sp.dma_start(mod_w[:, i % MOD_SLOTS, :].rearrange("p (k n) -> p k n", k=s.rows),
                             src.rearrange("(k p) n -> p k n", p=P)).then_inc(mod_landed[i % MOD_SLOTS], 16)

            for ph in phases:
                if ph.name == "w_o":
                    sp.wait_ge(h_lo, 1)
                for j in range(ph.n_chunks):
                    chunk(ph, 0, j, True)
                    for i in pieces_at(ph, j):
                        side(ph, 0, i, True)
                if ph.iters > 1:
                    with sp.Fori(1, ph.iters) as it:
                        for j in range(ph.n_chunks):
                            chunk(ph, it, j, False)
                            for i in pieces_at(ph, j):
                                side(ph, it, i, False)
            for g in range(8):
                quarter, half = divmod(g, 2)
                cut = slice(quarter * 512, (quarter + 1) * 512)
                sp.wait_ge(out_moved, g + 1)
                sp.dma_start(out[0, half * P:(half + 1) * P, cut], y_nat[:, half, cut]).then_inc(out_stored, 16)
            sp.wait_ge(out_stored, 8 * 16)

        @block.gpsimd
        def _(pool):
            pool.dma_start(masks_i[:, :], d["masks"]).then_inc(late_loads, 16)
            for dst, src in vector_loads(d, v_rows, early=False):
                pool.dma_start(dst, src).then_inc(late_loads, 16)

            pool.wait_ge(h_lo, 1)
            pool.dma_start(pos_i[ROPE:P, :],
                           d["positions"][0:1, :].to_broadcast([ROPE, T])).then_inc(pos_landed, 16)
            pool.wait_ge(*r_m1.added(4))
            for r in range(GRID_ROWS):
                for i in range(GRID_ROWS):
                    src = bass.AP(d["rpb_2"].tensor,
                                  (i - r + WIN_R - 1) * RPB_W + WIN_C - 1 - (GRID_W - 1),
                                  [[1, GRID_W], [RPB_H * RPB_W, HEADS], [1, GRID_W]])
                    rows = slice((r % 2) * GRID_W, (r % 2 + 1) * GRID_W)
                    pool.dma_start(bias[rows, r // 2, :, i, :], src).then_inc(bias_landed, 16)

        @block.tensor
        def _(pe):
            def panel(ph, it, b, first, opens=False):
                lin_ = ph.body[b][0]
                seq, pair = panel_seq(ph, it, b), bank_pair(ph, b)
                if not (first and ph.panel0 + b < 2):
                    pe.wait_ge(summed, seq - 1)
                ids = chunk_ids(ph, b)
                for j in ids:
                    _, k0, kn = ph.chunks[j]
                    slot = j % SLOTS
                    pe.wait_ge(lo_ready, chunk_seq(ph, it, j) + 1)
                    if first and b == 0 and ph.name in ready:
                        pe.wait_ge(*ready[ph.name](k0 + kn))
                    for k in range(kn):
                        kk = k0 + k
                        at_first, at_last = j == ids[0] and k == 0, j == ids[-1] and k == kn - 1
                        for n, c in enumerate(lin_.tiles):
                            hi = w_hi[:, slot, k, c:c + P]
                            lo = w_lo[:, slot, k, c:c + P]
                            bank = 2 * pair + n
                            pe.matmul(ps[:, bank, :], hi, lin_.act[:, kk, :, :], start=at_first,
                                      stop=False, skip_group_check=True)
                            mm = pe.matmul(ps[:, bank, 0:T], lo, lin_.act[:, kk, 0, :], start=False,
                                           stop=at_last, skip_group_check=True)
                    mm.then_inc(chunk_used, 1)
                    beside(ph, j)
                if ph.name in out_norm and not first:
                    n = out_norm[ph.name]
                    for i in range(2):
                        done = (it * 2 + (b - 2)) * 2 + i
                        pe.wait_ge(*n.squared(done + 1))
                        pe.matmul(ps[:, 5, 0:T], ones[:, :], ring[:, 2 * b + i, :], stop=False,
                                  start=opens and b == i == 0,
                                  skip_group_check=True).then_inc(n.added.sem, 1)

            def relu_tiles(name):
                return lambda k: (extra, by_name[name].extra0 + 3 * (k // 2))

            ready = {
                "in_h": a_x1.lo, "up_0": a_x2.lo, "in_c": a_x3.lo, "gate_up": a_x4.lo,
                "w_o": lambda k: att1.lo(min(k, HEADS)), "att_o": att2.lo,
                "conv_o": lambda k: s_conv.lo(k // 2), "out_2": lambda k: s_merged.lo(k // 2),
                "down_0": relu_tiles("up_0"), "down_1": relu_tiles("up_1"),
                "down_2": lambda k: (extra, by_name["gate_up"].extra0 + 4 * (k // 2)),
            }

            def norm(n, first=0):
                for k in range(first, n.tiles):
                    pe.wait_ge(*n.squared(k + 1))
                    pe.matmul(ps[:, n.bank, 0:T], ones[:, :], ring[:, k % 4, :], start=k == 0,
                              stop=k == n.tiles - 1, skip_group_check=first > 0).then_inc(n.added.sem, 1)

            def turn_values(tiles, done):
                for i in range(2 * HEADS):
                    half, h = divmod(i, HEADS)
                    pe.transpose(ps[:, 4 + i // 4, (i % 4) * P:(i % 4 + 1) * P],
                                 tiles[:, h, half * P:(half + 1) * P], ident).then_inc(done.sem, 1)

            def attention_step(a, scores, u):
                def pv(h):
                    pe.wait_ge(*a.moved(2 * h + 2))
                    if h >= 1:
                        pe.wait_ge(*a.lo(h))
                    for s in range(2):
                        mm = pe.matmul(ps[:, 7, 0:T], a.v_tok[:, s, h, :], a.prob_t[:, h % 2, s, :],
                                       start=s == 0, stop=s == 1)
                    mm.then_inc(a.out.sem, 1)

                if u < UNITS:
                    if u >= 2:
                        pe.wait_ge(*a.exped(u - 1))
                    scores(u // 2, u % 2, ps[:, 4 + u % 2, 0:T]).then_inc(a.scores.sem, 1)
                v = u - a.lag
                if 0 <= v < UNITS:
                    pe.wait_ge(*a.normed(v + 1))
                    if v >= 1:
                        pe.wait_ge(*a.moved(v))
                    for s in range(2):
                        mm = pe.transpose(ps[:, 6, s * P:(s + 1) * P],
                                          a.prob[:, v % 2, s * P:(s + 1) * P], ident)
                    mm.then_inc(a.turned.sem, 1)
                h, odd = divmod(u - a.lag - 2, 2)
                if not odd and 0 <= h < HEADS:
                    pv(h)

            def scores_2(h, half, o):
                return pe.matmul(o, q2[:, h, half * P:(half + 1) * P], k2[:, h, :], start=True, stop=True)

            def bias_step(i):
                if i >= 4:
                    pe.wait_ge(bias_done, i - 3)
                pe.matmul(ps[:, 4 + i % 4, :], consts[:, C_FLIP:C_FLIP + P], bias_rows[:, i, :],
                          start=True, stop=True).then_inc(bias_mm, 1)

            def beside(ph, j):
                if ph.name == "in_m" and j % 2 == 1 and j < 2 * N_STEPS - 1:
                    level_step((j + 1) // 2)
                if ph.name == "in_v" and j % 2 == 1 and j < 13:
                    bias_step((j + 3) // 2)
                if ph.name == "in_g" and j % 3 == 2 and (j + 1) // 3 < ATT_STEPS:
                    attention_step(att2, scores_2, (j + 1) // 3)
                if ph.name == "att_o" and 1 <= j <= 4:
                    for k in (2 * j - 2, 2 * j - 1):
                        pe.wait_ge(ln_sq, k + 1)
                        pe.matmul(ps[:, 5, 0:T], ones[:, :], ring[:, k % 4, :], start=k == 0,
                                  stop=k == HEADS - 1).then_inc(ln_mm, 1)

            def turn_vectors(tiles):
                for t in tiles:
                    rows = min(P, N_COLUMNS - t * P)
                    pe.transpose(ps[:, 4 + t // 4, (t % 4) * P:(t % 4) * P + rows], v_rows[0:rows, t, :],
                                 consts[0:rows, C_IDENT:C_IDENT + rows]).then_inc(cols_turned, 1)

            def sum_mods(acc, groups, first=0):
                for g in range(first, first + groups):
                    for i in range(8):
                        mm = pe.matmul(ps[:, 4, 8 * g + i:8 * g + i + 1], acc[:, g, i * P:(i + 1) * P],
                                       ones[:, 0:1], start=True, stop=True)
                    mm.then_inc(mod_mm, 1)

            def start():
                pe.wait_ge(loads, 16 * N_EARLY)
                turn_vectors([0])
                pe.wait_ge(x_loads, 32)
                for g in range(8):
                    half, b4 = divmod(g, 4)
                    if g >= 4:
                        pe.wait_ge(x_moved, g - 3)
                    for i in range(4):
                        mm = pe.transpose(ps[:, b4, i * P:(i + 1) * P],
                                          x_nat[:, half, (4 * b4 + i) * P:(4 * b4 + i + 1) * P], ident)
                    mm.then_inc(x_turned, 1)
                pe.wait_ge(cols_moved, 1)
                pe.wait_ge(late_loads, 16 * N_LATE)
                turn_vectors(range(1, V_TILES))
                pe.wait_ge(cols_moved, V_TILES)
                pe.wait_ge(const_set, 1)
                norm(n_x1)
                for section in range(2):
                    pe.wait_ge(mod_products, (section + 1) * SECTION_PIECES)
                    sum_mods(mod_acc_a, 2, 2 * section)

            def hgrn_start():
                turn_values(hv, hv_turned)
                pe.wait_ge(*hv_moved(4))
                pe.wait_ge(ksum_done, 1)
                for h in range(HEADS):
                    for half in range(2):
                        i = 2 * h + half
                        cut = slice(half * P, (half + 1) * P)
                        pe.matmul(ps[:, 4 + i // 4, (i % 4) * P:(i % 4 + 1) * P], qb[:, h, cut],
                                  hq[:, h, cut], start=True, stop=True).then_inc(diag_mm, 1)
                pe.wait_ge(diag_moved, 4)
                pe.wait_ge(q_done, 2)

            def level_step(step):
                n, way = divmod(step, 2)
                m = LEVELS[n]
                if n:
                    pe.wait_ge(level_updated, 6 * (n - 1) + 3 * (way + 1))
                kk, qq = ((kf, hq), (kb, qb))[way]
                for i in range(2 * HEADS):
                    h, half = divmod(i, 2)
                    q_ = qq[:, h, half * P:(half + 1) * P].rearrange("p (b two m) -> p b two m", two=2, m=m)
                    o = ps[:, 4 + 2 * way + i // 8, (i % 8) * 64:(i % 8 + 1) * 64]
                    mm = pe.matmul(o, kk[:, h, half * P:(half + 1) * P], q_[:, :, 1 - way, :],
                                   start=True, stop=True)
                mm.then_inc(level_mm, 1)

            def hgrn_end():
                pe.wait_ge(level_updated, 6 * len(LEVELS))
                for way in range(2):
                    kk, qq = ((kf, hq), (kb, qb))[way]
                    for h in range(HEADS):
                        s, t = (0, P) if way == 0 else (P, 0)
                        pe.matmul(ps[:, 4 + 2 * way + h // 4, (h % 4) * P:(h % 4 + 1) * P],
                                  kk[:, h, s:s + P], qq[:, h, t:t + P], start=True, stop=True).then_inc(off_mm, 1)
                norm(n_q)
                norm(n_kv)
                pe.wait_ge(off_moved, 4)
                for h in range(HEADS):
                    for t in range(2):
                        o = ps[:, 4 + h // 2, (h % 2) * T + t * P:(h % 2) * T + (t + 1) * P]
                        pe.matmul(o, hv_tok[:, t, h, :], a_diag[:, h, t, :], start=True, stop=False)
                        mm = pe.matmul(o, hv_tok[:, 1 - t, h, :], a_off[:, 1 - t, h, :], start=False, stop=True)
                    mm.then_inc(ho_mm, 1)
                for h in range(HEADS):
                    pe.wait_ge(ho_sq, h // 2 + 1)
                    if h == 0:
                        pe.wait_ge(ho_moved, 1)
                    sel = consts[:, C_HEAD + HEADS - h:C_HEAD + 2 * HEADS - h]
                    mm = pe.matmul(ps[0:HEADS, 4, 0:T], sel, kf[:, h, :], start=h == 0, stop=h == HEADS - 1)
                mm.then_inc(ho_sum, 1)
                pe.wait_ge(*ho_stat(3))
                pe.wait_ge(ho_moved, 4)
                for h in range(HEADS):
                    mm = pe.matmul(ps[:, 4 + h // 2, (h % 2) * T:(h % 2 + 1) * T],
                                   consts[0:HEADS, C_IDENT + h:C_IDENT + h + 1].to_broadcast([HEADS, P]),
                                   rstd_h, start=True, stop=True)
                mm.then_inc(ho_sum, 1)

            def before_in_m():
                pe.wait_ge(summed, summed_all("in_h"))
                pe.wait_ge(side_products, side_all("in_h"))
                sum_mods(mod_acc, 4)
                pe.wait_ge(mods_done, 8)
                hgrn_start()
                level_step(0)

            def before_uq():
                pe.wait_ge(summed, summed_all("in_m"))
                hgrn_end()
                pe.wait_ge(*a_q.lo(4))
                pe.wait_ge(*a_kv.lo(2))

            def before_w_o():
                pe.wait_ge(summed, summed_all("ukv"))
                pe.wait_ge(h_lo, 1)
                for first_, tiles, n in ((0, proj[ROPE:P, 6:7, :], 1), (1, q1, 4)):
                    for i in range(n):
                        rhs = proj[ROPE:P, 6, :] if n == 1 else q1[ROPE:P, 2 * i:2 * i + 2, 1, :]
                        width = T if n == 1 else 2 * T
                        if n == 4 and i == 0:
                            pe.wait_ge(rot_done, 3)
                        pe.matmul(ps[ROPE:P, i, 0:width], consts[ROPE:P, C_RT:C_RT + ROPE], rhs,
                                  start=True, stop=True).then_inc(rot_mm, 1)
                turn_values(att1.v, att1.v_turned)

                def scores(h, half, o):
                    q_ = slice(half * P, (half + 1) * P)
                    pe.matmul(o, q1[:, h, 0, q_], kv1[:, h, 0, :], start=True, stop=False)
                    return pe.matmul(o, q1[ROPE:P, h, 1, q_], proj[ROPE:P, 6, :], start=False, stop=True)

                pe.wait_ge(rot_done, 6)
                pe.wait_ge(*att1.v_moved(4))
                for u in range(ATT_STEPS):
                    attention_step(att1, scores, u)

            def before_up_0():
                pe.wait_ge(summed, summed_all("w_o"))
                norm(n_y1, DT - 4)
                pe.wait_ge(side_products, side_all("w_o"))
                sum_mods(mod_acc, 2)
                norm(n_x2)

            def before_down_0():
                pe.wait_ge(side_products, side_all("up_0"))
                sum_mods(mod_acc, 2)

            def before_in_c():
                pe.wait_ge(extra, extra_all("down_1"))
                norm(n_m1, DT - 4)
                norm(n_x3)

            def before_in_v():
                pe.wait_ge(bias_landed, 16 * GRID_ROWS ** 2)
                for i in range(2):
                    bias_step(i)

            def before_in_g():
                pe.wait_ge(summed, summed_all("in_v"))
                pe.wait_ge(bias_done, 8)
                turn_values(att2.v, att2.v_turned)
                pe.wait_ge(*att2.v_moved(4))
                attention_step(att2, scores_2, 0)

            def before_att_o():
                pe.wait_ge(conv_step, TAPS * HEADS)
                pe.wait_ge(*att2.lo(HEADS))
                for k in range(HEADS):
                    mm = pe.matmul(ps[:, 4, 0:T], ones[:, :], zc[:, k, :], start=k == 0, stop=k == HEADS - 1)
                mm.then_inc(ln_mm, 1)

            def before_gate_up():
                pe.wait_ge(summed, summed_all("out_2"))
                norm(n_y2, DT - 4)
                norm(n_x4)

            hooks = {
                "uq": before_uq, "w_o": before_w_o, "up_0": before_up_0, "down_0": before_down_0,
                "in_c": before_in_c, "in_m": before_in_m,
                "in_v": before_in_v, "in_g": before_in_g, "att_o": before_att_o,
                "gate_up": before_gate_up,
            }
            start()
            for ph in phases:
                hooks.get(ph.name, lambda: None)()
                for b in range(len(ph.body)):
                    panel(ph, 0, b, True)
                looped = 1
                if ph.name in out_norm:
                    looped = 2
                    for b in range(len(ph.body)):
                        panel(ph, 1, b, False, opens=True)
                if ph.iters > 1:
                    with pe.Fori(looped, ph.iters) as it:
                        for b in range(len(ph.body)):
                            panel(ph, it, b, False)
            pe.wait_ge(summed, summed_all("down_2"))
            norm(n_m2, DT - 4)
            for g in range(8):
                quarter, half = divmod(g, 2)
                pe.wait_ge(*r_m2.added(quarter + 1))
                if g >= 4:
                    pe.wait_ge(out_moved, g - 3)
                for i in range(4):
                    mm = pe.transpose(ps[:, g % 4, i * P:(i + 1) * P],
                                      x_res[:, 4 * quarter + i, half * P:(half + 1) * P], ident)
                mm.then_inc(out_turned, 1)

        @block.scalar
        def _(act):
            def split(ph, it, b, first, ids):
                lin_ = ph.body[b][0]
                for j in ids:
                    kn, slot = ph.chunks[j][2], j % SLOTS
                    uses = ph.use0[slot] + it * ph.slot_uses[slot] + j // SLOTS + 1
                    act.wait_ge(landed[slot], uses * 16)
                    free = freed(ph, it, j, first)
                    if free is not None:
                        act.wait_ge(chunk_used, free)
                    act.copy(w_hi[:, slot, 0:kn, 0:lin_.width],
                             w_raw[:, slot, 0:kn, 0:lin_.width]).then_inc(hi_ready, 1)
                    if not (first and b == 0):
                        beside(ph, it, j, first)

            def evict(ph, it, b, first):
                lin_ = ph.body[b][0]
                seq = panel_seq(ph, it, b)
                act.wait_ge(chunk_used, chunk_seq(ph, it, chunk_ids(ph, b)[-1]) + 1)
                if ph.name in out_norm and not (first and b == 0):
                    n = out_norm[ph.name]
                    before = (it, b - 1) if b else (it - 1, 1)
                    tile = (before[0] * 2 + before[1]) * 2
                    act.wait_ge(*panel_written(ph, *before))
                    act.wait_ge(*n.added(tile - 2))
                    for i in range(2):
                        act.activation(ring[:, 2 * (1 - b) + i, :], n.src[:, bass.ds(tile + i, 1), :],
                                       ACT.Square).then_inc(n.squared.sem, 1)
                pair, n = bank_pair(ph, b), len(lin_.tiles)
                if not (first and ph.panel0 + b < 2):
                    act.wait_ge(summed, seq - 1)
                act.copy(half_sum[:, pair, 0:n, :], ps[:, 2 * pair:2 * pair + n, T:2 * T]).then_inc(half_ready, 1)
                if lin_.kind == "gate":
                    act.wait_ge(summed, seq + 1)
                    if not first:
                        act.wait_ge(extra, extra_seq(ph, it, b))
                    act.activation(gate3[:, :, :], lin_.tmp[:, pair, :, :], ACT.Sigmoid).then_inc(sigmoid_ready, 1)

            def root(ap, stat):
                act.wait_ge(*stat(1))
                act.activation(ap, ap, ACT.Sqrt).then_inc(stat.sem, 1)

            def squares(n, residual=None, first=0):
                for k in range(first, n.tiles):
                    if residual and k % 4 == 0:
                        act.wait_ge(*residual.added(k // 4 + 1))
                    if k >= 4:
                        act.wait_ge(*n.added(k - 3))
                    act.activation(ring[:, k % 4, :], n.src[:, k, :], ACT.Square).then_inc(n.squared.sem, 1)

            def norm(n, residual=None, first=0):
                squares(n, residual, first)
                root(rstd[:, :], n.stat)

            def apply(a):
                for k in range(a.tiles):
                    act.wait_ge(*a.scaled(k + 1))
                    if a.shift is None:
                        act.copy(a.dst[:, k, 0, :], ring[:, k % 4, :]).then_inc(a.hi.sem, 1)
                    else:
                        tile, c0 = a.shift
                        act.activation(a.dst[:, k, 0, :], ring[:, k % 4, :], ACT.Identity,
                                       bias=tile[:, c0 + k:c0 + k + 1]).then_inc(a.hi.sem, 1)

            def split_tiles(s):
                for k in range(0, s.tiles, 2):
                    act.copy(s.dst[:, k:k + 2, 0, :], s.src[:, k:k + 2, :]).then_inc(s.hi.sem, 1)

            def move_values(tok, turned, moved):
                flat = tok.rearrange("p s h d -> p (s h d)")
                for i in range(4):
                    act.wait_ge(*turned(4 * i + 4))
                    act.copy(flat[:, i * 512:(i + 1) * 512], ps[:, 4 + i, :]).then_inc(moved.sem, 1)

            def attention_step(a, u):
                if u < UNITS:
                    act.wait_ge(*a.maxed(2 * u + 2))
                    if u >= 2:
                        act.wait_ge(*a.turned(u - 1))
                    src = ps[:, 4 + u % 2, 0:T] if a.bias is None else a.prob[:, u % 2, :]
                    act.activation(a.prob[:, u % 2, :], src, ACT.Exp, bias=small[:, u, 1:2],
                                   scale=a.scale if a.bias is None else 1.0,
                                   accum_out=small[:, u, 2:3]).then_inc(a.exped.sem, 1)
                if 2 <= u < UNITS + 2:
                    v = u - 2
                    h, half = divmod(v, 2)
                    act.wait_ge(*a.turned(v + 1))
                    if h >= 2:
                        act.wait_ge(*a.out(h - 1))
                    act.copy(a.prob_t[:, h % 2, :, half * P:(half + 1) * P],
                             ps[:, 6, 0:T].rearrange("p (s q) -> p s q", s=2)).then_inc(a.moved.sem, 1)
                if u >= 4 and u % 2 == 0 and (u - 4) // 2 < HEADS:
                    h = (u - 4) // 2
                    act.wait_ge(*a.out(h + 1))
                    act.copy(a.dst[:, h, 0, :], ps[:, 7, 0:T]).then_inc(a.hi.sem, 1)

            def beside(ph, it, j, first):
                if ph.name == "in_g" and j % 3 == 2 and (j - 2) // 3 < ATT_STEPS:
                    attention_step(att2, (j - 2) // 3)
                if ph.name == "att_o":
                    if 2 <= j <= 5:
                        for k in (2 * j - 4, 2 * j - 3):
                            act.wait_ge(ln_center, k + 1)
                            if k >= 4:
                                act.wait_ge(ln_mm, 1 + k - 3)
                            act.activation(ring[:, k % 4, :], zc[:, k, :], ACT.Square).then_inc(ln_sq, 1)
                    if j == 6:
                        act.activation(gate2[:, DT:, :], gate2[:, DT:, :], ACT.Sigmoid).then_inc(gates_sig, 1)
                    if j == 8:
                        root(rstd[:, :], ln_stat)
                    if j == 13:
                        act.wait_ge(ln_bias, HEADS)
                        act.activation(cb, zc, ACT.Sigmoid).then_inc(ln_sig, 1)

            def move_vectors(tiles):
                for t in tiles:
                    rows = min(P, N_COLUMNS - t * P)
                    act.wait_ge(cols_turned, tiles[-1] + 1)
                    act.copy(cols[:, t * P:t * P + rows],
                             ps[:, 4 + t // 4, (t % 4) * P:(t % 4) * P + rows]).then_inc(cols_moved, 1)

            def start():
                move_vectors([0])
                act.wait_ge(cols_moved, 1)
                act.activation(silu_c[:, 0:DT], column("c", 0, DT), ACT.Sigmoid).then_inc(c_sig, 1)
                for g in range(8):
                    half, b4 = divmod(g, 4)
                    act.wait_ge(x_turned, g + 1)
                    act.copy(x_res[:, 4 * b4:4 * b4 + 4, half * P:(half + 1) * P],
                             ps[:, b4, :].rearrange("p (i t) -> p i t", i=4)).then_inc(x_moved, 1)
                move_vectors(range(1, V_TILES))
                act.wait_ge(x_moved, 8)
                norm(n_x1)

            def before_in_h():
                act.wait_ge(mods_done, 4)
                apply(a_x1)

            def hgrn_start():
                act.wait_ge(lb_diff, 2)
                act.activation(lb[:, 0, :], lb[:, 0, :], ACT.Sigmoid).then_inc(lb_sig, 1)
                act.activation(lb[:, 2, :], lb[:, 2, :], ACT.Sigmoid).then_inc(lb_sig, 1)
                act.activation(hf[:, :, :], hf[:, :, :], ACT.Sigmoid).then_inc(f_sig, 1)
                act.activation(hb[:, :, :], hb[:, :, :], ACT.Sigmoid).then_inc(f_sig, 1)
                act.wait_ge(mods_done, 8)
                move_values(hv_tok[:], hv_turned, hv_moved)
                flat = a_diag[:].rearrange("p h s t -> p (h s t)")
                for i in range(4):
                    act.wait_ge(diag_mm, 16)
                    act.copy(flat[:, i * 512:(i + 1) * 512], ps[:, 4 + i, :]).then_inc(diag_moved, 1)

            def hgrn_end():
                squares(n_q)
                flat = a_off[:].rearrange("p s h t -> p (s h t)")
                for i in range(4):
                    act.wait_ge(off_mm, 4 * i + 4)
                    act.copy(flat[:, i * 512:(i + 1) * 512], ps[:, 4 + i, :]).then_inc(off_moved, 1)
                act.wait_ge(*n_q.added(4))
                squares(n_kv)
                root(rstd[:, :], n_q.stat)
                apply(a_q)
                root(rstd[:, :], n_kv.stat)
                apply(a_kv)
                flat = qb[:].rearrange("p h t -> p (h t)")
                squared = kf[:].rearrange("p h t -> p (h t)")
                for i in range(4):
                    cut = slice(i * 512, (i + 1) * 512)
                    act.wait_ge(ho_mm, 2 * i + 2)
                    act.copy(flat[:, cut], ps[:, 4 + i, :]).then_inc(ho_moved, 1)
                    act.wait_ge(ho_moved, i + 1)
                    act.activation(squared[:, cut], flat[:, cut], ACT.Square).then_inc(ho_sq, 1)
                act.activation(hb[:, :, :], hg[:, :, :], ACT.Sigmoid).then_inc(hg_sig, 1)
                root(rstd_h, ho_stat)
                act.wait_ge(h_out, 2)
                act.copy(acts[:, HEADS:2 * HEADS, 0, :], qb[:, :, :]).then_inc(h_hi, 1)

            def before_in_m():
                act.wait_ge(summed, summed_all("in_h"))
                hgrn_start()

            def before_uq():
                act.wait_ge(summed, summed_all("in_m"))
                hgrn_end()

            def before_ukv():
                act.wait_ge(angles, 2)
                act.activation(cos_sin[ROPE:P, :, :], ang[ROPE:P, 0:2, :], ACT.Sin).then_inc(sines, 1)

            def before_w_o():
                move_values(att1.v_tok[:], att1.v_turned, att1.v_moved)
                for u in range(ATT_STEPS):
                    attention_step(att1, u)

            def before_up_0():
                act.wait_ge(summed, summed_all("w_o"))
                norm(n_y1, first=DT - 2)
                norm(n_x2, r_y1)
                apply(a_x2)

            def gate_z():
                act.wait_ge(summed, summed_all("in_c"))
                act.activation(cb, cb, ACT.Sigmoid).then_inc(cb_sig, 1)

            def before_in_c():
                act.wait_ge(extra, extra_all("down_1"))
                norm(n_m1, first=DT - 2)
                norm(n_x3, r_m1)
                apply(a_x3)

            def before_att_o():
                act.wait_ge(summed, summed_all("in_g"))
                act.activation(gate2[:, 0:DT, :], gate2[:, 0:DT, :], ACT.Sigmoid).then_inc(gates_sig, 1)

            def before_in_g():
                move_values(att2.v_tok[:], att2.v_turned, att2.v_moved)

            def before_conv_o():
                act.wait_ge(ln_norm, HEADS + 1)
                split_tiles(s_conv)

            def before_out_2():
                act.wait_ge(extra, extra_all("conv_o"))
                split_tiles(s_merged)

            def before_gate_up():
                act.wait_ge(summed, summed_all("out_2"))
                norm(n_y2, first=DT - 2)
                norm(n_x4, r_y2)
                apply(a_x4)

            hooks = {"in_h": before_in_h, "in_m": before_in_m, "uq": before_uq, "ukv": before_ukv, "w_o": before_w_o,
                     "up_0": before_up_0, "in_c": before_in_c,
                     "in_qk": gate_z, "in_g": before_in_g, "att_o": before_att_o,
                     "conv_o": before_conv_o, "out_2": before_out_2, "gate_up": before_gate_up}
            start()
            follow_stream(act, phases, split, evict, hooks, beside)
            act.wait_ge(summed, summed_all("down_2"))
            norm(n_m2, first=DT - 2)
            for g in range(8):
                quarter, half = divmod(g, 2)
                act.wait_ge(out_turned, g + 1)
                act.copy(y_nat[:, half, quarter * 512:(quarter + 1) * 512], ps[:, g % 4, :]).then_inc(out_moved, 1)

        @block.vector
        def _(dve):
            count = [0]

            def link(ins):
                ins.then_inc(dve_chain, 1)
                count[0] += 1
                dve.wait_ge(dve_chain, count[0])

            def split(ph, it, b, first, ids):
                lin_ = ph.body[b][0]
                for j in ids:
                    kn, slot = ph.chunks[j][2], j % SLOTS
                    dve.wait_ge(hi_ready, chunk_seq(ph, it, j) + 1)
                    cut = (slice(None), slot, slice(0, kn), slice(0, lin_.width))
                    dve.tensor_tensor(w_lo[cut], w_raw[cut], w_hi[cut].bitcast(F32),
                                      ALU.subtract).then_inc(lo_ready, 1)
                    if not (first and b == 0):
                        beside(ph, it, j, first)

            def beside(ph, it, j, first):
                for i in pieces_at(ph, j):
                    modulation(ph, it, i, first)
                if ph.name == "in_m" and j % 2 == 1 and 3 <= j < 2 * N_STEPS + 3:
                    level_step((j - 3) // 2)
                if ph.name == "in_v" and j % 2 == 1:
                    bias_step((j - 1) // 2)
                if ph.name == "in_g" and j % 3 == 2 and (j - 2) // 3 < ATT_STEPS:
                    attention_step(att2, (j - 2) // 3)
                if ph.name == "att_o":
                    layer_norm_step(j)
                if ph.name in ("in_qk", "in_v", "in_g"):
                    round_ = ("in_qk", "in_v", "in_g").index(ph.name)
                    taps, before = ROUND_TAPS[round_], sum(ROUND_TAPS[:round_])
                    tiles = HEADS // ph.iters
                    steps = tiles * taps
                    for n in range(j * steps // ph.n_chunks, (j + 1) * steps // ph.n_chunks):
                        i, tap = divmod(n, taps)
                        convolution(it * tiles + i, before + tap, it * steps + (HEADS * before + n))

            def modulation(ph, it, i, first):
                s = ph.side
                slot = i % MOD_SLOTS
                uses = (s.piece0 + i) // MOD_SLOTS + it * (s.pieces // MOD_SLOTS) + 1
                dve.wait_ge(mod_landed[slot], uses * 16)
                acc = mod_acc[:].rearrange("p a b -> p (a b)")[:, i * s.width:(i + 1) * s.width]
                done = s.product0 + (it * s.pieces + i) * s.rows
                for k in range(s.rows):
                    w = mod_w[:, slot, k * s.width:(k + 1) * s.width]
                    c = silu_c[:, bass.ds(it * s.rows + (DT + k), 1)]
                    if first and k == 0:
                        ins = dve.tensor_scalar(acc, w, c, None, ALU.mult)
                    else:
                        dve.wait_ge(side_products, done + k)
                        ins = dve.scalar_tensor_tensor(acc, w, c, acc, ALU.mult, ALU.add)
                    ins.then_inc(side_products, 1)

            def convolution(tile, n, done):
                tap = (PAD, *range(PAD), *range(PAD + 1, TAPS))[n]
                shift = tap - PAD
                to, end = max(0, -shift), min(T, T - shift)
                w = cols[:, bass.ds(tile + (COLUMN["w_dw_2"] + tap * HEADS), 1)]
                z_ = z[:, bass.ds(tile, 1), to + shift:end + shift]
                o = zc[:, bass.ds(tile, 1), to:end]
                if n == 0:
                    ins = dve.tensor_scalar(o, z_, w, cols[:, bass.ds(tile + COLUMN["b_dw_2"], 1)],
                                            ALU.mult, ALU.add)
                else:
                    dve.wait_ge(conv_step, done)
                    ins = dve.scalar_tensor_tensor(o, z_, w, o, ALU.mult, ALU.add)
                ins.then_inc(conv_step, 1)

            def evict(ph, it, b, first):
                lin_, p0, stride = ph.body[b]
                seq = panel_seq(ph, it, b)
                pair, n = bank_pair(ph, b), len(lin_.tiles)
                tile0 = 2 * (p0 + it * stride)
                tiles = bass.ds(tile0, n)
                ex = extra_seq(ph, it, b)
                high, low = ps[:, 2 * pair:2 * pair + n, 0:T], half_sum[:, pair, 0:n, :]
                dve.wait_ge(half_ready, seq + 1)
                if lin_.kind == "plain":
                    dve.tensor_tensor(lin_.out[:, tiles, :], high, low, ALU.add).then_inc(summed, 1)
                    return
                tmp = lin_.tmp[:, pair, :, :]
                dve.tensor_tensor(tmp, high, low, ALU.add).then_inc(summed, 1)
                dve.wait_ge(summed, seq + 1)
                if lin_.kind == "add":
                    o = lin_.out[:, tiles, :]
                    dve.tensor_tensor(o, o, tmp, ALU.add).then_inc(extra, 1)
                elif lin_.kind == "gated":
                    o = lin_.out[:, tiles, :]
                    dve.tensor_tensor(o, o, tmp, ALU.mult).then_inc(extra, 1)
                elif lin_.kind == "gated_add":
                    dve.tensor_tensor(tmp, tmp, gate2[:, bass.ds(tile0 + DT, n), :], ALU.mult).then_inc(extra, 1)
                    dve.wait_ge(extra, ex + 1)
                    o = lin_.out[:, tiles, :]
                    dve.tensor_tensor(o, o, tmp, ALU.add).then_inc(extra, 1)
                elif lin_.kind == "gate":
                    dve.wait_ge(sigmoid_ready, it + 1)
                    dve.tensor_tensor(gate3[:, :, :], gate3[:, :, :], tmp, ALU.mult).then_inc(extra, 1)
                else:
                    if lin_.kind == "relu2":
                        dve.scalar_tensor_tensor(tmp, tmp, 0.0, tmp, ALU.max, ALU.mult).then_inc(extra, 1)
                    else:
                        dve.wait_ge(extra, ex)
                        dve.tensor_tensor(tmp, gate3[:, :, :], tmp, ALU.mult).then_inc(extra, 1)
                    dve.wait_ge(extra, ex + 1)
                    hi = lin_.out[:, tiles, 0, :]
                    dve.tensor_scalar(hi, tmp, 1.0, None, ALU.mult).then_inc(extra, 1)
                    dve.wait_ge(extra, ex + 2)
                    dve.tensor_tensor(lin_.out[:, tiles, 1, :], tmp, hi.bitcast(F32), ALU.subtract).then_inc(extra, 1)

            def invert_root(ap, stat):
                dve.wait_ge(*stat(2))
                dve.reciprocal(ap, ap).then_inc(stat.sem, 1)
                dve.wait_ge(*stat(3))

            def norm(n):
                dve.wait_ge(*n.added(n.tiles))
                dve.tensor_scalar(rstd[:, :], ps[:, n.bank, 0:T], 1.0 / n.dim, EPS, ALU.mult,
                                  ALU.add).then_inc(n.stat.sem, 1)
                invert_root(rstd[:, :], n.stat)

            def apply(a):
                def low(k):
                    dve.wait_ge(*a.hi(k + 1))
                    hi = a.dst[:, k, 0, :].bitcast(F32)
                    if a.shift is None:
                        ins = dve.tensor_tensor(a.dst[:, k, 1, :], ring[:, k % 4, :], hi, ALU.subtract)
                    else:
                        tile, c0 = a.shift
                        ins = dve.scalar_tensor_tensor(a.dst[:, k, 1, :], ring[:, k % 4, :],
                                                       tile[:, c0 + k:c0 + k + 1], hi, ALU.add, ALU.subtract)
                    ins.then_inc(a.lo.sem, 1)

                for k in range(a.tiles + 2):
                    if k < a.tiles:
                        if k >= 4:
                            dve.wait_ge(*a.lo(k - 3))
                        dve.scalar_tensor_tensor(ring[:, k % 4, :], a.src[:, k, :], a.gain[:, k:k + 1],
                                                 rstd[:, :], ALU.mult, ALU.mult).then_inc(a.scaled.sem, 1)
                    if k >= 2:
                        low(k - 2)
                dve.wait_ge(*a.lo(a.tiles))

            def residual(r, gain):
                for j in range(4):
                    for k in range(4 * j, 4 * j + 4):
                        dve.scalar_tensor_tensor(r.src[:, k, :], r.src[:, k, :], gain[:, k:k + 1],
                                                 rstd[:, :], ALU.mult, ALU.mult).then_inc(r.scaled.sem, 1)
                    dve.wait_ge(*r.scaled(4 * j + 4))
                    cut = slice(4 * j, 4 * j + 4)
                    dve.tensor_tensor(x_res[:, cut, :], x_res[:, cut, :], r.src[:, cut, :],
                                      ALU.add).then_inc(r.added.sem, 1)
                dve.wait_ge(*r.added(4))

            def scale_gain(name, scale):
                link(dve.scalar_tensor_tensor(gains[:, :], mods[:, scale * DT:(scale + 1) * DT], 1.0,
                                              column(name, 0, DT), ALU.add, ALU.mult))

            def gate_gain(name, gate):
                link(dve.tensor_tensor(gains[:, :], mods[:, gate * DT:(gate + 1) * DT],
                                       column(name, 0, DT), ALU.mult))

            def split_tiles(s):
                for n, k in enumerate(range(0, s.tiles, 2)):
                    dve.wait_ge(*s.hi(n + 1))
                    dve.tensor_tensor(s.dst[:, k:k + 2, 1, :], s.src[:, k:k + 2, :],
                                      s.dst[:, k:k + 2, 0, :].bitcast(F32), ALU.subtract).then_inc(s.lo.sem, 1)

            def attention_step(a, u):
                if u < UNITS:
                    dve.wait_ge(*a.scores(u + 1))
                    src = ps[:, 4 + u % 2, 0:T]
                    if a.bias is not None:
                        if u >= 2:
                            dve.wait_ge(*a.turned(u - 1))
                        h, half = divmod(u, 2)
                        dve.scalar_tensor_tensor(
                            a.prob[:, u % 2, :], src, a.scale,
                            a.bias[:, half, h, :, :].rearrange("p i c -> p (i c)"),
                            ALU.mult, ALU.add).then_inc(a.biased.sem, 1)
                        dve.wait_ge(*a.biased(u + 1))
                        src = a.prob[:, u % 2, :]
                    dve.tensor_reduce(small[:, u, 0:1], src, AX.X, ALU.max).then_inc(a.maxed.sem, 1)
                    dve.wait_ge(*a.maxed(2 * u + 1))
                    dve.tensor_scalar(small[:, u, 1:2], small[:, u, 0:1],
                                      -(a.scale if a.bias is None else 1.0), None,
                                      ALU.mult).then_inc(a.maxed.sem, 1)
                if 1 <= u <= UNITS:
                    v = u - 1
                    dve.wait_ge(*a.exped(v + 1))
                    dve.reciprocal(small[:, v, 3:4], small[:, v, 2:3]).then_inc(a.inverted.sem, 1)
                    dve.wait_ge(*a.inverted(v + 1))
                    dve.tensor_scalar(a.prob[:, v % 2, :], a.prob[:, v % 2, :], small[:, v, 3:4], None,
                                      ALU.mult).then_inc(a.normed.sem, 1)
                if u >= 4 and u % 2 == 0 and (u - 4) // 2 < HEADS:
                    h = (u - 4) // 2
                    dve.wait_ge(*a.hi(h + 1))
                    dve.tensor_tensor(a.dst[:, h, 1, :], ps[:, 7, 0:T], a.dst[:, h, 0, :].bitcast(F32),
                                      ALU.subtract).then_inc(a.lo.sem, 1)

            def bias_step(i):
                outside = consts[:, C_WIN:C_WIN + GRID_W].rearrange("p (o c) -> p o c", o=1)
                dve.wait_ge(bias_mm, i + 1)
                dve.tensor_tensor(bias_rows[:, i, :].rearrange("p (n c) -> p n c", c=GRID_W),
                                  ps[:, 4 + i % 4, :].rearrange("p (n c) -> p n c", c=GRID_W),
                                  outside.to_broadcast([P, 512 // GRID_W, GRID_W]),
                                  ALU.add).then_inc(bias_done, 1)

            def layer_norm_step(j):
                if j == 0:
                    dve.wait_ge(ln_mm, 1)
                    dve.tensor_scalar(mean[:, :], ps[:, 4, 0:T], 1.0 / (HEADS * P), None,
                                      ALU.mult).then_inc(ln_mean, 1)
                    dve.wait_ge(ln_mean, 1)
                if 1 <= j <= 4:
                    for k in (2 * j - 2, 2 * j - 1):
                        dve.tensor_tensor(zc[:, k, :], zc[:, k, :], mean[:, :], ALU.subtract).then_inc(ln_center, 1)
                if j == 8:
                    dve.wait_ge(ln_mm, 1 + HEADS)
                    dve.tensor_scalar(rstd[:, :], ps[:, 5, 0:T], 1.0 / (HEADS * P), EPS, ALU.mult,
                                      ALU.add).then_inc(ln_stat.sem, 1)
                if j == 9:
                    invert_root(rstd[:, :], ln_stat)
                if 10 <= j <= 11:
                    for k in range(4 * j - 40, 4 * j - 36):
                        dve.scalar_tensor_tensor(zc[:, k, :], zc[:, k, :], column("conv_ln_g_2", k), rstd[:, :],
                                                 ALU.mult, ALU.mult).then_inc(ln_norm, 1)
                    for k in range(4 * j - 40, 4 * j - 36):
                        dve.wait_ge(ln_norm, k + 1)
                        dve.tensor_scalar(zc[:, k, :], zc[:, k, :], column("conv_ln_b_2", k), None,
                                          ALU.add).then_inc(ln_bias, 1)
                if j == 14:
                    dve.wait_ge(ln_sig, 1)
                    dve.wait_ge(ln_bias, HEADS)
                    dve.tensor_tensor(zc, zc, cb, ALU.mult).then_inc(ln_norm, 1)
                    dve.wait_ge(ln_norm, HEADS + 1)

            def take_mods(groups, before):
                dve.wait_ge(mod_mm, before + groups)
                at_ = 8 * before
                dve.tensor_tensor(mods[:, at_:at_ + 8 * groups], ps[:, 4, 0:8 * groups],
                                  column("b_mod", at_, 8 * groups), ALU.add).then_inc(mods_done, groups)
                dve.wait_ge(mods_done, before + groups)

            def start():
                dve.memset(ones[:, :], 1.0).then_inc(const_set, 1)
                dve.wait_ge(c_sig, 1)
                dve.tensor_tensor(silu_c[:, DT:2 * DT], silu_c[:, 0:DT], column("c", 0, DT),
                                  ALU.mult).then_inc(c_silu, 1)
                dve.wait_ge(c_silu, 1)
                for section in range(2):
                    done = section * SECTION_PIECES
                    landings = section * DT // 2

                    def piece(pair, s, first):
                        dve.wait_ge(landed[s], (pair + (landings + 1)) * 16)
                        acc = mod_acc_a[:, 2 * section + s % 2, :]
                        c_k = silu_c[:, bass.ds(pair * 2 + (DT + s // 2), 1)]
                        if first:
                            ins = dve.tensor_scalar(acc, w_mod_slots[:, s, :], c_k, None, ALU.mult)
                        else:
                            dve.wait_ge(mod_products, pair * SLOTS + (done + s - 1))
                            ins = dve.scalar_tensor_tensor(acc, w_mod_slots[:, s, :], c_k, acc,
                                                           ALU.mult, ALU.add)
                        ins.then_inc(mod_products, 1)

                    for s in range(SLOTS):
                        piece(0, s, s < 2)
                    with dve.Fori(1, DT // 2) as pair:
                        for s in range(SLOTS):
                            piece(pair, s, False)
                dve.wait_ge(late_loads, 16 * N_LATE)
                link(dve.tensor_copy(masks[:].rearrange("p a l t -> p (a l t)"), masks_i[:, :]))
                norm(n_x1)

            def before_in_h():
                take_mods(4, 0)
                scale_gain("pre_mix_g", 1)
                apply(a_x1)

            def hgrn_start():
                for i, name in enumerate(("hgrn_lb_logits_fwd", "hgrn_lb_logits_bwd")):
                    dve.tensor_tensor(lb[:, 2 * i, :], column(name, 0, HEADS), column(name, HEADS, HEADS),
                                      ALU.subtract).then_inc(lb_diff, 1)
                dve.wait_ge(lb_sig, 2)
                for i in range(2):
                    link(dve.tensor_scalar(lb[:, 2 * i + 1, :], lb[:, 2 * i, :], -1.0, 1.0, ALU.mult, ALU.add))
                for i, f in enumerate((hf, hb)):
                    dve.wait_ge(f_sig, i + 1)
                    for h in range(HEADS):
                        dve.tensor_scalar(f[:, h, :], f[:, h, :], lb[:, 2 * i + 1, h:h + 1],
                                          lb[:, 2 * i, h:h + 1], ALU.mult, ALU.add).then_inc(f_done, 1)
                take_mods(4, 4)
                for i, f in enumerate((hf, hb)):
                    dve.wait_ge(f_done, HEADS * (i + 1))
                    dve.tensor_scalar((kf, kb)[i][:, :, :], f, -1.0, 1.0, ALU.mult, ALU.add).then_inc(k_done, 1)
                dve.wait_ge(k_done, 2)
                dve.tensor_tensor(qb[:, :, :], kf[:, :, :], kb[:, :, :], ALU.add).then_inc(ksum_done, 1)
                dve.wait_ge(diag_mm, 16)
                dve.tensor_tensor(qb[:, :, :], hq, hb, ALU.mult).then_inc(q_done, 1)
                dve.wait_ge(q_done, 1)
                dve.tensor_tensor(hq, hq, hf, ALU.mult).then_inc(q_done, 1)
                dve.wait_ge(q_done, 2)
                dve.wait_ge(diag_moved, 4)

            def level_step(step):
                n, way = divmod(step, 2)
                m = LEVELS[n]
                kk, qq, ff = ((kf, hq, hf), (kb, qb, hb))[way]
                late, early = 1 - way, way
                dve.wait_ge(level_mm, step + 1)
                if step:
                    dve.wait_ge(level_selected, step)
                a = a_diag[:].rearrange("p h s (b two m) -> p (h s) b two m", two=2, m=m)
                got = ps[:, 4 + 2 * way:6 + 2 * way, :].rearrange("p k (g b m) -> p (k g) b m", g=8, m=m)
                mask = masks[:, way, n, :].rearrange("p (g b m) -> p g b m", g=1, m=m)
                dve.copy_predicated(a[:, :, :, late, :], mask.to_broadcast([P, 2 * HEADS, 64 // m, m]),
                                    got).then_inc(level_selected, 1)
                q_ = qq[:].rearrange("p h (b two m) -> p (h b) two m", two=2, m=m)
                k_ = kk[:].rearrange("p h (b two m) -> p (h b) two m", two=2, m=m)
                f_ = ff[:].rearrange("p h (b two m) -> p (h b) two m", two=2, m=m)
                pairs = HEADS * T // (2 * m)
                dve.tensor_tensor(q_[:, :, late, :], q_[:, :, late, :],
                                  f_[:, :, early, 0:1].to_broadcast([P, pairs, m]),
                                  ALU.mult).then_inc(level_updated, 1)
                dve.tensor_tensor(k_[:, :, early, :], k_[:, :, early, :],
                                  f_[:, :, late, 0:1].to_broadcast([P, pairs, m]),
                                  ALU.mult).then_inc(level_updated, 1)
                dve.wait_ge(level_updated, 3 * step + 2)
                dve.tensor_tensor(f_[:, :, 0, 0:1], f_[:, :, 0, 0:1], f_[:, :, 1, 0:1],
                                  ALU.mult).then_inc(level_updated, 1)

            def hgrn_end():
                dve.wait_ge(level_selected, N_STEPS)
                dve.wait_ge(level_updated, 3 * N_STEPS)
                norm(n_q)
                dve.wait_ge(*n_kv.added(2))
                dve.wait_ge(off_moved, 4)
                apply(a_q)
                norm(n_kv)
                apply(a_kv)
                dve.wait_ge(ho_sum, 1)
                dve.tensor_scalar(rstd_h, ps[0:HEADS, 4, 0:T], 1.0 / P, EPS, ALU.mult, ALU.add
                                  ).then_inc(ho_stat.sem, 1)
                dve.wait_ge(hg_sig, 1)
                dve.tensor_tensor(hg, hg, hb, ALU.mult).then_inc(hg_gate, 1)
                invert_root(rstd_h, ho_stat)
                dve.wait_ge(ho_sq, 4)
                dve.wait_ge(ho_sum, 2)
                dve.scalar_tensor_tensor(qb[:, :, :], qb[:, :, :], column("hgrn_norm_g"),
                                         ps[:, 4:8, :].rearrange("p b (h t) -> p (b h) t", t=T),
                                         ALU.mult, ALU.mult).then_inc(h_out, 1)
                dve.wait_ge(h_out, 1)
                dve.wait_ge(hg_gate, 1)
                dve.tensor_tensor(qb[:, :, :], qb[:, :, :], hg, ALU.mult).then_inc(h_out, 1)
                dve.wait_ge(h_hi, 1)
                dve.wait_ge(h_out, 2)
                dve.tensor_tensor(acts[:, HEADS:2 * HEADS, 1, :], qb[:, :, :],
                                  acts[:, HEADS:2 * HEADS, 0, :].bitcast(F32), ALU.subtract).then_inc(h_lo, 1)
                dve.wait_ge(h_lo, 1)

            def before_in_m():
                dve.wait_ge(summed, summed_all("in_h"))
                hgrn_start()

            def before_uq():
                dve.wait_ge(summed, summed_all("in_m"))
                hgrn_end()

            def rope_angles():
                r = slice(ROPE, P)
                c1 = 6.28125
                c2 = float(np.float32(np.floor((TWO_PI - c1) * 2 ** 21) / 2 ** 21))
                c3 = TWO_PI - c1 - c2
                magic = 12582912.0
                dve.wait_ge(pos_landed, 16)
                link(dve.tensor_copy(ang[r, 1, :], pos_i[r, :]))
                link(dve.tensor_scalar(ang[r, 1, :], ang[r, 1, :], consts[r, C_FREQ:C_FREQ + 1], None, ALU.mult))
                link(dve.tensor_copy(ang[r, 0, :], ang[r, 1, :]))
                for i, quarter in ((0, 0.25), (1, 0.0)):
                    a, n = ang[r, i, :], ang[r, 2, :]
                    link(dve.tensor_scalar(n, a, 1 / TWO_PI, quarter, ALU.mult, ALU.add))
                    link(dve.tensor_scalar(n, n, magic, None, ALU.add))
                    link(dve.tensor_scalar(n, n, -magic, None, ALU.add))
                    for c in (c1, c2, c3):
                        link(dve.scalar_tensor_tensor(a, n, -c, a, ALU.mult, ALU.add))
                    link(dve.tensor_scalar(a, a, quarter * TWO_PI, 3.1415925, ALU.add, ALU.min))
                    dve.tensor_scalar(a, a, -3.1415925, None, ALU.max).then_inc(angles, 1)
                    dve.wait_ge(angles, i + 1)

            def before_w_o():
                r = slice(ROPE, P)
                dve.wait_ge(sines, 1)
                dve.wait_ge(summed, summed_all("ukv"))
                dve.wait_ge(rot_mm, 1)
                kr = proj[r, 6, :]
                dve.tensor_tensor(rot[r, 0, :], ps[r, 0, 0:T], cos_sin[r, 1, :], ALU.mult).then_inc(rot_done, 1)
                dve.tensor_tensor(kr, kr, cos_sin[r, 0, :], ALU.mult).then_inc(rot_done, 1)
                dve.wait_ge(rot_done, 2)
                dve.tensor_tensor(kr, kr, rot[r, 0, :], ALU.add).then_inc(rot_done, 1)
                dve.wait_ge(rot_done, 3)
                dve.wait_ge(rot_mm, 5)
                qr = q1[r, :, 1, :]

                def over_heads(i):
                    return cos_sin[r, i:i + 1, :].to_broadcast([ROPE, HEADS, T])

                dve.tensor_tensor(rot[r, :, :], ps[r, 0:4, :].rearrange("p b (h t) -> p (b h) t", t=T),
                                  over_heads(1), ALU.mult).then_inc(rot_done, 1)
                dve.tensor_tensor(qr, qr, over_heads(0), ALU.mult).then_inc(rot_done, 1)
                dve.wait_ge(rot_done, 5)
                dve.tensor_tensor(qr, qr, rot[r, :, :], ALU.add).then_inc(rot_done, 1)
                for u in range(ATT_STEPS):
                    attention_step(att1, u)
                dve.wait_ge(*att1.lo(HEADS))

            def before_up_0():
                dve.wait_ge(summed, summed_all("w_o"))
                gate_gain("post_mix_g", 2)
                norm(n_y1)
                residual(r_y1, gains)
                take_mods(2, 8)
                scale_gain("pre_mlp_g", 4)
                norm(n_x2)
                apply(a_x2)

            def before_in_c():
                dve.wait_ge(extra, extra_all("down_1"))
                gate_gain("post_mlp_g", 5)
                norm(n_m1)
                residual(r_m1, gains)
                norm(n_x3)
                apply(a_x3)

            def gate_z():
                dve.wait_ge(cb_sig, 1)
                dve.tensor_tensor(z, ca, cb, ALU.mult).then_inc(z_done, 1)
                dve.wait_ge(z_done, 1)

            def before_att_o():
                dve.wait_ge(summed, summed_all("in_g"))
                dve.wait_ge(conv_step, TAPS * HEADS)
                dve.wait_ge(gates_sig, 1)

            def before_conv_o():
                split_tiles(s_conv)
                dve.wait_ge(gates_sig, 2)

            def before_out_2():
                dve.wait_ge(extra, extra_all("conv_o"))
                split_tiles(s_merged)

            def before_gate_up():
                dve.wait_ge(summed, summed_all("out_2"))
                norm(n_y2)
                residual(r_y2, column("mix_post_g_2", 0, DT))
                norm(n_x4)
                apply(a_x4)

            hooks = {"in_h": before_in_h, "in_m": before_in_m, "uq": before_uq, "ukv": rope_angles, "w_o": before_w_o,
                     "up_0": before_up_0,
                     "down_0": lambda: take_mods(2, 10), "in_c": before_in_c, "in_qk": gate_z,
                     "att_o": before_att_o, "conv_o": before_conv_o, "out_2": before_out_2,
                     "gate_up": before_gate_up}
            start()
            follow_stream(dve, phases, split, evict, hooks, beside)
            dve.wait_ge(summed, summed_all("down_2"))
            norm(n_m2)
            residual(r_m2, column("ffn_post_g_2", 0, DT))


def follow_stream(eng, phases, split, evict, hooks, beside):
    def run(ph, it, first, before):
        for b in range(len(ph.body)):
            ids = chunk_ids(ph, b)
            split(ph, it, b, first, ids[:SLOTS])
            if b:
                evict(ph, it, b - 1, first)
            elif before:
                evict(*before)
            if first and b == 0 and ph.name in hooks:
                hooks[ph.name]()
            if first and b == 0:
                for j in ids:
                    beside(ph, it, j, first)
            split(ph, it, b, first, ids[SLOTS:])

    before = None
    for ph in phases:
        last = len(ph.body) - 1
        run(ph, 0, True, before)
        if ph.iters > 1:
            with eng.Fori(1, ph.iters) as it:
                run(ph, it, False, (ph, it - 1, last, False))
        before = (ph, ph.iters - 1, last, ph.iters == 1)
    evict(*before)


def chunk_ids(ph, b):
    return [j for j, (bb, _, _) in enumerate(ph.chunks) if bb == b]


def vector_loads(d, v_rows, early):
    for name, rows in VECTORS:
        src = d[name].rearrange("a (r p) -> (a r) p", p=P) if name != "w_dw_2" else \
            d[name][0].rearrange("j (r p) -> (j r) p", p=P)
        done = 0
        while done < rows:
            tile, at_row = divmod(COLUMN[name] + done, P)
            n = min(rows - done, P - at_row)
            if early == (tile == 0):
                yield v_rows[at_row:at_row + n, tile, :], src[done:done + n, :]
            done += n


N_VECTOR_LOADS = sum((COLUMN[n] + r - 1) // P - COLUMN[n] // P + 1 for n, r in VECTORS)
N_EARLY_VECTORS = sum(COLUMN[n] < P for n, _ in VECTORS)
N_EARLY = 1 + N_EARLY_VECTORS
N_LATE = 1 + N_VECTOR_LOADS - N_EARLY_VECTORS

INPUTS = ["x", "positions", "w_mod", "w_in", "w_uq", "w_ukv", "w_out", "w_up", "w_down", "w_in_2",
          "rpb_2", "w_attn_o_2", "w_conv_o_2", "w_out_2", "w_gate_up_2", "w_down_2"]


def kernel(**inputs):
    import concourse.bacc as bacc
    from concourse.bass_utils import run_bass_kernel_spmd

    nc = bacc.Bacc("TRN2", target_bir_lowering=False, num_devices=1)
    arrays, d = {}, {}
    for name in INPUTS + [n for n, _ in VECTORS]:
        arrays[f"in_{name}"] = np.ascontiguousarray(inputs[name])
    arrays["in_consts"], arrays["in_masks"] = constants()
    for key, a in arrays.items():
        d[key[3:]] = nc.dram_tensor(key, a.shape, mybir.dt.from_np(a.dtype), kind="ExternalInput").ap()
    out = nc.dram_tensor("out", (1, T, D), F32, kind="ExternalOutput").ap()
    build(nc, d, out)
    r = run_bass_kernel_spmd(nc, [arrays], core_ids=[0])
    return r.results[0]["out"]
```
